# Optimizing a Trainium2 kernel written in Bass

```python
import jax, jax.numpy as jnp
from jax import lax
import numpy as np

D_MODEL = 1024
BATCH = 1
SEQ = 2048
DEPTH = 1
DEC_BATCH = 8
DEC_SEQ = 8
PAST_LEN = 4096
PAGE_SIZE = 128

GLA_HEADS = 8
GLA_DK = 32
GLA_DV = 64
GLA_LOW_RANK = 16
GLA_GATE_NORM = 16.0
GLA_CHUNK = 64
SWA_HEADS = 8
SWA_KV_HEADS = 2
SWA_DIM = 64
WINDOW = 128
SWA_BLOCK = 128
MIX_WIDTH = GLA_HEADS * GLA_DV + SWA_HEADS * SWA_DIM
D_FF = -(-8 * D_MODEL // (3 * 256)) * 256
PLE_DIM = 256
EPS = 1e-6
IN_SPLITS = (GLA_HEADS * GLA_DK, GLA_HEADS * GLA_DK, GLA_HEADS * GLA_DV, GLA_HEADS * GLA_DV,
             GLA_LOW_RANK, SWA_HEADS * SWA_DIM, SWA_KV_HEADS * SWA_DIM, SWA_KV_HEADS * SWA_DIM)
D_IN = sum(IN_SPLITS)

kernel_name = "hymba_gla_swa_sink_alibi_decode_step"

def rmsnorm(x, w):
    xf = x.astype(jnp.float32)
    y = xf * lax.rsqrt(jnp.mean(xf * xf, axis=-1, keepdims=True) + EPS)
    return (y * w.astype(jnp.float32)).astype(x.dtype)

def alibi_slopes(n):
    return 2.0 ** (-8.0 * jnp.arange(1, n + 1, dtype=jnp.float32) / n)

def split_points():
    return [int(c) for c in np.cumsum(IN_SPLITS)[:-1]]

def sink_softmax(s, sink):
    m = jnp.maximum(jnp.max(s, axis=-1, keepdims=True), sink)
    e = jnp.exp(s - m)
    return e / (jnp.sum(e, axis=-1, keepdims=True) + jnp.exp(sink - m))

def gla_recurrence(q, k, v, log_a, s0):
    B, T, H, DK = q.shape
    DV = v.shape[-1]
    C = min(GLA_CHUNK, T)
    n = -(-T // C)
    pad = n * C - T

    def prep(a):
        a = jnp.pad(a.astype(jnp.float32), ((0, 0), (0, pad), (0, 0), (0, 0)))
        return a.reshape(B, n, C, H, a.shape[-1]).swapaxes(0, 1)

    mask = jnp.tril(jnp.ones((C, C), dtype=bool))[None, :, :, None, None]

    def step(S, inp):
        qc, kc, vc, gc = inp
        G = jnp.cumsum(gc, axis=1)
        diff = G[:, :, None] - G[:, None, :]
        decay = jnp.exp(jnp.where(mask, diff, -jnp.inf))
        A = jnp.einsum('bihd,bjhd,bijhd->bhij', qc, kc, decay)
        o = (jnp.einsum('bhij,bjhv->bihv', A, vc)
             + jnp.einsum('bihd,bhdv->bihv', qc * jnp.exp(G), S))
        G_last = G[:, -1]
        S = (S * jnp.exp(G_last)[..., None]
             + jnp.einsum('bjhd,bjhv->bhdv', kc * jnp.exp(G_last[:, None] - G), vc))
        return S, o

    S, o = lax.scan(step, s0.astype(jnp.float32), (prep(q), prep(k), prep(v), prep(log_a)))
    o = o.swapaxes(0, 1).reshape(B, n * C, H, DV)[:, :T]
    return o, S

def swa_prompt(q, k, v, sinks, slopes):
    B, T, Hq, D = q.shape
    Hkv = k.shape[2]
    G = Hq // Hkv
    L = SWA_BLOCK
    n = T // L
    qb = q.reshape(B, n, L, Hkv, G, D)

    def band(a):
        prev = jnp.pad(a, ((0, 0), (L, 0), (0, 0), (0, 0)))[:, :T]
        return jnp.concatenate([prev.reshape(B, n, L, Hkv, D), a.reshape(B, n, L, Hkv, D)], axis=2)

    kb, vb = band(k), band(v)
    blk = jnp.arange(n)[:, None]
    qpos = blk * L + jnp.arange(L)[None]
    kpos = blk * L - L + jnp.arange(2 * L)[None]
    dist = qpos[:, :, None] - kpos[:, None, :]
    valid = (dist >= 0) & (dist < WINDOW) & (kpos[:, None, :] >= 0)
    s = jnp.einsum('bnqhgd,bnkhd->bnhgqk', qb, kb).astype(jnp.float32) * (D ** -0.5)
    s = s - slopes.reshape(Hkv, G)[:, :, None, None] * dist[:, None, None].astype(jnp.float32)
    s = jnp.where(valid[:, None, None], s, -jnp.inf)
    pr = sink_softmax(s, sinks.reshape(Hkv, G)[:, :, None, None].astype(jnp.float32))
    o = jnp.einsum('bnhgqk,bnkhd->bnqhgd', pr.astype(v.dtype), vb)
    return o.reshape(B, T, Hq * D)

def swa_with_buffer(q, k, v, k_buf, v_buf, sinks, slopes):
    B, T, Hq, D = q.shape
    Hkv = k.shape[2]
    G = Hq // Hkv
    Wb = k_buf.shape[1]
    kk = jnp.concatenate([k_buf.astype(k.dtype), k], axis=1)
    vv = jnp.concatenate([v_buf.astype(v.dtype), v], axis=1)
    qpos = Wb + jnp.arange(T)
    kpos = jnp.arange(Wb + T)
    dist = qpos[:, None] - kpos[None, :]
    valid = (dist >= 0) & (dist < WINDOW)
    qg = q.reshape(B, T, Hkv, G, D)
    s = jnp.einsum('bqhgd,bkhd->bhgqk', qg, kk).astype(jnp.float32) * (D ** -0.5)
    s = s - slopes.reshape(Hkv, G)[:, :, None, None] * dist.astype(jnp.float32)
    s = jnp.where(valid, s, -jnp.inf)
    pr = sink_softmax(s, sinks.reshape(Hkv, G)[:, :, None, None].astype(jnp.float32))
    o = jnp.einsum('bhgqk,bkhd->bqhgd', pr.astype(vv.dtype), vv).reshape(B, T, Hq * D)
    return o, kk[:, -Wb:], vv[:, -Wb:]

def trunk_layer(x, p, gla_s0, k_buf, v_buf,
                w_pre_mix, w_in, gla_gate_up, gla_gate_b, gla_norm_w, swa_sinks, w_out,
                w_post_mix, w_pre_ffn, w_gate, w_up, w_down, w_post_ffn, w_ple_gate, w_ple_proj,
                is_prompt):
    B, T, _ = x.shape
    hn = rmsnorm(x, w_pre_mix)
    z = hn @ w_in
    q_g, k_g, v_g, og_g, lr_g, q_s, k_s, v_s = jnp.split(z, split_points(), axis=-1)

    log_a = jax.nn.log_sigmoid((lr_g @ gla_gate_up + gla_gate_b).astype(jnp.float32)) / GLA_GATE_NORM
    if gla_s0 is None:
        gla_s0 = jnp.zeros((B, GLA_HEADS, GLA_DK, GLA_DV), jnp.float32)
    o_g, s_new = gla_recurrence(q_g.reshape(B, T, GLA_HEADS, GLA_DK) * (GLA_DK ** -0.5),
                                k_g.reshape(B, T, GLA_HEADS, GLA_DK),
                                v_g.reshape(B, T, GLA_HEADS, GLA_DV),
                                log_a.reshape(B, T, GLA_HEADS, GLA_DK), gla_s0)
    o_g = rmsnorm(o_g.astype(x.dtype), gla_norm_w) * jax.nn.silu(og_g).reshape(B, T, GLA_HEADS, GLA_DV)
    o_g = o_g.reshape(B, T, GLA_HEADS * GLA_DV)

    slopes = alibi_slopes(SWA_HEADS)
    q_s = q_s.reshape(B, T, SWA_HEADS, SWA_DIM)
    k_s = k_s.reshape(B, T, SWA_KV_HEADS, SWA_DIM)
    v_s = v_s.reshape(B, T, SWA_KV_HEADS, SWA_DIM)
    if is_prompt:
        o_s = swa_prompt(q_s, k_s, v_s, swa_sinks, slopes)
        keep = min(WINDOW, T)
        k_new, v_new = k_s[:, T - keep:], v_s[:, T - keep:]
    else:
        o_s, k_new, v_new = swa_with_buffer(q_s, k_s, v_s, k_buf, v_buf, swa_sinks, slopes)
        s_new = s_new.astype(gla_s0.dtype)

    mix = jnp.concatenate([o_g, o_s.astype(x.dtype)], axis=-1) @ w_out
    h = x + rmsnorm(mix, w_post_mix)
    f = rmsnorm(h, w_pre_ffn)
    f = (jax.nn.silu(f @ w_gate) * (f @ w_up)) @ w_down
    h = h + rmsnorm(f, w_post_ffn)
    h = h + jax.nn.sigmoid(h @ w_ple_gate) * (p @ w_ple_proj)
    return h, s_new, k_new, v_new

def setup_inputs(seed: int = 0) -> dict:
    key = jax.random.key(seed)
    ks = jax.random.split(key, 24)
    f32 = jnp.float32

    def nrm(k, shape, scale):
        return jax.random.normal(k, shape, f32) * scale

    def gain(k, n):
        return 1.0 + 0.05 * jax.random.normal(k, (DEPTH, n), f32)

    w_buf = min(WINDOW, PAST_LEN)
    return {
        "x_prompt": nrm(ks[0], (BATCH, SEQ, D_MODEL), 1.0),
        "x_sample": nrm(ks[1], (DEC_BATCH, DEC_SEQ, D_MODEL), 1.0),
        "p_prompt": nrm(ks[2], (DEPTH, BATCH, SEQ, PLE_DIM), 1.0),
        "p_sample": nrm(ks[3], (DEPTH, DEC_BATCH, DEC_SEQ, PLE_DIM), 1.0),
        "state_gla": nrm(ks[4], (DEPTH, DEC_BATCH, GLA_HEADS, GLA_DK, GLA_DV), 0.5),
        "cache_swa_k": nrm(ks[5], (DEPTH, DEC_BATCH, w_buf, SWA_KV_HEADS, SWA_DIM), 1.0),
        "cache_swa_v": nrm(ks[6], (DEPTH, DEC_BATCH, w_buf, SWA_KV_HEADS, SWA_DIM), 1.0),
        "w_pre_mix": gain(ks[7], D_MODEL),
        "w_in": nrm(ks[8], (DEPTH, D_MODEL, D_IN), D_MODEL ** -0.5),
        "gla_gate_up": nrm(ks[9], (DEPTH, GLA_LOW_RANK, GLA_HEADS * GLA_DK), GLA_LOW_RANK ** -0.5),
        "gla_gate_b": nrm(ks[10], (DEPTH, GLA_HEADS * GLA_DK), 0.1),
        "gla_norm_w": gain(ks[11], GLA_DV),
        "swa_sinks": nrm(ks[12], (DEPTH, SWA_HEADS), 1.0),
        "w_out": nrm(ks[13], (DEPTH, MIX_WIDTH, D_MODEL), MIX_WIDTH ** -0.5),
        "w_post_mix": gain(ks[14], D_MODEL),
        "w_pre_ffn": gain(ks[15], D_MODEL),
        "w_gate": nrm(ks[16], (DEPTH, D_MODEL, D_FF), D_MODEL ** -0.5),
        "w_up": nrm(ks[17], (DEPTH, D_MODEL, D_FF), D_MODEL ** -0.5),
        "w_down": nrm(ks[18], (DEPTH, D_FF, D_MODEL), D_FF ** -0.5),
        "w_post_ffn": gain(ks[19], D_MODEL),
        "w_ple_gate": nrm(ks[20], (DEPTH, D_MODEL, D_MODEL), D_MODEL ** -0.5),
        "w_ple_proj": nrm(ks[21], (DEPTH, PLE_DIM, D_MODEL), PLE_DIM ** -0.5),
    }

def reference(x_prompt, x_sample, p_prompt, p_sample, state_gla, cache_swa_k, cache_swa_v,
              w_pre_mix, w_in, gla_gate_up, gla_gate_b, gla_norm_w, swa_sinks, w_out,
              w_post_mix, w_pre_ffn, w_gate, w_up, w_down, w_post_ffn, w_ple_gate, w_ple_proj):
    h_p, h_s = x_prompt, x_sample
    gla_p, k_p, v_p, gla_s, k_s, v_s = [], [], [], [], [], []
    for i in range(DEPTH):
        lw = (w_pre_mix[i], w_in[i], gla_gate_up[i], gla_gate_b[i], gla_norm_w[i], swa_sinks[i],
              w_out[i], w_post_mix[i], w_pre_ffn[i], w_gate[i], w_up[i], w_down[i], w_post_ffn[i],
              w_ple_gate[i], w_ple_proj[i])
        h_p, sg, kb, vb = trunk_layer(h_p, p_prompt[i], None, None, None, *lw, is_prompt=True)
        gla_p.append(sg); k_p.append(kb); v_p.append(vb)
        h_s, sg, kb, vb = trunk_layer(h_s, p_sample[i], state_gla[i], cache_swa_k[i], cache_swa_v[i],
                                      *lw, is_prompt=False)
        gla_s.append(sg); k_s.append(kb); v_s.append(vb)
    return (h_p, h_s, jnp.stack(gla_p), jnp.stack(k_p), jnp.stack(v_p),
            jnp.stack(gla_s), jnp.stack(k_s), jnp.stack(v_s))


_drawn_inputs = setup_inputs


def setup_inputs(seed=0):
    import zlib

    import numpy as np

    out = dict(_drawn_inputs(seed))
    spreads = {}
    factors = {'swa_sinks': 2.744}
    for name, (base, spread) in spreads.items():
        noise = np.random.default_rng([zlib.crc32(name.encode()), seed]).standard_normal(out[name].shape)
        drawn = base * np.exp(spread * noise) if base else spread * noise
        out[name] = __import__('jax').numpy.asarray(drawn.astype(out[name].dtype))
    for name, factor in factors.items():
        out[name] = (out[name] * factor).astype(out[name].dtype)
    return out
```

```python
from contextlib import ExitStack

import numpy as np
import concourse.bass as bass
from concourse import mybir

f32 = mybir.dt.float32
f32r = mybir.dt.float32r
u32 = mybir.dt.uint32
ACT = mybir.ActivationFunctionType
ALU = mybir.AluOpType
AX = mybir.AxisListType

P = 128
D_MODEL, SEQ, DEC_BATCH, DEC_SEQ, PLE_DIM, D_FF = 1024, 2048, 8, 8, 256, 2816
HEADS, DK, DV, LOW_RANK, KV_HEADS, SWA_DIM, WINDOW = 8, 32, 64, 16, 2, 64, 128
GATE_NORM, EPS = 16.0, 1e-6
CHUNKS = 4
PT = SEQ // CHUNKS
TILES = PT // P
DB = DEC_BATCH // CHUNKS
DT = DB * DEC_SEQ
T = PT + DT
H = T // 2
KM = D_MODEL // P
KF = D_FF // P // 2
KP = PLE_DIM // P
KVT = P + DT
SCALE_G = DK ** -0.5
SCALE_S = SWA_DIM ** -0.5
FAR = 1e32
NEG = -1e30

ZQ, ZK, ZV, ZO, ZSQ, ZSK, ZSV, ZN = 0, 2, 4, 8, 12, 16, 17, 18
LEVELS = 7
DEC_LEVELS = 3
SLOPES = [2.0 ** (-8.0 * (h + 1) / HEADS) for h in range(HEADS)]

PHASES = [("z", ZN, KM), ("out", KM, KM), ("gu0", 2 * KF, KM), ("dn0", KM, KF),
          ("gu1", 2 * KF, KM), ("dn1", KM, KF), ("ple", KM, KM + KP)]
UNITS = sum(n for _, n, _ in PHASES)
PAIRS = UNITS // 2
PAIR0 = [sum(n for _, n, _ in PHASES[:i]) // 2 for i in range(len(PHASES) + 1)]
WCOLS = max(k for _, _, k in PHASES) * P

W_PRE, W_POST, W_FFN, W_PFFN, C_GB, C_HN, C_EPS, N_COLS = 0, KM, 2 * KM, 3 * KM, 4 * KM, 4 * KM + 2, 4 * KM + 3, 4 * KM + 4


class Signal:

    def __init__(self, sem, chunk, first=0, unit=1):
        self.sem, self.chunk, self.first, self.unit = sem, chunk, first, unit

    def at(self, c, k):
        return c * (self.chunk * self.unit) + (k + self.first) * self.unit


class TileSignal:

    def __init__(self, sem, tile, dec):
        self.sem, self.tile, self.dec = sem, tile, dec

    def at(self, c, t, k):
        return c * (TILES * self.tile + self.dec) + t * self.tile + k

    def chunk_end(self, c):
        return self.at(c, TILES, self.dec)


def build(nc, A, O):
    ctx = ExitStack()
    with ctx:
        def sb(name, shape, dt=f32):
            return ctx.enter_context(nc.sbuf_tensor(name, shape, dt))

        def sem(name):
            return ctx.enter_context(nc.semaphore(name))

        x = sb("x", [P, KM, T])
        mix = sb("mix", [P, KM, T])
        w_raw = [sb(f"w_raw{s}", [P, WCOLS]) for s in range(2)]
        wh = [sb(f"wh{s}", [P, WCOLS], f32r) for s in range(2)]
        wl = [sb(f"wl{s}", [P, WCOLS], f32r) for s in range(2)]
        lr_raw = sb("lr_raw", [P, KM, LOW_RANK])
        lrh = sb("lrh", [P, KM, LOW_RANK], f32r)
        lrl = sb("lrl", [P, KM, LOW_RANK], f32r)
        gate_up = sb("gate_up", [LOW_RANK, 2 * P])
        cols = sb("cols", [P, N_COLS])
        mean_w = sb("mean_w", [P, P])
        head_w = sb("head_w", [P, P])
        ident = sb("ident", [P, P])
        head_mask = sb("head_mask", [P, 4])
        block_mask = sb("block_mask", [P, 4 * DV])
        lev_mask = sb("lev_mask", [P, LEVELS, P // 2], u32)
        keep = sb("keep", [P, 2 * T])
        dist = sb("dist", [P, 2, P])
        dist_prev = sb("dist_prev", [P, P])
        bias_dec = sb("bias_dec", [P, P + DT])
        sinks = sb("sinks", [P, HEADS])
        sink_dec = sb("sink_dec", [P, 1])
        rs = sb("rs", [P, T])
        tmp_a = sb("tmp_a", [P, T])
        tmp = sb("tmp", [P, 2, T])
        S = sb("S", [P, 2, 4 * DV])
        Sd = sb("Sd", [P, DB, 2, 4 * DV])
        kwin = sb("kwin", [P, 2, 2, P])
        kdec = sb("kdec", [P, DB, 2, P + DT])
        vsp = sb("vsp", [P, 2, 4 * DV])
        vdec = sb("vdec", [P, DB, 4 * DV])
        vpad = sb("vpad", [P, HEADS * P])
        ke2 = sb("ke2", [P, DB, 2, DT])
        st = sb("st", [P, 9, 16])
        st_dec = sb("st_dec", [P, 8])

        def region(name, bytes_):
            return nc.bump_sbuf(bytes_)[0] if False else ctx.enter_context(
                nc.sbuf_tensor(name, [P, bytes_ // 4], f32)), bytes_

        class Region:
            def __init__(self, offset, size):
                self.offset, self.size, self.used = offset, size, 0

            def put(self, name, shape, dt=f32, at=None):
                n = int(np.prod(shape[1:])) * 4
                o = self.used if at is None else at
                assert o + n <= self.size, (name, o + n, self.size)
                self.used = max(self.used, o + n)
                return nc.alloc_sbuf_tensor_at(name, shape, dt, offset=self.offset + o)

        free = nc.sbuf_base
        sz_a, sz_p, sz_f = 2 * KM * T * 4, 3 * KP * T * 4, 2 * KF * T * 4
        arena = sb("arena", [P, (sz_a + sz_p + sz_f) // 4])
        ra = Region(free, sz_a)
        ah = ra.put("ah", [P, KM, T], f32r)
        al = ra.put("al", [P, KM, T], f32r)
        ra.used = 0
        qm = ra.put("qm", [P, 2, 4, P])
        e_lev = [ra.put(f"e_lev{i}", [P, 2, P]) for i in range(2)]
        kd = [ra.put(f"kd{i}", [P, 2, P]) for i in range(2)]
        qd = [ra.put(f"qd{i}", [P, 2, 4, P // 2]) for i in range(2)]
        A_t = ra.put("A_t", [P, HEADS, P])
        gla_end = ra.used
        sc = ra.put("sc", [P, 4, 2, 2, P], at=0)
        pt = ra.put("pt", [P, 2, 2, 4 * P], at=8192)
        ra.used = gla_end
        eg = ra.put("eg", [P, 2, P])
        ke = ra.put("ke", [P, 2, P])
        qe = ra.put("qe", [P, 2, P])
        gt = ra.put("gt", [P, 2, P])
        ktok = ra.put("ktok", [P, DB, 2 * P])
        um = ra.put("um", [P, DB, 2, 4 * DV])
        sq = ra.put("sq", [P, 4 * P])
        nrm = [ra.put(f"nrm{i}", [P, 4 * P]) for i in range(2)]
        gend = ra.put("gend", [P, 2, DB])
        scf = sc[:, :, :, :, :].rearrange("p m h g k -> p (m h g k)")
        ptf = pt[:, :, :, :].rearrange("p h g k -> p (h g k)")
        rp = Region(free + sz_a, sz_p)
        p_raw = rp.put("p_raw", [P, KP, T])
        ph = rp.put("ph", [P, KP, T], f32r)
        pl = rp.put("pl", [P, KP, T], f32r)
        rp.used = 0
        zt = rp.put("zt", [P, ZN, P])
        rf = Region(free + sz_a + sz_p, sz_f)
        gh = rf.put("gh", [P, KF, T], f32r)
        gl = rf.put("gl", [P, KF, T], f32r)
        rf.used = 0
        z = rf.put("z", [P, ZN, T])
        G = rf.put("G", [P, 2, T])
        lr_t = rf.put("lr_t", [LOW_RANK, T])
        squares = z[:, 0:KM, :]

        ps = ctx.enter_context(nc.psum_tensor("ps", [P, 8, 512], f32))

        def acc(s):
            return ps[:, 2 * s:2 * s + 2, 0:H]

        def half2(ap):
            return ap.rearrange("p (a b) -> p a b", a=2)

        def at(tensor, i):
            return tensor[:, i, :] if isinstance(i, int) else \
                tensor[:, bass.ds(i, 1), :].rearrange("p u n -> p (u n)")

        def ready_f32(ap):
            return ap.bitcast(f32)

        consts_in = sem("consts_in")
        consts_set = sem("consts_set")
        w_in = [sem(f"w_in{s}") for s in range(2)]
        w_hi = Signal(sem("w_hi"), UNITS)
        w_lo = Signal(sem("w_lo"), UNITS, 2)
        w_used = Signal(sem("w_used"), UNITS, 2)
        drained = [Signal(sem(f"drained{s}"), PAIRS, 1) for s in range(2)]
        x_in = Signal(sem("x_in"), 1, unit=16)
        p_in = Signal(sem("p_in"), 1, unit=16)
        p_hi = Signal(sem("p_hi"), 1)
        p_lo = Signal(sem("p_lo"), 1)
        y_out = Signal(sem("y_out"), 1, unit=16)
        sq_done = Signal(sem("sq_done"), 4)
        ss_done = Signal(sem("ss_done"), 4)
        ss_mean = Signal(sem("ss_mean"), 4)
        rs_guess = Signal(sem("rs_guess"), 8)
        rs_newton = Signal(sem("rs_newton"), 16)
        normed = Signal(sem("normed"), 2 * KM)
        a_hi = Signal(sem("a_hi"), 4 * KM)
        a_lo = Signal(sem("a_lo"), 4 * KM)
        branch = Signal(sem("branch"), 2 * KM)
        res = Signal(sem("res"), 3 * KM)
        gu_hi = Signal(sem("gu_hi"), 2 * KF)
        gu_lo = Signal(sem("gu_lo"), 2 * KF, 1)
        sig = Signal(sem("sig"), KM)
        lr_sum = Signal(sem("lr_sum"), 1)
        lr_got = Signal(sem("lr_got"), 1)
        gate_sum = Signal(sem("gate_sum"), 1)
        gate_act = Signal(sem("gate_act"), 2)
        gate_vec = Signal(sem("gate_vec"), 5)
        og_silu = Signal(sem("og_silu"), 1)
        L, LD = LEVELS, DEC_LEVELS
        v_q = TileSignal(sem("v_q"), 4, 4)
        a_stage = TileSignal(sem("a_stage"), 5, 5)
        t_diag = TileSignal(sem("t_diag"), 1, 1)
        v_diag = TileSignal(sem("v_diag"), 2, 2)
        t_vt = TileSignal(sem("t_vt"), 1, 1)
        a_vt = TileSignal(sem("a_vt"), 2, 2)
        t_sc = TileSignal(sem("t_sc"), 1, 1)
        v_sc = TileSignal(sem("v_sc"), 9, 1)
        v_diff = TileSignal(sem("v_diff"), 2 * L, 2 * LD)
        a_lev = TileSignal(sem("a_lev"), L, LD)
        v_lev = TileSignal(sem("v_lev"), 3 * L, 3 * LD)
        t_lev = TileSignal(sem("t_lev"), L, LD)
        v_put = TileSignal(sem("v_put"), L, LD)
        v_gend = TileSignal(sem("v_gend"), 1, DB)
        a_eg = TileSignal(sem("a_eg"), 3, 1 + 2 * DB)
        v_qe = TileSignal(sem("v_qe"), 2, 1 + DB)
        t_kt = TileSignal(sem("t_kt"), 1, 1)
        a_kt = TileSignal(sem("a_kt"), 1, 1)
        t_u = TileSignal(sem("t_u"), 1, DB)
        v_u = TileSignal(sem("v_u"), 1, DB)
        v_s = TileSignal(sem("v_s"), 2, 2 * DB)
        t_o = TileSignal(sem("t_o"), 1, 1)
        a_sq = TileSignal(sem("a_sq"), 1, 1)
        t_hn = TileSignal(sem("t_hn"), 1, 1)
        a_rs = TileSignal(sem("a_rs"), 2, 2)
        v_rs = TileSignal(sem("v_rs"), 6, 6)
        v_max = TileSignal(sem("v_max"), 5, 4)
        a_exp = TileSignal(sem("a_exp"), HEADS + 1, 2)
        v_den = TileSignal(sem("v_den"), 4, 3)
        t_pt = TileSignal(sem("t_pt"), 1, 1)
        a_pt = TileSignal(sem("a_pt"), 4, 2)
        t_pv = TileSignal(sem("t_pv"), 1, 1)
        v_pv = TileSignal(sem("v_pv"), 1, DB)
        a_shift = TileSignal(sem("a_shift"), 2, 0)
        dec_in = Signal(sem("dec_in"), 2 + DB + 4, unit=16)
        kv_out = Signal(sem("kv_out"), 1, unit=16)
        s_out = Signal(sem("s_out"), 4, unit=16)
        last_out = sem("last_out")
        passed = {e: sem(f"passed_{e}") for e in ("sp", "dve", "pe")}

        loads = [(lr_raw[:, :, :], A["w_lr"]), (gate_up[:], A["gate_up"]), (cols[:], A["cols"]),
                 (mean_w[:], A["mean_w"]), (head_w[:], A["head_w"]), (ident[:], A["ident"]),
                 (head_mask[:], A["head_mask"]), (block_mask[:], A["block_mask"]),
                 (lev_mask[:, :, :], A["lev_mask"]), (keep[:], A["keep"]), (dist[:, :, :], A["dist"]),
                 (dist_prev[:], A["dist_prev"]), (bias_dec[:], A["bias_dec"]), (sinks[:], A["sinks"]),
                 (sink_dec[:], A["sink_dec"])]
        zeroed = [S, Sd, kwin, kdec, vsp, vdec, vpad, ke2]
        N_SET = len(zeroed) + 2

        block = ctx.enter_context(nc.Block())

        W = {k: A[k].rearrange("u p n -> p u n") for k in ("w_z", "w_out", "w_gu", "w_dn", "w_ple")}
        SRC = {"z": ("w_z", 0), "out": ("w_out", 0), "gu0": ("w_gu", 0), "gu1": ("w_gu", 2 * KF),
               "dn0": ("w_dn", 0), "dn1": ("w_dn", KM), "ple": ("w_ple", 0)}

        def following(i):
            return PHASES[(i + 1) % len(PHASES)]

        def columns(tensor, lo, hi, t, w):
            if isinstance(t, int):
                return tensor[:, lo:hi, PT:PT + w]
            return tensor[:, lo:hi, bass.ds(t * P, w)]

        def padded(ap):
            return ap.rearrange("p (j a d) -> p j a d", a=4, d=DV)[:, :, 0:4:3, :]

        @block.sync
        def _(sp):
            def load_unit(c, name, u, pair, s):
                key, off = SRC[name]
                n = A[key].shape[-1]
                sp.wait_ge(w_lo.sem, c * UNITS + pair * 2 + (s + 1))
                sp.dma_start(w_raw[s][:, 0:n], at(W[key], u + off)).then_inc(w_in[s], 16)

            for s in range(2):
                sp.dma_start(w_raw[s][:, 0:KM * P], W["w_z"][:, s, :]).then_inc(w_in[s], 16)
            with sp.Fori(0, CHUNKS) as c:
                sp.dma_start(x[:, :, :], A["x"][:, bass.ds(c * (KM * T), KM * T)]
                             .rearrange("p (k t) -> p k t", k=KM)).then_inc(x_in.sem, 16)
                for i, (name, n, _) in enumerate(PHASES):
                    with sp.Fori(0, n // 2 - 1) as j:
                        for s in range(2):
                            load_unit(c, name, j * 2 + (2 + s), j + (PAIR0[i] + 1), s)
                    for s in range(2):
                        load_unit(c, following(i)[0], s, PAIR0[i + 1], s)
                sp.wait_ge(res.sem, res.at(c, 3 * KM))
                sp.sem_inc(passed["sp"])
                sp.dma_start(O["y"][:, bass.ds(c * (KM * T), KM * T)].rearrange("p (k t) -> p k t", k=KM),
                             x[:, :, :]).then_inc(y_out.sem, 16)
                sp.wait_ge(y_out.sem, y_out.at(c, 1))
                sp.sem_inc(passed["sp"])

        @block.gpsimd
        def _(gp):
            for dst, src in loads:
                gp.dma_start(dst, src).then_inc(consts_in, 16)
            gp.dma_start(O["k_keep"], A["cache_k"][:, DEC_SEQ:, :]).then_inc(last_out, 16)
            gp.dma_start(O["v_keep"], A["cache_v"][:, DEC_SEQ:, :]).then_inc(last_out, 16)
            gp.wait_ge(consts_set, N_SET)
            with gp.Fori(0, CHUNKS) as c:
                gp.wait_ge(a_lo.sem, a_lo.at(c, KM))
                for g in range(2):
                    r = slice(DV * g, DV * g + DV)
                    gp.dma_start(kdec[r, :, g, 0:P],
                                 A["cache_kT"][r, bass.ds(c * (DB * P), DB * P)].rearrange("p (b n) -> p b n", b=DB)
                                 ).then_inc(dec_in.sem, 16)
                for b in range(DB):
                    gp.dma_start(padded(vdec[:, b, :]).rearrange("p j a d -> p (j a) d"),
                                 A["cache_vr"][:, bass.ds(c * (DB * P) + b * P, P)].rearrange("p (g d) -> p g d", g=2)
                                 ).then_inc(dec_in.sem, 16)
                for h in range(4):
                    r = slice(DK * h, DK * h + DK)
                    gp.dma_start(Sd[r, :, :, DV * h:DV * h + DV].rearrange("p b q v -> p (b q) v"),
                                 A["state"][r, bass.ds(c * (DB * 2 * DV), DB * 2 * DV)]
                                 .rearrange("p (b v) -> p b v", v=DV)).then_inc(dec_in.sem, 16)
                gp.wait_ge(v_pv.sem, v_pv.chunk_end(c))
                gp.dma_start(p_raw[:, :, :], A["p"][:, bass.ds(c * (KP * T), KP * T)]
                             .rearrange("p (k t) -> p k t", k=KP)).then_inc(p_in.sem, 16)
                gp.dma_start(O["kv"][:, bass.ds(c * (2 * KVT), 2 * KVT)].rearrange("p (a t) -> p a t", a=2),
                             z[:, ZSK:ZSK + 2, T - KVT:T]).then_inc(kv_out.sem, 16)
                for h in range(4):
                    r = slice(DK * h, DK * h + DK)
                    gp.dma_start(O["state"][r, bass.ds(c * (DB * 2 * DV), DB * 2 * DV)]
                                 .rearrange("p (b v) -> p b v", v=DV),
                                 Sd[r, :, :, DV * h:DV * h + DV].rearrange("p b q v -> p (b q) v")
                                 ).then_inc(s_out.sem, 16)
                gp.wait_ge(kv_out.sem, kv_out.at(c, 1))
                gp.wait_ge(s_out.sem, s_out.at(c, 4))
            for h in range(4):
                r = slice(DK * h, DK * h + DK)
                gp.dma_start(O["state_p"][r, :, :], S[r, :, DV * h:DV * h + DV]).then_inc(last_out, 16)
            gp.wait_ge(last_out, 16 * 6)

        @block.scalar
        def _(act):
            A_ = nc.scalar.activation

            def split_hi(c, K, pair, s):
                act.wait_ge(w_in[s], c * (16 * PAIRS) + pair * 16 + 16)
                act.wait_ge(w_used.sem, c * UNITS + pair * 2 + (s + 1))
                A_(wh[s][:, 0:K * P], w_raw[s][:, 0:K * P], ACT.Copy).then_inc(w_hi.sem, 1)

            def units(c, i, work):
                _, n, K = PHASES[i]
                with act.Fori(0, n // 2 - 1) as j:
                    for s in range(2):
                        split_hi(c, K, j + (PAIR0[i] + 1), s)
                        work(j, s, j + PAIR0[i])
                for s in range(2):
                    split_hi(c, following(i)[2], PAIR0[i + 1], s)
                    work(n // 2 - 1, s, PAIR0[i + 1] - 1)

            def product_done(c, pair, s):
                act.wait_ge(w_used.sem, c * UNITS + pair * 2 + (s + 3))

            def both_drained(c, i):
                for s in range(2):
                    act.wait_ge(drained[s].sem, drained[s].at(c, PAIR0[i + 1]))

            def first_guess(c, i):
                act.wait_ge(ss_mean.sem, ss_mean.at(c, i + 1))
                A_(half2(tmp_a[:]), ps[:, 4:6, 0:H], ACT.Ln, bias=cols[:, C_EPS:C_EPS + 1]).then_inc(rs_guess.sem, 1)
                act.wait_ge(rs_guess.sem, rs_guess.at(c, 2 * i + 1))
                A_(rs[:], tmp_a[:], ACT.Exp, scale=-0.5).then_inc(rs_guess.sem, 1)

            def split_normed(c, n0):
                for k in range(KM):
                    act.wait_ge(normed.sem, normed.at(c, n0 + k + 1))
                    A_(ah[:, k, :], tmp[:, k % 2, :], ACT.Copy).then_inc(a_hi.sem, 1)

            def tile_work(c, t, w, levels):
                sample = isinstance(t, int)
                A_(zt[:, ZV:ZV + 4, 0:w], columns(z, ZV, ZV + 4, t, w), ACT.Copy).then_inc(a_stage.sem, 1)
                A_(zt[:, ZSV:ZSV + 1, 0:w], columns(z, ZSV, ZSV + 1, t, w), ACT.Copy).then_inc(a_stage.sem, 1)
                zq_, q_in = zt[:, ZSQ:ZSQ + 4, 0:w], columns(z, ZSQ, ZSQ + 4, t, w)
                if sample:
                    zq_ = zt[:, ZSQ, 0:4 * DT].rearrange("p (b m i) -> p m b i", b=DB, m=4)
                    q_in = q_in.rearrange("p m (b i) -> p m b i", b=DB)
                A_(zq_, q_in, ACT.Copy, scale=SCALE_S).then_inc(a_stage.sem, 1)
                for g in range(2):
                    r = slice(DV * g, DV * g + DV)
                    if sample:
                        if g == 0:
                            act.wait_ge(dec_in.sem, dec_in.at(c, 2 + DB + 4))
                        A_(kdec[r, :, g, P:P + DT], z[r, ZSK:ZSK + 1, PT:PT + DT].broadcast_to([DV, DB, DT]), ACT.Copy
                           ).then_inc(a_stage.sem, 1)
                    else:
                        A_(kwin[r, 1, g, :], z[r, ZSK, bass.ds(t * P, P)], ACT.Copy).then_inc(a_stage.sem, 1)
                act.wait_ge(t_vt.sem, t_vt.at(c, t, 1))
                A_(padded(vpad[0:w, :]), ps[0:w, 2, :].rearrange("p (j a d) -> p j a d", a=2, d=DV), ACT.Copy
                   ).then_inc(a_vt.sem, 1)
                A_(padded(vsp[0:w, 1, :]), ps[0:w, 3, 0:P].rearrange("p (j a d) -> p j a d", a=2, d=DV), ACT.Copy
                   ).then_inc(a_vt.sem, 1)

                def lev(l):
                    act.wait_ge(v_diff.sem, v_diff.at(c, t, 2 * l + 2))
                    A_(e_lev[l % 2][:, :, 0:w], e_lev[l % 2][:, :, 0:w], ACT.Exp, scale=1 / GATE_NORM
                       ).then_inc(a_lev.sem, 1)
                lev(0)
                A_(eg[:, :, 0:w], gt[:, :, 0:w], ACT.Exp, scale=1 / GATE_NORM).then_inc(a_eg.sem, 1)
                act.wait_ge(v_gend.sem, v_gend.at(c, t, v_gend.dec if sample else 1))
                spans = [(b, slice(DEC_SEQ * b, DEC_SEQ * b + DEC_SEQ)) for b in range(DB)] if sample \
                    else [(0, slice(0, P))]
                for q in range(2):
                    for b, r in spans:
                        A_(ke[:, q, r], gt[:, q, r], ACT.Exp, bias=gend[:, q, b:b + 1], scale=-1 / GATE_NORM
                           ).then_inc(a_eg.sem, 1)
                lev(1)
                act.wait_ge(t_kt.sem, t_kt.at(c, t, 1))
                n = 2 * P * (DB if sample else 1)
                A_(ktok[0:w, :, :].rearrange("p b n -> p (b n)")[:, 0:n], ps[0:w, 3, 0:n], ACT.Copy
                   ).then_inc(a_kt.sem, 1)
                for l in range(2, levels):
                    lev(l)
                act.wait_ge(t_o.sem, t_o.at(c, t, 1))
                A_(sq[:, 0:4 * w], ps[:, 3, 0:4 * w], ACT.Square).then_inc(a_sq.sem, 1)
                act.wait_ge(t_hn.sem, t_hn.at(c, t, 1))
                A_(nrm[0][:, 0:4 * w], ps[:, 2, 0:4 * w], ACT.Ln, bias=cols[:, C_EPS:C_EPS + 1]).then_inc(a_rs.sem, 1)
                act.wait_ge(a_rs.sem, a_rs.at(c, t, 1))
                A_(nrm[0][:, 0:4 * w], nrm[0][:, 0:4 * w], ACT.Exp, scale=-0.5).then_inc(a_rs.sem, 1)
                act.wait_ge(v_max.sem, v_max.at(c, t, 4 if sample else 5))
                if sample:
                    A_(scf[:, 0:P + DT], scf[:, 0:P + DT], ACT.Exp, bias=st_dec[:, 1:2], accum_out=st_dec[:, 3:4]
                       ).then_inc(a_exp.sem, 1)
                    A_(st_dec[:, 4:5], st_dec[:, 2:3], ACT.Exp).then_inc(a_exp.sem, 1)
                else:
                    for m in range(4):
                        for g in range(2):
                            i = 2 * m + g
                            A_(sc[:, m, :, g, :], sc[:, m, :, g, :], ACT.Exp, bias=st[:, 3, i:i + 1],
                               accum_out=st[:, 5, i:i + 1]).then_inc(a_exp.sem, 1)
                    A_(st[:, 6, 0:HEADS], st[:, 4, 0:HEADS], ACT.Exp).then_inc(a_exp.sem, 1)
                act.wait_ge(t_pt.sem, t_pt.at(c, t, 1))
                if sample:
                    A_(ptf[:, 0:P], ps[:, 4, 0:P], ACT.Copy).then_inc(a_pt.sem, 1)
                    A_(ptf[0:DT, P:2 * P], ps[0:DT, 4, P:2 * P], ACT.Copy).then_inc(a_pt.sem, 1)
                else:
                    for hf in range(2):
                        for g in range(2):
                            A_(pt[:, hf, g, :], ps[:, 4 + 2 * hf + g, :], ACT.Copy).then_inc(a_pt.sem, 1)
                    act.wait_ge(t_pv.sem, t_pv.at(c, t, 1))
                    A_(kwin[:, 0, :, :], kwin[:, 1, :, :], ACT.Copy).then_inc(a_shift.sem, 1)
                    A_(vsp[:, 0, :], vsp[:, 1, :], ACT.Copy).then_inc(a_shift.sem, 1)
                    act.wait_ge(a_shift.sem, a_shift.at(c, t, 2))

            act.wait_ge(consts_in, 16 * len(loads))
            A_(lrh[:, :, :], lr_raw[:, :, :], ACT.Copy).then_inc(consts_set, 1)
            act.wait_ge(consts_set, N_SET)
            for s in range(2):
                act.wait_ge(w_in[s], 16)
                A_(wh[s][:, 0:KM * P], w_raw[s][:, 0:KM * P], ACT.Copy).then_inc(w_hi.sem, 1)

            with act.Fori(0, CHUNKS) as c:
                act.wait_ge(x_in.sem, x_in.at(c, 1))
                A_(squares, x[:, :, :], ACT.Square).then_inc(sq_done.sem, 1)
                first_guess(c, 0)
                split_normed(c, 0)
                act.wait_ge(lr_sum.sem, lr_sum.at(c, 1))
                A_(half2(lr_t[:]), ps[0:LOW_RANK, 4:6, 0:H], ACT.Copy).then_inc(lr_got.sem, 1)
                act.wait_ge(gate_vec.sem, gate_vec.at(c, 3))
                A_(tmp[:, :, :], tmp[:, :, :], ACT.Exp).then_inc(gate_act.sem, 1)
                act.wait_ge(gate_act.sem, gate_act.at(c, 1))
                A_(tmp[:, :, :], tmp[:, :, :], ACT.Ln, bias=1.0).then_inc(gate_act.sem, 1)

                def z_work(j, s, pair):
                    if s == 1:
                        product_done(c, pair, s)
                        A_(half2(at(z, j * 2 + 1)), acc(1), ACT.Copy).then_inc(drained[1].sem, 1)
                units(c, 0, z_work)
                both_drained(c, 0)
                A_(z[:, ZO:ZO + 4, :], z[:, ZO:ZO + 4, :], ACT.Silu).then_inc(og_silu.sem, 1)

                with act.Fori(0, TILES) as t:
                    tile_work(c, t, P, LEVELS)
                tile_work(c, TILES, DT, DEC_LEVELS)
                act.wait_ge(v_pv.sem, v_pv.chunk_end(c))
                for k in range(KM):
                    A_(ah[:, k, :], mix[:, k, :], ACT.Copy).then_inc(a_hi.sem, 1)

                def out_work(j, s, pair):
                    if s == 1:
                        product_done(c, pair, s)
                        A_(half2(at(mix, j * 2 + 1)), acc(1), ACT.Copy).then_inc(drained[1].sem, 1)
                units(c, 1, out_work)
                both_drained(c, 1)
                A_(squares, mix[:, :, :], ACT.Square).then_inc(sq_done.sem, 1)
                act.wait_ge(p_in.sem, p_in.at(c, 1))
                A_(ph[:, :, :], p_raw[:, :, :], ACT.Copy).then_inc(p_hi.sem, 1)
                first_guess(c, 1)
                act.wait_ge(res.sem, res.at(c, KM))
                A_(squares, x[:, :, :], ACT.Square).then_inc(sq_done.sem, 1)
                first_guess(c, 2)
                split_normed(c, KM)

                for f in range(2):
                    if f == 0:
                        act.wait_ge(kv_out.sem, kv_out.at(c, 1))

                    def gu_work(j, s, pair):
                        product_done(c, pair, s)
                        if s == 0:
                            act.wait_ge(drained[1].sem, c * PAIRS + pair + 1)
                            A_(half2(tmp[:, 0, :]), acc(0), ACT.Silu).then_inc(drained[0].sem, 1)
                        else:
                            act.wait_ge(drained[1].sem, c * PAIRS + pair + 2)
                            A_(at(gh, j), tmp[:, 1, :], ACT.Copy).then_inc(gu_hi.sem, 1)
                    units(c, 2 + 2 * f, gu_work)
                    units(c, 3 + 2 * f, lambda j, s, pair: None)
                both_drained(c, 5)
                A_(squares, mix[:, :, :], ACT.Square).then_inc(sq_done.sem, 1)
                first_guess(c, 3)
                for k in range(KM):
                    act.wait_ge(res.sem, res.at(c, KM + k + 1))
                    A_(ah[:, k, :], x[:, k, :], ACT.Copy).then_inc(a_hi.sem, 1)

                def ple_work(j, s, pair):
                    product_done(c, pair, s)
                    act.wait_ge(res.sem, c * res.chunk + j * 2 + (2 * KM + s - 1))
                    A_(half2(tmp[:, s, :]), acc(s), ACT.Sigmoid).then_inc(sig.sem, 1)
                units(c, 6, ple_work)

        @block.vector
        def _(dve):
            V = nc.vector

            def split_lo(c, K, pair, s):
                dve.wait_ge(w_hi.sem, c * UNITS + pair * 2 + (s + 1))
                V.tensor_tensor(wl[s][:, 0:K * P], w_raw[s][:, 0:K * P], wh[s][:, 0:K * P].bitcast(f32),
                                ALU.subtract).then_inc(w_lo.sem, 1)

            def units(c, i, work):
                _, n, K = PHASES[i]
                with dve.Fori(0, n // 2 - 1) as j:
                    for s in range(2):
                        split_lo(c, K, j + (PAIR0[i] + 1), s)
                        work(j, s, j + PAIR0[i])
                for s in range(2):
                    split_lo(c, following(i)[2], PAIR0[i + 1], s)
                    work(n // 2 - 1, s, PAIR0[i + 1] - 1)

            def product_done(c, pair, s):
                dve.wait_ge(w_used.sem, c * UNITS + pair * 2 + (s + 3))

            def sum_squares(c, i):
                dve.wait_ge(sq_done.sem, sq_done.at(c, i + 1))
                V.reduce_sum(tmp_a[:], squares.rearrange("p k t -> p t k"), AX.X).then_inc(ss_done.sem, 1)

            def newton(c, i):
                steps = (
                    lambda: V.tensor_tensor(tmp_a[:], rs[:], rs[:], ALU.mult),
                    lambda: V.scalar_tensor_tensor(half2(tmp_a[:]), ps[:, 4:6, 0:H], cols[:, C_EPS:C_EPS + 1],
                                                   half2(tmp_a[:]), ALU.add, ALU.mult),
                    lambda: V.tensor_scalar(tmp_a[:], tmp_a[:], -0.5, 1.5, ALU.mult, ALU.add),
                    lambda: V.tensor_tensor(rs[:], rs[:], tmp_a[:], ALU.mult))
                dve.wait_ge(rs_guess.sem, rs_guess.at(c, 2 * i + 2))
                for n, step in enumerate(steps):
                    step().then_inc(rs_newton.sem, 1)
                    dve.wait_ge(rs_newton.sem, rs_newton.at(c, 4 * i + n + 1))

            def lo(c, a0, k, src):
                dve.wait_ge(a_hi.sem, a_hi.at(c, a0 + k + 1))
                V.tensor_tensor(al[:, k, :], src, ah[:, k, :].bitcast(f32), ALU.subtract).then_inc(a_lo.sem, 1)

            def split_normed(c, n0, a0, wcol):
                for k in range(KM + 1):
                    if k < KM:
                        if k >= 2:
                            dve.wait_ge(a_lo.sem, a_lo.at(c, a0 + k - 1))
                        V.scalar_tensor_tensor(tmp[:, k % 2, :], x[:, k, :], cols[:, wcol + k:wcol + k + 1], rs[:],
                                               ALU.mult, ALU.mult).then_inc(normed.sem, 1)
                    if k:
                        lo(c, a0, k - 1, tmp[:, (k - 1) % 2, :])

            def add_branch(c, n0, r0, wcol):
                for k in range(KM):
                    if k >= 2:
                        dve.wait_ge(res.sem, res.at(c, r0 + k - 1))
                    V.scalar_tensor_tensor(tmp[:, k % 2, :], mix[:, k, :], cols[:, wcol + k:wcol + k + 1], rs[:],
                                           ALU.mult, ALU.mult).then_inc(branch.sem, 1)
                    dve.wait_ge(branch.sem, branch.at(c, n0 + k + 1))
                    V.tensor_tensor(x[:, k, :], x[:, k, :], tmp[:, k % 2, :], ALU.add).then_inc(res.sem, 1)

            def tile_work(c, t, w, levels):
                sample = isinstance(t, int)
                rt = w // 2
                spans = [(b, slice(DEC_SEQ * b, DEC_SEQ * b + DEC_SEQ)) for b in range(DB)] if sample \
                    else [(0, slice(0, P))]
                V.tensor_copy(zt[:, 0:4, 0:w], columns(z, 0, 4, t, w)).then_inc(v_q.sem, 1)
                V.tensor_copy(gt[:, :, 0:w], columns(G, 0, 2, t, w)).then_inc(v_q.sem, 1)
                dve.wait_ge(v_q.sem, v_q.at(c, t, 2))
                for q in range(2):
                    V.scalar_tensor_tensor(
                        qm[:, q, :, 0:w], zt[:, ZQ + q:ZQ + q + 1, 0:w].broadcast_to([P, 4, w]), SCALE_G,
                        head_mask[:, :].rearrange("p (h a) -> p h a", a=1).broadcast_to([P, 4, w]),
                        ALU.mult, ALU.mult).then_inc(v_q.sem, 1)

                def split_blocks(ap, l):
                    return ap.rearrange("p q (b two s) -> p q b two s", two=2, s=1 << l)

                def diff(l):
                    s, e = 1 << l, split_blocks(e_lev[l % 2][:, :, 0:w], l)
                    g = split_blocks(gt[:, :, 0:w], l)
                    n = w // (2 * s)
                    if l >= 2:
                        dve.wait_ge(v_lev.sem, v_lev.at(c, t, 3 * (l - 1)))
                    left = g[:, :, :, 0, :]
                    mid = g[:, :, :, 0, s - 1:s].broadcast_to([P, 2, n, s])
                    V.tensor_tensor(e[:, :, :, 0, :], mid, left, ALU.subtract).then_inc(v_diff.sem, 1)
                    V.tensor_tensor(e[:, :, :, 1, :], g[:, :, :, 1, :], mid, ALU.subtract).then_inc(v_diff.sem, 1)

                def decay(l):
                    s, n = 1 << l, w >> (l + 1)
                    e = split_blocks(e_lev[l % 2][:, :, 0:w], l)
                    dve.wait_ge(a_lev.sem, a_lev.at(c, t, l + 1))
                    if l >= 2:
                        dve.wait_ge(t_lev.sem, t_lev.at(c, t, l - 1))
                    V.tensor_tensor(kd[l % 2][:, :, 0:w], zt[:, ZK:ZK + 2, 0:w], e_lev[l % 2][:, :, 0:w], ALU.mult
                                    ).then_inc(v_lev.sem, 1)
                    for q in range(2):
                        V.tensor_tensor(
                            qd[l % 2][:, q, :, 0:rt].rearrange("p h (b s) -> p h b s", s=s),
                            split_blocks(qm[:, q, :, 0:w], l)[:, :, :, 1, :],
                            e[:, q:q + 1, :, 1, :].broadcast_to([P, 4, n, s]), ALU.mult).then_inc(v_lev.sem, 1)

                def put(l):
                    s, n = 1 << l, w >> (l + 1)
                    dve.wait_ge(t_lev.sem, t_lev.at(c, t, l + 1))
                    if l:
                        dve.wait_ge(v_put.sem, v_put.at(c, t, l))
                    else:
                        dve.wait_ge(v_diag.sem, v_diag.at(c, t, 2))
                    dve.sem_inc(passed["dve"])
                    V.copy_predicated(
                        split_blocks(A_t[0:w, :, 0:w], l)[:, :, :, 1, :],
                        lev_mask[0:w, l:l + 1, 0:rt].rearrange("p h (b s) -> p h b s", s=s).broadcast_to([w, 8, n, s]),
                        ps[0:w, l % 2, 0:8 * rt].rearrange("p (h b s) -> p h b s", h=8, s=s)).then_inc(v_put.sem, 1)

                for b, r in spans:
                    V.tensor_scalar(gend[:, :, b:b + 1], gt[:, :, r.stop - 1:r.stop], 1 / GATE_NORM, None, ALU.mult
                                    ).then_inc(v_gend.sem, 1)
                diff(0)
                diff(1)
                decay(0)
                dve.wait_ge(t_diag.sem, t_diag.at(c, t, 1))
                for q in range(2):
                    V.tensor_tensor(A_t[0:w, 4 * q:4 * q + 4, 0:w],
                                    ps[0:w, q, 0:4 * w].rearrange("p (h i) -> p h i", h=4),
                                    ident[0:w, 0:w].rearrange("p (a i) -> p a i", a=1).broadcast_to([w, 4, w]),
                                    ALU.mult).then_inc(v_diag.sem, 1)
                dve.wait_ge(a_eg.sem, a_eg.at(c, t, a_eg.dec if sample else 3))
                V.scalar_tensor_tensor(qe[:, :, 0:w], zt[:, ZQ:ZQ + 2, 0:w], SCALE_G, eg[:, :, 0:w],
                                       ALU.mult, ALU.mult).then_inc(v_qe.sem, 1)
                if sample:
                    for b, r in spans:
                        V.tensor_tensor(ke2[:, b, :, r], zt[:, ZK:ZK + 2, r], ke[:, :, r], ALU.mult
                                        ).then_inc(v_qe.sem, 1)
                else:
                    V.tensor_tensor(ke[:, :, :], zt[:, ZK:ZK + 2, :], ke[:, :, :], ALU.mult).then_inc(v_qe.sem, 1)
                for l in range(1, levels):
                    if l + 1 < levels:
                        diff(l + 1)
                    decay(l)
                    put(l - 1)
                    if l == 1:
                        for b, _ in spans:
                            dve.wait_ge(t_u.sem, t_u.at(c, t, b + 1))
                            V.tensor_tensor(um[:, b, :, :], ps[:, 2 + b, :].rearrange("p (q n) -> p q n", q=2),
                                            block_mask[:, :].rearrange("p (a n) -> p a n", a=1)
                                            .broadcast_to([P, 2, 4 * DV]), ALU.mult).then_inc(v_u.sem, 1)
                put(levels - 1)
                dve.wait_ge(t_o.sem, t_o.at(c, t, 1))
                dve.wait_ge(v_u.sem, v_u.at(c, t, len(spans)))
                for b, r in spans:
                    for q in range(2):
                        state = Sd[:, b, q, :] if sample else S[:, q, :]
                        V.scalar_tensor_tensor(state, state, eg[:, q, r.stop - 1:r.stop], um[:, b, q, :],
                                               ALU.mult, ALU.add).then_inc(v_s.sem, 1)
                dve.wait_ge(t_sc.sem, t_sc.at(c, t, 1))
                if sample:
                    V.tensor_tensor(scf[:, 0:P + DT], ps[:, 4, 0:P + DT], bias_dec[:], ALU.add).then_inc(v_sc.sem, 1)
                    dve.wait_ge(v_sc.sem, v_sc.at(c, t, 1))
                    V.reduce_max(st_dec[:, 0:1], scf[:, 0:P + DT], AX.X).then_inc(v_max.sem, 1)
                    dve.wait_ge(v_max.sem, v_max.at(c, t, 1))
                    V.tensor_tensor(st_dec[:, 5:6], st_dec[:, 0:1], sink_dec[:], ALU.max).then_inc(v_max.sem, 1)
                    dve.wait_ge(v_max.sem, v_max.at(c, t, 2))
                    V.tensor_scalar(st_dec[:, 1:2], st_dec[:, 5:6], -1.0, None, ALU.mult).then_inc(v_max.sem, 1)
                    V.tensor_tensor(st_dec[:, 2:3], sink_dec[:], st_dec[:, 5:6], ALU.subtract).then_inc(v_max.sem, 1)
                else:
                    for m in range(4):
                        for g in range(2):
                            V.scalar_tensor_tensor(
                                sc[:, m, :, g, :], dist[:, :, :], -SLOPES[4 * g + m],
                                ps[:, 4 + m, :].rearrange("p (h g k) -> p h g k", h=2, g=2)[:, :, g, :],
                                ALU.mult, ALU.add).then_inc(v_sc.sem, 1)
                    dve.wait_ge(v_sc.sem, v_sc.at(c, t, 8))
                    V.tensor_copy(dist[:, 0, :], dist_prev[:]).then_inc(v_sc.sem, 1)
                    V.reduce_max(st[:, 0, :], scf.rearrange("p (a k) -> p a k", k=P), AX.X).then_inc(v_max.sem, 1)
                    dve.wait_ge(v_max.sem, v_max.at(c, t, 1))
                    mx = st[:, 0, :].rearrange("p (m h g) -> p m h g", h=2, g=2)
                    V.tensor_tensor(st[:, 1, 0:8].rearrange("p (m g) -> p m g", g=2), mx[:, :, 0, :], mx[:, :, 1, :],
                                    ALU.max).then_inc(v_max.sem, 1)
                    dve.wait_ge(v_max.sem, v_max.at(c, t, 2))
                    V.tensor_tensor(st[:, 2, 0:8], st[:, 1, 0:8], sinks[:], ALU.max).then_inc(v_max.sem, 1)
                    dve.wait_ge(v_max.sem, v_max.at(c, t, 3))
                    V.tensor_scalar(st[:, 3, 0:8], st[:, 2, 0:8], -1.0, None, ALU.mult).then_inc(v_max.sem, 1)
                    V.tensor_tensor(st[:, 4, 0:8], sinks[:], st[:, 2, 0:8], ALU.subtract).then_inc(v_max.sem, 1)
                mean, o = ps[:, 2, 0:4 * w], ps[:, 3, 0:4 * w]
                r_, h_ = nrm[0][:, 0:4 * w], nrm[1][:, 0:4 * w]
                steps = (
                    lambda: V.tensor_tensor(h_, r_, r_, ALU.mult),
                    lambda: V.scalar_tensor_tensor(h_, mean, cols[:, C_EPS:C_EPS + 1], h_, ALU.add, ALU.mult),
                    lambda: V.tensor_scalar(h_, h_, -0.5, 1.5, ALU.mult, ALU.add),
                    lambda: V.tensor_tensor(r_, r_, h_, ALU.mult),
                    lambda: V.scalar_tensor_tensor(h_, o, cols[:, C_HN:C_HN + 1], r_, ALU.mult, ALU.mult),
                    lambda: V.tensor_tensor(columns(mix, 0, 4, t, w), h_.rearrange("p (j i) -> p j i", j=4),
                                            columns(z, ZO, ZO + 4, t, w), ALU.mult))
                dve.wait_ge(a_rs.sem, a_rs.at(c, t, 2))
                for n, step in enumerate(steps):
                    step().then_inc(v_rs.sem, 1)
                    dve.wait_ge(v_rs.sem, v_rs.at(c, t, n + 1))
                if sample:
                    dve.wait_ge(a_exp.sem, a_exp.at(c, t, 2))
                    V.tensor_tensor(st_dec[:, 6:7], st_dec[:, 3:4], st_dec[:, 4:5], ALU.add).then_inc(v_den.sem, 1)
                    dve.wait_ge(v_den.sem, v_den.at(c, t, 1))
                    V.reciprocal(st_dec[:, 7:8], st_dec[:, 6:7]).then_inc(v_den.sem, 1)
                    dve.wait_ge(v_den.sem, v_den.at(c, t, 2))
                    V.tensor_scalar(scf[:, 0:P + DT], scf[:, 0:P + DT], st_dec[:, 7:8], None, ALU.mult
                                    ).then_inc(v_den.sem, 1)
                else:
                    dve.wait_ge(a_exp.sem, a_exp.at(c, t, HEADS + 1))
                    V.tensor_tensor(st[:, 7, 0:8], st[:, 5, 0:8], st[:, 6, 0:8], ALU.add).then_inc(v_den.sem, 1)
                    dve.wait_ge(v_den.sem, v_den.at(c, t, 1))
                    V.reciprocal(st[:, 8, 0:8], st[:, 7, 0:8]).then_inc(v_den.sem, 1)
                    dve.wait_ge(v_den.sem, v_den.at(c, t, 2))
                    for hf in range(2):
                        V.tensor_tensor(sc[:, :, hf, :, :], sc[:, :, hf, :, :],
                                        st[:, 8, 0:8].rearrange("p (m g a) -> p m g a", g=2, a=1)
                                        .broadcast_to([P, 4, 2, P]), ALU.mult).then_inc(v_den.sem, 1)
                dve.wait_ge(t_pv.sem, t_pv.at(c, t, 1))
                if sample:
                    for b, r in spans:
                        V.tensor_copy(mix[:, 4:8, PT + r.start:PT + r.stop],
                                      ps[:, 0, 32 * b:32 * b + 32].rearrange("p (m i) -> p m i", m=4)
                                      ).then_inc(v_pv.sem, 1)
                else:
                    V.tensor_copy(columns(mix, 4, 8, t, w), ps[:, 0, :].rearrange("p (m i) -> p m i", m=4)
                                  ).then_inc(v_pv.sem, 1)

            early = [w_lo.sem, w_lo.sem, w_used.sem, w_used.sem, drained[0].sem, drained[1].sem, gu_lo.sem]
            for s_ in early:
                V.memset(st[:, :, :], 0.0).then_inc(s_, 1)
                dve.drain()
            for b in zeroed:
                V.memset(b[:] if len(b.shape) == 2 else b[(slice(None),) * len(b.shape)], 0.0).then_inc(consts_set, 1)
            dve.wait_ge(consts_set, N_SET - 1)
            V.tensor_tensor(lrl[:, :, :], lr_raw[:, :, :], lrh[:, :, :].bitcast(f32), ALU.subtract
                            ).then_inc(consts_set, 1)
            dve.wait_ge(consts_set, N_SET)
            for s in range(2):
                dve.wait_ge(w_hi.sem, 1 + s)
                V.tensor_tensor(wl[s][:, 0:KM * P], w_raw[s][:, 0:KM * P], wh[s][:, 0:KM * P].bitcast(f32),
                                ALU.subtract).then_inc(w_lo.sem, 1)

            with dve.Fori(0, CHUNKS) as c:
                sum_squares(c, 0)
                newton(c, 0)
                split_normed(c, 0, 0, W_PRE)
                dve.wait_ge(gate_sum.sem, gate_sum.at(c, 1))
                for q in range(2):
                    V.tensor_scalar(half2(G[:, q, :]), ps[:, 4 + 2 * q:6 + 2 * q, 0:H],
                                    cols[:, C_GB + q:C_GB + q + 1], None, ALU.add).then_inc(gate_vec.sem, 1)
                dve.wait_ge(gate_vec.sem, gate_vec.at(c, 2))
                V.scalar_tensor_tensor(tmp[:, :, :], G[:, :, :], -1.0, G[:, :, :], ALU.mult, ALU.min
                                       ).then_inc(gate_vec.sem, 1)
                dve.wait_ge(gate_act.sem, gate_act.at(c, 2))
                V.scalar_tensor_tensor(tmp[:, :, :], G[:, :, :], 0.0, tmp[:, :, :], ALU.min, ALU.subtract
                                       ).then_inc(gate_vec.sem, 1)
                dve.wait_ge(gate_vec.sem, gate_vec.at(c, 4))
                V.tensor_tensor_scan(G[:, :, :].rearrange("p q t -> p (q t)"), keep[:],
                                     tmp[:, :, :].rearrange("p q t -> p (q t)"), 0.0, ALU.mult, ALU.add
                                     ).then_inc(gate_vec.sem, 1)

                def z_work(j, s, pair):
                    if s == 0:
                        product_done(c, pair, s)
                        V.tensor_copy(half2(at(z, j * 2)), acc(0)).then_inc(drained[0].sem, 1)
                units(c, 0, z_work)
                dve.wait_ge(og_silu.sem, og_silu.at(c, 1))
                dve.wait_ge(gate_vec.sem, gate_vec.at(c, 5))
                dve.wait_ge(drained[0].sem, drained[0].at(c, PAIR0[1]))
                dve.sem_inc(passed["dve"])
                with dve.Fori(0, TILES) as t:
                    tile_work(c, t, P, LEVELS)
                dve.wait_ge(dec_in.sem, dec_in.at(c, 2 + DB + 4))
                tile_work(c, TILES, DT, DEC_LEVELS)
                dve.wait_ge(v_pv.sem, v_pv.chunk_end(c))
                for k in range(KM):
                    lo(c, KM, k, mix[:, k, :])

                def out_work(j, s, pair):
                    if s == 0:
                        product_done(c, pair, s)
                        V.tensor_copy(half2(at(mix, j * 2)), acc(0)).then_inc(drained[0].sem, 1)
                units(c, 1, out_work)
                sum_squares(c, 1)
                dve.wait_ge(p_hi.sem, p_hi.at(c, 1))
                V.tensor_tensor(pl[:, :, :], p_raw[:, :, :], ph[:, :, :].bitcast(f32), ALU.subtract
                                ).then_inc(p_lo.sem, 1)
                newton(c, 1)
                add_branch(c, 0, 0, W_POST)
                sum_squares(c, 2)
                newton(c, 2)
                split_normed(c, KM, 2 * KM, W_FFN)
                for f in range(2):
                    def gu_work(j, s, pair):
                        if s == 0:
                            return
                        product_done(c, pair, s)
                        dve.wait_ge(drained[0].sem, c * PAIRS + pair + 2)
                        if f == 0:
                            dve.wait_ge(kv_out.sem, kv_out.at(c, 1))
                        dve.wait_ge(gu_lo.sem, c * gu_lo.chunk + j + (f * KF + 1))
                        V.tensor_tensor(half2(tmp[:, 1, :]), half2(tmp[:, 0, :]), acc(1), ALU.mult
                                        ).then_inc(drained[1].sem, 1)
                        dve.wait_ge(gu_hi.sem, c * gu_hi.chunk + j + (f * KF + 1))
                        V.tensor_tensor(at(gl, j), tmp[:, 1, :], at(gh, j).bitcast(f32), ALU.subtract
                                        ).then_inc(gu_lo.sem, 1)
                    units(c, 2 + 2 * f, gu_work)

                    def down_work(j, s, pair):
                        product_done(c, pair, s)
                        dst = half2(at(mix, j * 2 + s))
                        if f == 0:
                            V.tensor_copy(dst, acc(s)).then_inc(drained[s].sem, 1)
                        else:
                            V.tensor_tensor(dst, dst, acc(s), ALU.add).then_inc(drained[s].sem, 1)
                    units(c, 3 + 2 * f, down_work)
                sum_squares(c, 3)
                newton(c, 3)
                add_branch(c, KM, KM, W_PFFN)
                dve.wait_ge(res.sem, res.at(c, 2 * KM))
                for k in range(KM):
                    lo(c, 3 * KM, k, x[:, k, :])

                def ple_work(j, s, pair):
                    dve.wait_ge(sig.sem, c * KM + j * 2 + (s + 1))
                    V.tensor_tensor(half2(tmp[:, s, :]), half2(tmp[:, s, :]), ps[:, 4 + 2 * s:6 + 2 * s, 0:H], ALU.mult
                                    ).then_inc(drained[s].sem, 1)
                    dve.wait_ge(drained[s].sem, c * PAIRS + pair + 2)
                    dst = at(x, j * 2 + s)
                    V.tensor_tensor(dst, dst, tmp[:, s, :], ALU.add).then_inc(res.sem, 1)
                units(c, 6, ple_work)

        @block.tensor
        def _(pe):
            MM = nc.tensor.matmul

            def three_pass(out, k, K, whi, wlo, xhi, xlo, first):
                last = None
                for n_pass, (w_, x_) in enumerate(((whi, xhi), (whi, xlo), (wlo, xhi))):
                    for n in range(2):
                        last = MM(out[:, n, :], w_, x_[:, n * H:(n + 1) * H], start=(first and n_pass == 0),
                                  stop=(k == K - 1 and n_pass == 2))
                return last

            def unit(c, s, pair, K, hi, lo_):
                pe.wait_ge(w_lo.sem, c * UNITS + pair * 2 + (s + 3))
                pe.wait_ge(drained[s].sem, c * PAIRS + pair + 1)
                for k in range(K):
                    last = three_pass(acc(s), k, K, wh[s][:, k * P:(k + 1) * P], wl[s][:, k * P:(k + 1) * P],
                                      hi[:, k, :], lo_[:, k, :], k == 0)
                return last

            def units(c, i, hi, lo_, K, extra=None):
                _, n, _ = PHASES[i]
                with pe.Fori(0, n // 2) as j:
                    for s in range(2):
                        last = unit(c, s, j + PAIR0[i], K, hi, lo_)
                        if extra:
                            last = extra(s)
                        last.then_inc(w_used.sem, 1)

            def mean(c, i):
                pe.wait_ge(ss_done.sem, ss_done.at(c, i + 1))
                for n in range(2):
                    last = MM(ps[:, 4 + n, 0:H], mean_w[:], tmp_a[:, n * H:(n + 1) * H], start=True, stop=True)
                last.then_inc(ss_mean.sem, 1)

            def tile_work(c, t, w, levels):
                sample = isinstance(t, int)
                rt = w // 2
                spans = range(DB) if sample else range(1)
                pe.wait_ge(v_q.sem, v_q.at(c, t, 4))
                for q in range(2):
                    last = MM(ps[0:w, q, 0:4 * w].rearrange("p (h i) -> p h i", h=4), zt[:, ZK + q, 0:w],
                              qm[:, q, :, 0:w], start=True, stop=True)
                last.then_inc(t_diag.sem, 1)
                pe.wait_ge(a_stage.sem, a_stage.at(c, t, 5))
                for j in range(4):
                    nc.tensor.transpose(ps[0:w, 2, j * P:(j + 1) * P], zt[:, ZV + j, 0:w], ident[:])
                nc.tensor.transpose(ps[0:w, 3, 0:P], zt[:, ZSV, 0:w], ident[:]).then_inc(t_vt.sem, 1)
                if sample:
                    for b in range(DB):
                        for g in range(2):
                            i = 32 * (2 * b + g)
                            last = MM(ps[i:i + 32, 4, 0:P + DT],
                                      zt[:, ZSQ, 32 * b:32 * b + 32], kdec[:, b, g, :],
                                      start=True, stop=True)
                else:
                    for m in range(4):
                        last = MM(ps[:, 4 + m, :], zt[:, ZSQ + m, :], kwin[:, :, :, :].rearrange("p h g k -> p (h g k)"),
                                  start=True, stop=True)
                last.then_inc(t_sc.sem, 1)
                pe.wait_ge(v_qe.sem, v_qe.at(c, t, v_qe.dec if sample else 2))
                pe.wait_ge(a_vt.sem, a_vt.at(c, t, 2))
                for b in spans:
                    for q in range(2):
                        last = nc.tensor.transpose(ps[0:w, 3, (2 * b + q) * P:(2 * b + q + 1) * P],
                                                   ke2[:, b, q, :] if sample else ke[:, q, :], ident[:])
                last.then_inc(t_kt.sem, 1)
                pe.wait_ge(a_kt.sem, a_kt.at(c, t, 1))
                for b in spans:
                    for q in range(2):
                        last = MM(ps[:, 2 + b, q * 4 * DV:(q + 1) * 4 * DV], ktok[0:w, b, q * P:(q + 1) * P],
                                  padded(vpad[0:w, q * 4 * P:(q + 1) * 4 * P]), start=True, stop=True)
                    last.then_inc(t_u.sem, 1)
                for l in range(levels):
                    pe.wait_ge(v_lev.sem, v_lev.at(c, t, 3 * l + 3))
                    if l < 2:
                        pe.wait_ge(v_diag.sem, v_diag.at(c, t, 2))
                    else:
                        pe.wait_ge(v_put.sem, v_put.at(c, t, l - 1))
                    for q in range(2):
                        last = MM(ps[0:w, l % 2, q * 4 * rt:(q + 1) * 4 * rt].rearrange("p (h i) -> p h i", h=4),
                                  kd[l % 2][:, q, 0:w], qd[l % 2][:, q, :, 0:rt], start=True, stop=True)
                    last.then_inc(t_lev.sem, 1)
                pe.wait_ge(v_put.sem, v_put.at(c, t, levels))
                pe.wait_ge(v_u.sem, v_u.at(c, t, len(spans)))
                for j in range(4):
                    out = ps[:, 3, j * w:(j + 1) * w]
                    q = j // 2
                    for hh in range(2):
                        h = 2 * j + hh
                        MM(out, vpad[0:w, h * P:(h + 1) * P], A_t[0:w, h, 0:w], start=(hh == 0), stop=False)
                    r = slice((j % 2) * P, (j % 2) * P + P)
                    if sample:
                        for b in range(DB):
                            last = MM(out[:, DEC_SEQ * b:DEC_SEQ * b + DEC_SEQ], Sd[:, b, q, r],
                                      qe[:, q, DEC_SEQ * b:DEC_SEQ * b + DEC_SEQ], start=False, stop=(b == DB - 1))
                    else:
                        last = MM(out, S[:, q, r], qe[:, q, :], start=False, stop=True)
                last.then_inc(t_o.sem, 1)
                pe.wait_ge(a_sq.sem, a_sq.at(c, t, 1))
                MM(ps[:, 2, 0:4 * w], head_w[:], sq[:, 0:4 * w], start=True, stop=True).then_inc(t_hn.sem, 1)
                if sample:
                    pe.wait_ge(v_den.sem, v_den.at(c, t, 3))
                    nc.tensor.transpose(ps[:, 4, 0:P], scf[:, 0:P], ident[:])
                    nc.tensor.transpose(ps[0:DT, 4, P:2 * P], scf[:, P:P + DT], ident[:]).then_inc(t_pt.sem, 1)
                    pe.wait_ge(a_pt.sem, a_pt.at(c, t, 2))
                    for b in range(DB):
                        out = ps[:, 0, 32 * b:32 * b + 32]
                        for g in range(2):
                            i = 32 * (2 * b + g)
                            MM(out, vdec[:, b, g * P:(g + 1) * P], ptf[:, i:i + 32], start=(g == 0), stop=False)
                            last = MM(out, vsp[0:DT, 1, g * P:(g + 1) * P], ptf[0:DT, P + i:P + i + 32],
                                      start=False, stop=(g == 1))
                else:
                    pe.wait_ge(v_den.sem, v_den.at(c, t, 4))
                    for hf in range(2):
                        for g in range(2):
                            for m in range(4):
                                last = nc.tensor.transpose(ps[:, 4 + 2 * hf + g, m * P:(m + 1) * P],
                                                           sc[:, m, hf, g, :], ident[:])
                    last.then_inc(t_pt.sem, 1)
                    pe.wait_ge(a_pt.sem, a_pt.at(c, t, 4))
                    for i in range(4):
                        hf, g = divmod(i, 2)
                        last = MM(ps[:, 0, :], vsp[:, hf, g * P:(g + 1) * P], pt[:, hf, g, :],
                                  start=(i == 0), stop=(i == 3))
                last.then_inc(t_pv.sem, 1)

            pe.wait_ge(consts_set, N_SET)
            with pe.Fori(0, CHUNKS) as c:
                mean(c, 0)
                pe.wait_ge(a_lo.sem, a_lo.at(c, KM))
                for k in range(KM):
                    last = three_pass(ps[0:LOW_RANK, 4:6, 0:H], k, KM, lrh[:, k, :], lrl[:, k, :],
                                      ah[:, k, :], al[:, k, :], k == 0)
                last.then_inc(lr_sum.sem, 1)
                pe.wait_ge(lr_got.sem, lr_got.at(c, 1))
                for q in range(2):
                    for n in range(2):
                        last = MM(ps[:, 4 + 2 * q + n, 0:H], gate_up[:, q * P:(q + 1) * P], lr_t[:, n * H:(n + 1) * H],
                                  start=True, stop=True)
                last.then_inc(gate_sum.sem, 1)
                units(c, 0, ah, al, KM)
                with pe.Fori(0, TILES) as t:
                    tile_work(c, t, P, LEVELS)
                tile_work(c, TILES, DT, DEC_LEVELS)
                pe.wait_ge(a_lo.sem, a_lo.at(c, 2 * KM))
                pe.sem_inc(passed["pe"])
                units(c, 1, ah, al, KM)
                mean(c, 1)
                mean(c, 2)
                pe.wait_ge(a_lo.sem, a_lo.at(c, 3 * KM))
                pe.sem_inc(passed["pe"])
                for f in range(2):
                    units(c, 2 + 2 * f, ah, al, KM)
                    pe.wait_ge(gu_lo.sem, gu_lo.at(c, (f + 1) * KF))
                    pe.sem_inc(passed["pe"])
                    units(c, 3 + 2 * f, gh, gl, KF)
                mean(c, 3)
                pe.wait_ge(a_lo.sem, a_lo.at(c, 4 * KM))
                pe.wait_ge(p_lo.sem, p_lo.at(c, 1))
                pe.sem_inc(passed["pe"])

                def projection(s):
                    for k in range(KP):
                        col = slice((KM + k) * P, (KM + k + 1) * P)
                        last = three_pass(ps[:, 4 + 2 * s:6 + 2 * s, 0:H], k, KP, wh[s][:, col], wl[s][:, col],
                                          ph[:, k, :], pl[:, k, :], k == 0)
                    return last
                units(c, 6, ah, al, KM, projection)


def constants():
    part = np.arange(P)
    head_mask = (part[:, None] // DK == np.arange(4)[None]).astype(np.float32)
    lev = np.zeros((P, LEVELS, P // 2), np.uint32)
    r = np.arange(P // 2)
    for l in range(LEVELS):
        s = 1 << l
        block = r // s
        lev[:, l, :] = (part[:, None] // (2 * s) == block[None]) & (part[:, None] % (2 * s) < s)
    keep = np.ones((2, T), np.float32)
    keep[:, 0:PT:P] = 0
    keep[:, PT::DEC_SEQ] = 0
    d = part[:, None, None] - (np.arange(P)[None, None] - P * (1 - np.arange(2))[None, :, None])
    dist = np.where((d >= 0) & (d < WINDOW), d, FAR).astype(np.float32)
    first = dist.copy()
    first[:, 0, :] = FAR
    bias_dec = np.full((DB, 2, 4, DEC_SEQ, P + DT), NEG, np.float32)
    for b in range(DB):
        for g in range(2):
            for m in range(4):
                for i in range(DEC_SEQ):
                    d = P + i - np.arange(P)
                    bias_dec[b, g, m, i, :P] = np.where(d < WINDOW, -SLOPES[4 * g + m] * d, NEG)
                    for j in range(i + 1):
                        bias_dec[b, g, m, i, P + DEC_SEQ * b + j] = -SLOPES[4 * g + m] * (i - j)
    return {
        "mean_w": np.full((P, P), 1 / D_MODEL, np.float32),
        "head_w": (part[:, None] // DV == part[None] // DV).astype(np.float32) / DV,
        "ident": np.eye(P, dtype=np.float32),
        "head_mask": head_mask,
        "block_mask": np.repeat(head_mask, DV, axis=1),
        "lev_mask": lev,
        "keep": np.broadcast_to(keep.reshape(1, -1), (P, 2 * T)).copy(),
        "dist": first,
        "dist_prev": dist[:, 0, :].copy(),
        "bias_dec": bias_dec.reshape(P, P + DT),
    }


def kernel(**inputs):
    import concourse.bacc as bacc
    from concourse.bass_utils import run_bass_kernel_spmd

    a = {k: np.asarray(v) for k, v in inputs.items()}

    def by_chunk(prompt, sample):
        F = prompt.shape[-1]
        both = np.concatenate([prompt.reshape(CHUNKS, PT, F), sample.reshape(CHUNKS, DT, F)], 1)
        return np.ascontiguousarray(both.reshape(CHUNKS, T, F // P, P).transpose(3, 0, 2, 1)).reshape(P, -1)

    def as_units(w):
        K, M = w.shape
        return np.ascontiguousarray(w.reshape(K // P, P, M // P, P).transpose(2, 1, 0, 3)).reshape(M // P, P, K)

    def per_tile(v):
        return v.reshape(-1, P).T

    w_in = a["w_in"][0]
    cut = np.cumsum([256, 256, 512, 512, LOW_RANK, 512, 128, 128])
    q_g, k_g, v_g, og, lr, q_s, k_s, v_s = np.split(w_in, cut[:-1], axis=1)
    q_s = q_s.reshape(D_MODEL, 2, 4, SWA_DIM).transpose(0, 2, 1, 3).reshape(D_MODEL, 512)
    w_out = a["w_out"][0]
    swa_rows = w_out[512:].reshape(2, 4, SWA_DIM, D_MODEL).transpose(1, 0, 2, 3).reshape(512, D_MODEL)
    gate, up = as_units(a["w_gate"][0]), as_units(a["w_up"][0])
    down = a["w_down"][0]
    state = a["state_gla"][0].reshape(CHUNKS, DB, 2, 4, DK, DV)
    sinks = a["swa_sinks"][0].reshape(2, 4)
    cache_k = a["cache_swa_k"][0].reshape(DEC_BATCH, P, P)
    cache_v = a["cache_swa_v"][0].reshape(DEC_BATCH, P, P)
    arrays = {
        "x": by_chunk(a["x_prompt"][0], a["x_sample"]),
        "p": by_chunk(a["p_prompt"][0, 0], a["p_sample"][0]),
        "w_z": as_units(np.concatenate([q_g, k_g, v_g, og, q_s, k_s, v_s], 1)),
        "w_lr": np.ascontiguousarray(lr.reshape(KM, P, LOW_RANK).transpose(1, 0, 2)),
        "w_out": as_units(np.concatenate([w_out[:512], swa_rows], 0)),
        "w_gu": np.stack([gate, up], 1).reshape(4 * KF, P, D_MODEL),
        "w_dn": np.concatenate([as_units(down[:KF * P]), as_units(down[KF * P:])], 0),
        "w_ple": np.concatenate([as_units(a["w_ple_gate"][0]), as_units(a["w_ple_proj"][0])], 2),
        "gate_up": a["gla_gate_up"][0],
        "cols": np.concatenate([per_tile(a["w_pre_mix"][0]), per_tile(a["w_post_mix"][0]), per_tile(a["w_pre_ffn"][0]),
                                per_tile(a["w_post_ffn"][0]), per_tile(a["gla_gate_b"][0]),
                                np.tile(a["gla_norm_w"][0], 2)[:, None], np.full((P, 1), EPS, np.float32)], 1),
        "sinks": np.broadcast_to(sinks.T.reshape(1, HEADS), (P, HEADS)),
        "sink_dec": np.broadcast_to(sinks.reshape(1, HEADS, 1), (DB, HEADS, DEC_SEQ)).reshape(P, 1),
        "state": state.transpose(3, 4, 0, 1, 2, 5).reshape(P, CHUNKS * DB * 2 * DV),
        "cache_k": cache_k,
        "cache_v": cache_v,
        "cache_kT": cache_k.transpose(2, 0, 1).reshape(P, DEC_BATCH * P),
        "cache_vr": cache_v.transpose(1, 0, 2).reshape(P, DEC_BATCH * P),
        **constants(),
    }
    outputs = {"y": (P, CHUNKS * KM * T), "kv": (P, CHUNKS * 2 * KVT), "state": (P, CHUNKS * DB * 2 * DV),
               "state_p": (P, 2, DV), "k_keep": (DEC_BATCH, P - DEC_SEQ, P), "v_keep": (DEC_BATCH, P - DEC_SEQ, P)}

    nc = bacc.Bacc("TRN2", target_bir_lowering=False, num_devices=1)
    arrays = {f"in_{k}": np.ascontiguousarray(v) for k, v in arrays.items()}
    ins = {k[3:]: nc.dram_tensor(k, v.shape, mybir.dt.from_np(v.dtype), kind="ExternalInput").ap()
           for k, v in arrays.items()}
    outs = {k: nc.dram_tensor(f"out_{k}", s, f32, kind="ExternalOutput").ap() for k, s in outputs.items()}
    build(nc, ins, outs)
    r = run_bass_kernel_spmd(nc, [arrays], core_ids=[0]).results[0]
    o = {k: r[f"out_{k}"] for k in outputs}

    y = o["y"].reshape(P, CHUNKS, KM, T).transpose(1, 3, 2, 0).reshape(CHUNKS, T, D_MODEL)
    kv = o["kv"].reshape(P, CHUNKS, 2, KVT).transpose(2, 1, 3, 0)
    prompt_kv = kv[:, CHUNKS - 1, :P].reshape(2, 1, 1, P, KV_HEADS, SWA_DIM)
    new = kv[:, :, P:].reshape(2, DEC_BATCH, DEC_SEQ, P)
    sample_kv = [np.concatenate([o[f"{n}_keep"], new[i]], 1).reshape(1, DEC_BATCH, P, KV_HEADS, SWA_DIM)
                 for i, n in enumerate("kv")]
    state_s = o["state"].reshape(4, DK, CHUNKS, DB, 2, DV).transpose(2, 3, 4, 0, 1, 5)
    state_p = o["state_p"].reshape(4, DK, 2, DV).transpose(2, 0, 1, 3)
    return (y[:, :PT].reshape(1, SEQ, D_MODEL), y[:, PT:].reshape(DEC_BATCH, DEC_SEQ, D_MODEL),
            state_p.reshape(1, 1, HEADS, DK, DV), prompt_kv[0], prompt_kv[1],
            state_s.reshape(1, DEC_BATCH, HEADS, DK, DV), sample_kv[0], sample_kv[1])
```

```python
from contextlib import ExitStack

import numpy as np
import concourse.bass as bass
from concourse import mybir

f32 = mybir.dt.float32
f32r = mybir.dt.float32r
u32 = mybir.dt.uint32
ACT = mybir.ActivationFunctionType
ALU = mybir.AluOpType
AX = mybir.AxisListType

P = 128
D_MODEL, SEQ, DEC_BATCH, DEC_SEQ, PLE_DIM, D_FF = 1024, 2048, 8, 8, 256, 2816
HEADS, DK, DV, LOW_RANK, KV_HEADS, SWA_DIM, WINDOW = 8, 32, 64, 16, 2, 64, 128
GATE_NORM, EPS = 16.0, 1e-6
CHUNKS = 4
PT = SEQ // CHUNKS
TILES = PT // P
DB = DEC_BATCH // CHUNKS
DT = DB * DEC_SEQ
T = PT + DT
H = T // 2
KM = D_MODEL // P
KF = D_FF // P // 2
KP = PLE_DIM // P
KVT = P + DT
SCALE_G = DK ** -0.5
SCALE_S = SWA_DIM ** -0.5
FAR = 1e32
NEG = -1e30

ZQ, ZK, ZV, ZSQ, ZSK, ZSV, ZO, ZN = 0, 2, 4, 8, 12, 13, 14, 18
LEVELS = 7
DEC_LEVELS = 3
SLOPES = [2.0 ** (-8.0 * (h + 1) / HEADS) for h in range(HEADS)]

PHASES = [("og", ZN - ZO, KM), ("z", ZO, KM), ("out", KM, KM), ("gu0", 2 * KF, KM), ("dn0", KM, KF),
          ("gu1", 2 * KF, KM), ("dn1", KM, KF), ("ple", KM, KM + KP)]
OG, ZZ, OUT, GU, PLE = 0, 1, 2, 3, 7
UNITS = sum(n for _, n, _ in PHASES)
PAIRS = UNITS // 2
PAIR0 = [sum(n for _, n, _ in PHASES[:i]) // 2 for i in range(len(PHASES) + 1)]
WCOLS = max(k for _, _, k in PHASES) * P

W_PRE, W_POST, W_FFN, W_PFFN, C_GB, C_HN, C_EPS, N_COLS = 0, KM, 2 * KM, 3 * KM, 4 * KM, 4 * KM + 2, 4 * KM + 3, 4 * KM + 4


class Signal:

    def __init__(self, sem, chunk, first=0, unit=1):
        self.sem, self.chunk, self.first, self.unit = sem, chunk, first, unit

    def at(self, c, k):
        return c * (self.chunk * self.unit) + (k + self.first) * self.unit


class TileSignal:

    def __init__(self, sem, tile, dec):
        self.sem, self.tile, self.dec = sem, tile, dec

    def at(self, c, t, k):
        return c * (TILES * self.tile + self.dec) + t * self.tile + k

    def chunk_end(self, c):
        return self.at(c, TILES, self.dec)


def build(nc, A, O):
    ctx = ExitStack()
    with ctx:
        def sb(name, shape, dt=f32):
            return ctx.enter_context(nc.sbuf_tensor(name, shape, dt))

        def sem(name):
            return ctx.enter_context(nc.semaphore(name))

        x = sb("x", [P, KM, T])
        mix = sb("mix", [P, KM, T])
        w_raw = [sb(f"w_raw{s}", [P, WCOLS]) for s in range(2)]
        wh = [sb(f"wh{s}", [P, WCOLS], f32r) for s in range(2)]
        wl = [sb(f"wl{s}", [P, WCOLS], f32r) for s in range(2)]
        lr_raw = sb("lr_raw", [P, KM, LOW_RANK])
        lrh = sb("lrh", [P, KM, LOW_RANK], f32r)
        lrl = sb("lrl", [P, KM, LOW_RANK], f32r)
        gate_up = sb("gate_up", [LOW_RANK, 2 * P])
        cols = sb("cols", [P, N_COLS])
        mean_w = sb("mean_w", [P, P])
        head_w = sb("head_w", [P, P])
        ident = sb("ident", [P, P])
        head_mask = sb("head_mask", [P, 4])
        block_mask = sb("block_mask", [P, 4 * DV])
        lev_mask = sb("lev_mask", [P, LEVELS, P // 2], u32)
        keep = sb("keep", [P, 2 * T])
        dist = sb("dist", [P, 2, P])
        dist_prev = sb("dist_prev", [P, P])
        bias_dec = sb("bias_dec", [P, P + DT])
        sinks = sb("sinks", [P, HEADS])
        sink_dec = sb("sink_dec", [P, 1])
        rs = sb("rs", [P, T])
        tmp_a = sb("tmp_a", [P, T])
        tmp = sb("tmp", [P, 2, T])
        ssq = sb("ssq", [P, T])
        sqt = sb("sqt", [P, 2, T])
        S = sb("S", [P, 2, 4 * DV])
        Sd = sb("Sd", [P, DB, 2, 4 * DV])
        kwin = sb("kwin", [P, 2, 2, P])
        kdec = sb("kdec", [P, DB, 2, P + DT])
        vsp = sb("vsp", [P, 2, 4 * DV])
        vdec = sb("vdec", [P, DB, 4 * DV])
        vpad = sb("vpad", [P, HEADS * P])
        ke2 = sb("ke2", [P, DB, 2, DT])
        st = sb("st", [P, 9, 16])
        st_dec = sb("st_dec", [P, 8])

        def region(name, bytes_):
            return nc.bump_sbuf(bytes_)[0] if False else ctx.enter_context(
                nc.sbuf_tensor(name, [P, bytes_ // 4], f32)), bytes_

        class Region:
            def __init__(self, offset, size):
                self.offset, self.size, self.used = offset, size, 0

            def put(self, name, shape, dt=f32, at=None):
                n = int(np.prod(shape[1:])) * 4
                o = self.used if at is None else at
                assert o + n <= self.size, (name, o + n, self.size)
                self.used = max(self.used, o + n)
                return nc.alloc_sbuf_tensor_at(name, shape, dt, offset=self.offset + o)

        free = nc.sbuf_base
        sz_a, sz_p, sz_f = 2 * KM * T * 4, 3 * KP * T * 4, 2 * KF * T * 4
        arena = sb("arena", [P, (sz_a + sz_p + sz_f) // 4])
        ra = Region(free, sz_a)
        ah = ra.put("ah", [P, KM, T], f32r)
        al = ra.put("al", [P, KM, T], f32r)
        ra.used = 0
        qm = ra.put("qm", [P, 2, 4, P])
        e_lev = [ra.put(f"e_lev{i}", [P, 2, P]) for i in range(2)]
        kd = [ra.put(f"kd{i}", [P, 2, P]) for i in range(2)]
        qd = [ra.put(f"qd{i}", [P, 2, 4, P // 2]) for i in range(2)]
        A_t = ra.put("A_t", [P, HEADS, P])
        gla_end = ra.used
        sc = ra.put("sc", [P, 4, 2, 2, P], at=0)
        pt = ra.put("pt", [P, 2, 2, 4 * P], at=8192)
        ra.used = gla_end
        eg = ra.put("eg", [P, 2, P])
        ke = ra.put("ke", [P, 2, P])
        qe = ra.put("qe", [P, 2, P])
        gt = ra.put("gt", [P, 2, P])
        ktok = ra.put("ktok", [P, DB, 2 * P])
        um = ra.put("um", [P, DB, 2, 4 * DV])
        o_sq = ra.put("o_sq", [P, 4 * P])
        nrm = [ra.put(f"nrm{i}", [P, 4 * P]) for i in range(2)]
        gend = ra.put("gend", [P, 2, DB])
        scf = sc[:, :, :, :, :].rearrange("p m h g k -> p (m h g k)")
        ptf = pt[:, :, :, :].rearrange("p h g k -> p (h g k)")
        rp = Region(free + sz_a, sz_p)
        p_raw = rp.put("p_raw", [P, KP, T])
        ph = rp.put("ph", [P, KP, T], f32r)
        pl = rp.put("pl", [P, KP, T], f32r)
        rp.used = 0
        zt = rp.put("zt", [P, ZO, P])
        rf = Region(free + sz_a + sz_p, sz_f)
        gh = rf.put("gh", [P, KF, T], f32r)
        gl = rf.put("gl", [P, KF, T], f32r)
        rf.used = 0
        z = rf.put("z", [P, ZN, T])
        G = rf.put("G", [P, 2, T])
        lr_t = rf.put("lr_t", [LOW_RANK, T])

        ps = ctx.enter_context(nc.psum_tensor("ps", [P, 8, 512], f32))

        def acc(s):
            return ps[:, 2 * s:2 * s + 2, 0:H]

        def half2(ap):
            return ap.rearrange("p (a b) -> p a b", a=2)

        def at(tensor, i):
            return tensor[:, i, :] if isinstance(i, int) else \
                tensor[:, bass.ds(i, 1), :].rearrange("p u n -> p (u n)")

        def ready_f32(ap):
            return ap.bitcast(f32)

        consts_in = sem("consts_in")
        consts_set = sem("consts_set")
        w_in = [sem(f"w_in{s}") for s in range(2)]
        w_hi = Signal(sem("w_hi"), UNITS)
        w_lo = Signal(sem("w_lo"), UNITS, 2)
        w_used = Signal(sem("w_used"), UNITS, 2)
        drained = [Signal(sem(f"drained{s}"), PAIRS, 1) for s in range(2)]
        x_in = [Signal(sem(f"x_in{s}"), KM // 2, unit=16) for s in range(2)]
        y_out = [Signal(sem(f"y_out{s}"), KM // 2, unit=16) for s in range(2)]
        p_in = Signal(sem("p_in"), 1, unit=16)
        p_hi = Signal(sem("p_hi"), 1)
        p_lo = Signal(sem("p_lo"), 1)
        sq_x = Signal(sem("sq_x"), KM)
        sq = Signal(sem("sq"), 3 * KM)
        ss = Signal(sem("ss"), 4 * (KM - 2))
        ss_mean = Signal(sem("ss_mean"), 4)
        rs_guess = Signal(sem("rs_guess"), 8)
        rs_newton = Signal(sem("rs_newton"), 12)
        a_hi = Signal(sem("a_hi"), 4 * KM)
        a_lo = Signal(sem("a_lo"), 4 * KM)
        branch = Signal(sem("branch"), 2 * KM)
        res = Signal(sem("res"), 3 * KM)
        gu_hi = Signal(sem("gu_hi"), 2 * KF)
        gu_lo = Signal(sem("gu_lo"), 2 * KF, 1)
        sig = Signal(sem("sig"), 2 * KF)
        prod = Signal(sem("prod"), 2 * KF)
        sigm = Signal(sem("sigm"), KM)
        lr_sum = Signal(sem("lr_sum"), 1)
        lr_got = Signal(sem("lr_got"), 1)
        gate_sum = Signal(sem("gate_sum"), 1)
        gate_act = Signal(sem("gate_act"), 2)
        gate_vec = Signal(sem("gate_vec"), 5)
        og_silu = Signal(sem("og_silu"), 1)
        L, LD = LEVELS, DEC_LEVELS
        v_q = TileSignal(sem("v_q"), 4, 4)
        a_stage = TileSignal(sem("a_stage"), 5, 5)
        t_diag = TileSignal(sem("t_diag"), 1, 1)
        v_diag = TileSignal(sem("v_diag"), 2, 2)
        t_vt = TileSignal(sem("t_vt"), 1, 1)
        a_vt = TileSignal(sem("a_vt"), 2, 2)
        t_sc = TileSignal(sem("t_sc"), 1, 1)
        v_sc = TileSignal(sem("v_sc"), 9, 1)
        v_diff = TileSignal(sem("v_diff"), 2 * L, 2 * LD)
        a_lev = TileSignal(sem("a_lev"), L, LD)
        v_lev = TileSignal(sem("v_lev"), 3 * L, 3 * LD)
        t_lev = TileSignal(sem("t_lev"), L, LD)
        v_put = TileSignal(sem("v_put"), L, LD)
        v_gend = TileSignal(sem("v_gend"), 1, DB)
        a_eg = TileSignal(sem("a_eg"), 3, 1 + 2 * DB)
        v_qe = TileSignal(sem("v_qe"), 2, 1 + DB)
        t_kt = TileSignal(sem("t_kt"), 1, 1)
        a_kt = TileSignal(sem("a_kt"), 1, 1)
        t_u = TileSignal(sem("t_u"), 1, DB)
        v_u = TileSignal(sem("v_u"), 1, DB)
        v_s = TileSignal(sem("v_s"), 2, 2 * DB)
        t_o = TileSignal(sem("t_o"), 1, 1)
        a_sq = TileSignal(sem("a_sq"), 1, 1)
        t_hn = TileSignal(sem("t_hn"), 1, 1)
        a_rs = TileSignal(sem("a_rs"), 2, 2)
        v_rs = TileSignal(sem("v_rs"), 6, 6)
        v_max = TileSignal(sem("v_max"), 5, 4)
        a_exp = TileSignal(sem("a_exp"), HEADS + 1, 2)
        v_den = TileSignal(sem("v_den"), 4, 3)
        t_pt = TileSignal(sem("t_pt"), 1, 1)
        a_pt = TileSignal(sem("a_pt"), 4, 2)
        t_pv = TileSignal(sem("t_pv"), 1, 1)
        v_pv = TileSignal(sem("v_pv"), 1, DB)
        a_shift = TileSignal(sem("a_shift"), 2, 0)
        dec_in = Signal(sem("dec_in"), 2 + DB + 4, unit=16)
        kv_out = Signal(sem("kv_out"), 1, unit=16)
        s_out = Signal(sem("s_out"), 4, unit=16)
        last_out = sem("last_out")
        passed = {e: sem(f"passed_{e}") for e in ("sp", "dve", "pe")}

        loads = [(lr_raw[:, :, :], A["w_lr"]), (gate_up[:], A["gate_up"]), (cols[:], A["cols"]),
                 (mean_w[:], A["mean_w"]), (head_w[:], A["head_w"]), (ident[:], A["ident"]),
                 (head_mask[:], A["head_mask"]), (block_mask[:], A["block_mask"]),
                 (lev_mask[:, :, :], A["lev_mask"]), (keep[:], A["keep"]), (dist[:, :, :], A["dist"]),
                 (dist_prev[:], A["dist_prev"]), (bias_dec[:], A["bias_dec"]), (sinks[:], A["sinks"]),
                 (sink_dec[:], A["sink_dec"])]
        zeroed = [S, Sd, kwin, kdec, vsp, vdec, vpad, ke2]
        N_SET = len(zeroed) + 4

        block = ctx.enter_context(nc.Block())

        W = {k: A[k].rearrange("u p n -> p u n") for k in ("w_z", "w_out", "w_gu", "w_dn", "w_ple")}
        SRC = {"og": ("w_z", ZO), "z": ("w_z", 0), "out": ("w_out", 0), "gu0": ("w_gu", 0), "gu1": ("w_gu", 2 * KF),
               "dn0": ("w_dn", 0), "dn1": ("w_dn", KM), "ple": ("w_ple", 0)}

        def following(i):
            return PHASES[(i + 1) % len(PHASES)]

        def columns(tensor, lo, hi, t, w):
            if isinstance(t, int):
                return tensor[:, lo:hi, PT:PT + w]
            return tensor[:, lo:hi, bass.ds(t * P, w)]

        def padded(ap):
            return ap.rearrange("p (j a d) -> p j a d", a=4, d=DV)[:, :, 0:4:3, :]

        @block.sync
        def _(sp):
            def load_unit(c, name, u, pair, s):
                key, off = SRC[name]
                n = A[key].shape[-1]
                sp.wait_ge(w_lo.sem, c * UNITS + pair * 2 + (s + 1))
                sp.dma_start(w_raw[s][:, 0:n], at(W[key], u + off)).then_inc(w_in[s], 16)

            for s in range(2):
                sp.dma_start(w_raw[s][:, 0:KM * P], W["w_z"][:, ZO + s, :]).then_inc(w_in[s], 16)
            with sp.Fori(0, CHUNKS) as c:
                for i, (name, n, _) in enumerate(PHASES):
                    with sp.Fori(0, n // 2 - 1) as j:
                        for s in range(2):
                            load_unit(c, name, j * 2 + (2 + s), j + (PAIR0[i] + 1), s)
                    for s in range(2):
                        load_unit(c, following(i)[0], s, PAIR0[i + 1], s)

        @block.gpsimd
        def _(gp):
            for k in range(KM):
                if k >= 2:
                    gp.wait_ge(x_in[k % 2].sem, 16 * (k // 2))
                gp.dma_start(x[:, k, :], A["x"][:, k * T:(k + 1) * T]).then_inc(x_in[k % 2].sem, 16)
                for dst, src in loads[2 * k:2 * k + 2]:
                    gp.dma_start(dst, src).then_inc(consts_in, 16)
            assert len(loads) <= 2 * KM
            gp.dma_start(O["k_keep"], A["cache_k"][:, DEC_SEQ:, :]).then_inc(last_out, 16)
            gp.dma_start(O["v_keep"], A["cache_v"][:, DEC_SEQ:, :]).then_inc(last_out, 16)
            gp.wait_ge(consts_set, N_SET)

            def x_square(c, k):
                gp.wait_ge(x_in[k % 2].sem, x_in[k % 2].at(c, k // 2 + 1))
                if k >= 3:
                    gp.wait_ge(ss.sem, ss.at(c, k - 2))
                nc.gpsimd.tensor_tensor(sqt[:, k % 2, :] if k else ssq[:], x[:, k, :], x[:, k, :], ALU.mult
                                        ).then_inc(sq_x.sem, 1)
                if 1 <= k < KM - 1:
                    gp.wait_ge(sq_x.sem, sq_x.at(c, k + 1))
                    if k >= 2:
                        gp.wait_ge(ss.sem, ss.at(c, k - 1))
                    nc.gpsimd.tensor_tensor(ssq[:], ssq[:], sqt[:, k % 2, :], ALU.add).then_inc(ss.sem, 1)

            def add_squares(c, i):
                for k in range(1, KM - 1):
                    gp.wait_ge(sq.sem, sq.at(c, (i - 1) * KM + k + 1))
                    if k >= 2:
                        gp.wait_ge(ss.sem, ss.at(c, i * (KM - 2) + k - 1))
                    nc.gpsimd.tensor_tensor(ssq[:], ssq[:], sqt[:, k % 2, :], ALU.add).then_inc(ss.sem, 1)

            def chunk(c, last):
                gp.wait_ge(a_lo.sem, a_lo.at(c, KM))
                for g in range(2):
                    r = slice(DV * g, DV * g + DV)
                    gp.dma_start(kdec[r, :, g, 0:P],
                                 A["cache_kT"][r, bass.ds(c * (DB * P), DB * P)].rearrange("p (b n) -> p b n", b=DB)
                                 ).then_inc(dec_in.sem, 16)
                for b in range(DB):
                    gp.dma_start(padded(vdec[:, b, :]).rearrange("p j a d -> p (j a) d"),
                                 A["cache_vr"][:, bass.ds(c * (DB * P) + b * P, P)].rearrange("p (g d) -> p g d", g=2)
                                 ).then_inc(dec_in.sem, 16)
                for h in range(4):
                    r = slice(DK * h, DK * h + DK)
                    gp.dma_start(Sd[r, :, :, DV * h:DV * h + DV].rearrange("p b q v -> p (b q) v"),
                                 A["state"][r, bass.ds(c * (DB * 2 * DV), DB * 2 * DV)]
                                 .rearrange("p (b v) -> p b v", v=DV)).then_inc(dec_in.sem, 16)
                gp.wait_ge(v_pv.sem, v_pv.chunk_end(c))
                gp.dma_start(p_raw[:, :, :], A["p"][:, bass.ds(c * (KP * T), KP * T)]
                             .rearrange("p (k t) -> p k t", k=KP)).then_inc(p_in.sem, 16)
                gp.dma_start(O["kv"][:, bass.ds(c * (2 * KVT), 2 * KVT)].rearrange("p (a t) -> p a t", a=2),
                             z[:, ZSK:ZSK + 2, T - KVT:T]).then_inc(kv_out.sem, 16)
                for h in range(4):
                    r = slice(DK * h, DK * h + DK)
                    gp.dma_start(O["state"][r, bass.ds(c * (DB * 2 * DV), DB * 2 * DV)]
                                 .rearrange("p (b v) -> p b v", v=DV),
                                 Sd[r, :, :, DV * h:DV * h + DV].rearrange("p b q v -> p (b q) v")
                                 ).then_inc(s_out.sem, 16)
                gp.wait_ge(kv_out.sem, kv_out.at(c, 1))
                gp.wait_ge(s_out.sem, s_out.at(c, 4))
                for i in range(1, 4):
                    add_squares(c, i)
                for k in range(KM + 2):
                    if k < KM:
                        gp.wait_ge(res.sem, res.at(c, 2 * KM + k + 1))
                        gp.dma_start(O["y"][:, bass.ds(c * (KM * T) + k * T, T)], x[:, k, :]
                                     ).then_inc(y_out[k % 2].sem, 16)
                    if 1 <= k <= KM:
                        s = (k - 1) % 2
                        gp.wait_ge(y_out[s].sem, y_out[s].at(c, (k - 1) // 2 + 1))
                        if not last:
                            gp.dma_start(x[:, k - 1, :], A["x"][:, bass.ds(c * (KM * T) + (KM + k - 1) * T, T)]
                                         ).then_inc(x_in[s].sem, 16)
                    if k >= 2 and not last:
                        x_square(c + 1, k - 2)

            for k in range(KM):
                x_square(0, k)
            with gp.Fori(0, CHUNKS - 1) as c:
                chunk(c, False)
            chunk(CHUNKS - 1, True)
            for h in range(4):
                r = slice(DK * h, DK * h + DK)
                gp.dma_start(O["state_p"][r, :, :], S[r, :, DV * h:DV * h + DV]).then_inc(last_out, 16)
            gp.wait_ge(last_out, 16 * 6)

        @block.scalar
        def _(act):
            A_ = nc.scalar.activation

            def split_hi(c, K, pair, s):
                act.wait_ge(w_in[s], c * (16 * PAIRS) + pair * 16 + 16)
                act.wait_ge(w_used.sem, c * UNITS + pair * 2 + (s + 1))
                A_(wh[s][:, 0:K * P], w_raw[s][:, 0:K * P], ACT.Copy).then_inc(w_hi.sem, 1)

            def units(c, i, work):
                _, n, K = PHASES[i]
                with act.Fori(0, n // 2 - 1) as j:
                    for s in range(2):
                        split_hi(c, K, j + (PAIR0[i] + 1), s)
                        work(j, s, j + PAIR0[i])
                for s in range(2):
                    split_hi(c, following(i)[2], PAIR0[i + 1], s)
                    work(n // 2 - 1, s, PAIR0[i + 1] - 1)

            def product_done(c, pair, s):
                act.wait_ge(w_used.sem, c * UNITS + pair * 2 + (s + 3))

            def both_drained(c, i):
                for s in range(2):
                    act.wait_ge(drained[s].sem, drained[s].at(c, PAIR0[i + 1]))

            def logs_and_exps():
                nc.scalar.preload_act_table_set("natural_log_exp_and_others")

            def first_guess(c, i):
                act.wait_ge(ss_mean.sem, ss_mean.at(c, i + 1))
                A_(half2(tmp_a[:]), ps[:, 6:8, 0:H], ACT.Ln, bias=cols[:, C_EPS:C_EPS + 1]).then_inc(rs_guess.sem, 1)
                act.wait_ge(rs_guess.sem, rs_guess.at(c, 2 * i + 1))
                A_(rs[:], tmp_a[:], ACT.Exp, scale=-0.5).then_inc(rs_guess.sem, 1)

            def square(c, i, k, src):
                if k >= 3:
                    act.wait_ge(ss.sem, ss.at(c, i * (KM - 2) + k - 2))
                A_(sqt[:, k % 2, :] if k else ssq[:], src, ACT.Square).then_inc(sq.sem, 1)

            def squares(c, i, phase, j):
                for s in range(2):
                    act.wait_ge(drained[s].sem, drained[s].at(c, PAIR0[phase] + j + 1))
                    square(c, i, 2 * j + s, mix[:, 2 * j + s, :])

            def unit_pair(c, i, j):
                _, n, K = PHASES[i]
                for s in range(2):
                    split_hi(c, K if j + 1 < n // 2 else following(i)[2], PAIR0[i] + j + 1, s)

            def tile_work(c, t, w, levels):
                sample = isinstance(t, int)
                A_(zt[:, ZV:ZV + 4, 0:w], columns(z, ZV, ZV + 4, t, w), ACT.Copy).then_inc(a_stage.sem, 1)
                A_(zt[:, ZSV:ZSV + 1, 0:w], columns(z, ZSV, ZSV + 1, t, w), ACT.Copy).then_inc(a_stage.sem, 1)
                zq_, q_in = zt[:, ZSQ:ZSQ + 4, 0:w], columns(z, ZSQ, ZSQ + 4, t, w)
                if sample:
                    zq_ = zt[:, ZSQ, 0:4 * DT].rearrange("p (b m i) -> p m b i", b=DB, m=4)
                    q_in = q_in.rearrange("p m (b i) -> p m b i", b=DB)
                A_(zq_, q_in, ACT.Copy, scale=SCALE_S).then_inc(a_stage.sem, 1)
                for g in range(2):
                    r = slice(DV * g, DV * g + DV)
                    if sample:
                        if g == 0:
                            act.wait_ge(dec_in.sem, dec_in.at(c, 2 + DB + 4))
                        A_(kdec[r, :, g, P:P + DT], z[r, ZSK:ZSK + 1, PT:PT + DT].broadcast_to([DV, DB, DT]), ACT.Copy
                           ).then_inc(a_stage.sem, 1)
                    else:
                        A_(kwin[r, 1, g, :], z[r, ZSK, bass.ds(t * P, P)], ACT.Copy).then_inc(a_stage.sem, 1)
                act.wait_ge(t_vt.sem, t_vt.at(c, t, 1))
                A_(padded(vpad[0:w, :]), ps[0:w, 2, :].rearrange("p (j a d) -> p j a d", a=2, d=DV), ACT.Copy
                   ).then_inc(a_vt.sem, 1)
                A_(padded(vsp[0:w, 1, :]), ps[0:w, 3, 0:P].rearrange("p (j a d) -> p j a d", a=2, d=DV), ACT.Copy
                   ).then_inc(a_vt.sem, 1)

                def lev(l):
                    act.wait_ge(v_diff.sem, v_diff.at(c, t, 2 * l + 2))
                    A_(e_lev[l % 2][:, :, 0:w], e_lev[l % 2][:, :, 0:w], ACT.Exp, scale=1 / GATE_NORM
                       ).then_inc(a_lev.sem, 1)
                lev(0)
                A_(eg[:, :, 0:w], gt[:, :, 0:w], ACT.Exp, scale=1 / GATE_NORM).then_inc(a_eg.sem, 1)
                act.wait_ge(v_gend.sem, v_gend.at(c, t, v_gend.dec if sample else 1))
                spans = [(b, slice(DEC_SEQ * b, DEC_SEQ * b + DEC_SEQ)) for b in range(DB)] if sample \
                    else [(0, slice(0, P))]
                for q in range(2):
                    for b, r in spans:
                        A_(ke[:, q, r], gt[:, q, r], ACT.Exp, bias=gend[:, q, b:b + 1], scale=-1 / GATE_NORM
                           ).then_inc(a_eg.sem, 1)
                lev(1)
                act.wait_ge(t_kt.sem, t_kt.at(c, t, 1))
                n = 2 * P * (DB if sample else 1)
                A_(ktok[0:w, :, :].rearrange("p b n -> p (b n)")[:, 0:n], ps[0:w, 3, 0:n], ACT.Copy
                   ).then_inc(a_kt.sem, 1)
                for l in range(2, levels):
                    lev(l)
                act.wait_ge(t_o.sem, t_o.at(c, t, 1))
                A_(o_sq[:, 0:4 * w], ps[:, 3, 0:4 * w], ACT.Square).then_inc(a_sq.sem, 1)
                act.wait_ge(t_hn.sem, t_hn.at(c, t, 1))
                A_(nrm[0][:, 0:4 * w], ps[:, 2, 0:4 * w], ACT.Ln, bias=cols[:, C_EPS:C_EPS + 1]).then_inc(a_rs.sem, 1)
                act.wait_ge(a_rs.sem, a_rs.at(c, t, 1))
                A_(nrm[0][:, 0:4 * w], nrm[0][:, 0:4 * w], ACT.Exp, scale=-0.5).then_inc(a_rs.sem, 1)
                act.wait_ge(v_max.sem, v_max.at(c, t, 4 if sample else 5))
                if sample:
                    A_(scf[:, 0:P + DT], scf[:, 0:P + DT], ACT.Exp, bias=st_dec[:, 1:2], accum_out=st_dec[:, 3:4]
                       ).then_inc(a_exp.sem, 1)
                    A_(st_dec[:, 4:5], st_dec[:, 2:3], ACT.Exp).then_inc(a_exp.sem, 1)
                else:
                    for m in range(4):
                        for g in range(2):
                            i = 2 * m + g
                            A_(sc[:, m, :, g, :], sc[:, m, :, g, :], ACT.Exp, bias=st[:, 3, i:i + 1],
                               accum_out=st[:, 5, i:i + 1]).then_inc(a_exp.sem, 1)
                    A_(st[:, 6, 0:HEADS], st[:, 4, 0:HEADS], ACT.Exp).then_inc(a_exp.sem, 1)
                act.wait_ge(t_pt.sem, t_pt.at(c, t, 1))
                if sample:
                    A_(ptf[:, 0:P], ps[:, 4, 0:P], ACT.Copy).then_inc(a_pt.sem, 1)
                    A_(ptf[0:DT, P:2 * P], ps[0:DT, 4, P:2 * P], ACT.Copy).then_inc(a_pt.sem, 1)
                else:
                    for hf in range(2):
                        for g in range(2):
                            A_(pt[:, hf, g, :], ps[:, 4 + 2 * hf + g, :], ACT.Copy).then_inc(a_pt.sem, 1)
                    act.wait_ge(t_pv.sem, t_pv.at(c, t, 1))
                    A_(kwin[:, 0, :, :], kwin[:, 1, :, :], ACT.Copy).then_inc(a_shift.sem, 1)
                    A_(vsp[:, 0, :], vsp[:, 1, :], ACT.Copy).then_inc(a_shift.sem, 1)
                    act.wait_ge(a_shift.sem, a_shift.at(c, t, 2))

            act.wait_ge(consts_in, 16 * len(loads))
            A_(lrh[:, :, :], lr_raw[:, :, :], ACT.Copy).then_inc(consts_set, 1)
            act.wait_ge(consts_set, N_SET)
            for s in range(2):
                act.wait_ge(w_in[s], 16)
                A_(wh[s][:, 0:KM * P], w_raw[s][:, 0:KM * P], ACT.Copy).then_inc(w_hi.sem, 1)

            with act.Fori(0, CHUNKS) as c:
                for k in range(KM):
                    act.wait_ge(x_in[k % 2].sem, x_in[k % 2].at(c, k // 2 + 1))
                    A_(ah[:, k, :], x[:, k, :], ACT.Copy, scale=cols[:, W_PRE + k:W_PRE + k + 1]).then_inc(a_hi.sem, 1)
                logs_and_exps()
                first_guess(c, 0)
                units(c, OG, lambda j, s, pair: None)
                both_drained(c, OG)
                A_(z[:, ZO:ZO + 4, :], z[:, ZO:ZO + 4, :], ACT.Silu).then_inc(og_silu.sem, 1)
                logs_and_exps()
                act.wait_ge(gate_vec.sem, gate_vec.at(c, 3))
                A_(tmp[:, :, :], tmp[:, :, :], ACT.Exp).then_inc(gate_act.sem, 1)
                act.wait_ge(gate_act.sem, gate_act.at(c, 1))
                A_(tmp[:, :, :], tmp[:, :, :], ACT.Ln, bias=1.0).then_inc(gate_act.sem, 1)
                units(c, ZZ, lambda j, s, pair: None)
                both_drained(c, ZZ)

                with act.Fori(0, TILES) as t:
                    tile_work(c, t, P, LEVELS)
                tile_work(c, TILES, DT, DEC_LEVELS)
                act.wait_ge(v_pv.sem, v_pv.chunk_end(c))
                for k in range(KM):
                    A_(ah[:, k, :], mix[:, k, :], ACT.Copy).then_inc(a_hi.sem, 1)

                for j in range(KM // 2):
                    unit_pair(c, OUT, j)
                    squares(c, 1, OUT, j)
                first_guess(c, 1)
                for k in range(KM):
                    act.wait_ge(res.sem, res.at(c, k + 1))
                    A_(ah[:, k, :], x[:, k, :], ACT.Copy, scale=cols[:, W_FFN + k:W_FFN + k + 1]).then_inc(a_hi.sem, 1)
                    square(c, 2, k, x[:, k, :])
                first_guess(c, 2)

                for f in range(2):
                    def gu_work(j, s, pair):
                        if s == 0:
                            act.wait_ge(drained[0].sem, c * PAIRS + pair + 2)
                            A_(tmp[:, 0, :], tmp[:, 0, :], ACT.Silu).then_inc(sig.sem, 1)
                        else:
                            act.wait_ge(prod.sem, c * prod.chunk + j + (KF * f + 1))
                            A_(at(gh, j), tmp[:, 1, :], ACT.Copy).then_inc(gu_hi.sem, 1)
                    units(c, GU + 2 * f, gu_work)
                    if f == 0:
                        act.wait_ge(p_in.sem, p_in.at(c, 1))
                        A_(ph[:, :, :], p_raw[:, :, :], ACT.Copy).then_inc(p_hi.sem, 1)
                        units(c, GU + 1, lambda j, s, pair: None)
                logs_and_exps()
                for j in range(KM // 2):
                    unit_pair(c, GU + 3, j)
                    squares(c, 3, GU + 3, j)
                first_guess(c, 3)
                for k in range(KM):
                    act.wait_ge(res.sem, res.at(c, KM + k + 1))
                    A_(ah[:, k, :], x[:, k, :], ACT.Copy).then_inc(a_hi.sem, 1)

                def ple_work(j, s, pair):
                    product_done(c, pair, s)
                    act.wait_ge(res.sem, c * res.chunk + j * 2 + (2 * KM + s - 1))
                    A_(half2(tmp[:, s, :]), acc(s), ACT.Sigmoid).then_inc(sigm.sem, 1)
                units(c, PLE, ple_work)

        @block.vector
        def _(dve):
            V = nc.vector

            def split_lo(c, K, pair, s):
                dve.wait_ge(w_hi.sem, c * UNITS + pair * 2 + (s + 1))
                V.tensor_tensor(wl[s][:, 0:K * P], w_raw[s][:, 0:K * P], wh[s][:, 0:K * P].bitcast(f32),
                                ALU.subtract).then_inc(w_lo.sem, 1)

            def units(c, i, work):
                _, n, K = PHASES[i]
                with dve.Fori(0, n // 2 - 1) as j:
                    for s in range(2):
                        split_lo(c, K, j + (PAIR0[i] + 1), s)
                        work(j, s, j + PAIR0[i])
                for s in range(2):
                    split_lo(c, following(i)[2], PAIR0[i + 1], s)
                    work(n // 2 - 1, s, PAIR0[i + 1] - 1)

            def product_done(c, pair, s):
                dve.wait_ge(w_used.sem, c * UNITS + pair * 2 + (s + 3))

            def newton(c, i):
                steps = (
                    lambda: V.tensor_tensor(tmp_a[:], rs[:], rs[:], ALU.mult),
                    lambda: V.scalar_tensor_tensor(half2(tmp_a[:]), ps[:, 6:8, 0:H], cols[:, C_EPS:C_EPS + 1],
                                                   half2(tmp_a[:]), ALU.add, ALU.mult),
                    lambda: V.scalar_tensor_tensor(rs[:], tmp_a[:], -3.0, rs[:], ALU.add, ALU.mult))
                dve.wait_ge(rs_guess.sem, rs_guess.at(c, 2 * i + 2))
                for n, step in enumerate(steps):
                    step().then_inc(rs_newton.sem, 1)
                    dve.wait_ge(rs_newton.sem, rs_newton.at(c, 3 * i + n + 1))

            def normed(dst, src, part=slice(0, P)):
                return V.scalar_tensor_tensor(dst, src, -0.5, half2(rs[part, :]), ALU.mult, ALU.mult)

            def lo(c, a0, k, src):
                dve.wait_ge(a_hi.sem, a_hi.at(c, a0 + k + 1))
                V.tensor_tensor(al[:, k, :], src, ah[:, k, :].bitcast(f32), ALU.subtract).then_inc(a_lo.sem, 1)

            def lo_weighted(c, a0, k, wcol):
                dve.wait_ge(a_hi.sem, a_hi.at(c, a0 + k + 1))
                V.scalar_tensor_tensor(al[:, k, :], x[:, k, :], cols[:, wcol + k:wcol + k + 1],
                                       ah[:, k, :].bitcast(f32), ALU.mult, ALU.subtract).then_inc(a_lo.sem, 1)

            def add_branch(c, n0, r0, wcol, then):
                for k in range(KM):
                    if k >= 2:
                        dve.wait_ge(res.sem, res.at(c, r0 + k - 1))
                    V.scalar_tensor_tensor(tmp[:, k % 2, :], mix[:, k, :], cols[:, wcol + k:wcol + k + 1], rs[:],
                                           ALU.mult, ALU.mult).then_inc(branch.sem, 1)
                    dve.wait_ge(branch.sem, branch.at(c, n0 + k + 1))
                    V.tensor_tensor(x[:, k, :], x[:, k, :], tmp[:, k % 2, :], ALU.add).then_inc(res.sem, 1)
                    if k:
                        then(k - 1)
                then(KM - 1)

            def tile_work(c, t, w, levels):
                sample = isinstance(t, int)
                rt = w // 2
                spans = [(b, slice(DEC_SEQ * b, DEC_SEQ * b + DEC_SEQ)) for b in range(DB)] if sample \
                    else [(0, slice(0, P))]
                V.tensor_copy(zt[:, 0:4, 0:w], columns(z, 0, 4, t, w)).then_inc(v_q.sem, 1)
                V.tensor_copy(gt[:, :, 0:w], columns(G, 0, 2, t, w)).then_inc(v_q.sem, 1)
                dve.wait_ge(v_q.sem, v_q.at(c, t, 2))
                for q in range(2):
                    V.scalar_tensor_tensor(
                        qm[:, q, :, 0:w], zt[:, ZQ + q:ZQ + q + 1, 0:w].broadcast_to([P, 4, w]), SCALE_G,
                        head_mask[:, :].rearrange("p (h a) -> p h a", a=1).broadcast_to([P, 4, w]),
                        ALU.mult, ALU.mult).then_inc(v_q.sem, 1)

                def split_blocks(ap, l):
                    return ap.rearrange("p q (b two s) -> p q b two s", two=2, s=1 << l)

                def diff(l):
                    s, e = 1 << l, split_blocks(e_lev[l % 2][:, :, 0:w], l)
                    g = split_blocks(gt[:, :, 0:w], l)
                    n = w // (2 * s)
                    if l >= 2:
                        dve.wait_ge(v_lev.sem, v_lev.at(c, t, 3 * (l - 1)))
                    left = g[:, :, :, 0, :]
                    mid = g[:, :, :, 0, s - 1:s].broadcast_to([P, 2, n, s])
                    V.tensor_tensor(e[:, :, :, 0, :], mid, left, ALU.subtract).then_inc(v_diff.sem, 1)
                    V.tensor_tensor(e[:, :, :, 1, :], g[:, :, :, 1, :], mid, ALU.subtract).then_inc(v_diff.sem, 1)

                def decay(l):
                    s, n = 1 << l, w >> (l + 1)
                    e = split_blocks(e_lev[l % 2][:, :, 0:w], l)
                    dve.wait_ge(a_lev.sem, a_lev.at(c, t, l + 1))
                    if l >= 2:
                        dve.wait_ge(t_lev.sem, t_lev.at(c, t, l - 1))
                    V.tensor_tensor(kd[l % 2][:, :, 0:w], zt[:, ZK:ZK + 2, 0:w], e_lev[l % 2][:, :, 0:w], ALU.mult
                                    ).then_inc(v_lev.sem, 1)
                    for q in range(2):
                        V.tensor_tensor(
                            qd[l % 2][:, q, :, 0:rt].rearrange("p h (b s) -> p h b s", s=s),
                            split_blocks(qm[:, q, :, 0:w], l)[:, :, :, 1, :],
                            e[:, q:q + 1, :, 1, :].broadcast_to([P, 4, n, s]), ALU.mult).then_inc(v_lev.sem, 1)

                def put(l):
                    s, n = 1 << l, w >> (l + 1)
                    dve.wait_ge(t_lev.sem, t_lev.at(c, t, l + 1))
                    if l:
                        dve.wait_ge(v_put.sem, v_put.at(c, t, l))
                    else:
                        dve.wait_ge(v_diag.sem, v_diag.at(c, t, 2))
                    dve.sem_inc(passed["dve"])
                    V.copy_predicated(
                        split_blocks(A_t[0:w, :, 0:w], l)[:, :, :, 1, :],
                        lev_mask[0:w, l:l + 1, 0:rt].rearrange("p h (b s) -> p h b s", s=s).broadcast_to([w, 8, n, s]),
                        ps[0:w, l % 2, 0:8 * rt].rearrange("p (h b s) -> p h b s", h=8, s=s)).then_inc(v_put.sem, 1)

                for b, r in spans:
                    V.tensor_scalar(gend[:, :, b:b + 1], gt[:, :, r.stop - 1:r.stop], 1 / GATE_NORM, None, ALU.mult
                                    ).then_inc(v_gend.sem, 1)
                diff(0)
                diff(1)
                decay(0)
                dve.wait_ge(t_diag.sem, t_diag.at(c, t, 1))
                for q in range(2):
                    V.tensor_tensor(A_t[0:w, 4 * q:4 * q + 4, 0:w],
                                    ps[0:w, q, 0:4 * w].rearrange("p (h i) -> p h i", h=4),
                                    ident[0:w, 0:w].rearrange("p (a i) -> p a i", a=1).broadcast_to([w, 4, w]),
                                    ALU.mult).then_inc(v_diag.sem, 1)
                dve.wait_ge(a_eg.sem, a_eg.at(c, t, a_eg.dec if sample else 3))
                V.scalar_tensor_tensor(qe[:, :, 0:w], zt[:, ZQ:ZQ + 2, 0:w], SCALE_G, eg[:, :, 0:w],
                                       ALU.mult, ALU.mult).then_inc(v_qe.sem, 1)
                if sample:
                    for b, r in spans:
                        V.tensor_tensor(ke2[:, b, :, r], zt[:, ZK:ZK + 2, r], ke[:, :, r], ALU.mult
                                        ).then_inc(v_qe.sem, 1)
                else:
                    V.tensor_tensor(ke[:, :, :], zt[:, ZK:ZK + 2, :], ke[:, :, :], ALU.mult).then_inc(v_qe.sem, 1)
                for l in range(1, levels):
                    if l + 1 < levels:
                        diff(l + 1)
                    decay(l)
                    put(l - 1)
                    if l == 1:
                        for b, _ in spans:
                            dve.wait_ge(t_u.sem, t_u.at(c, t, b + 1))
                            V.tensor_tensor(um[:, b, :, :], ps[:, 2 + b, :].rearrange("p (q n) -> p q n", q=2),
                                            block_mask[:, :].rearrange("p (a n) -> p a n", a=1)
                                            .broadcast_to([P, 2, 4 * DV]), ALU.mult).then_inc(v_u.sem, 1)
                put(levels - 1)
                dve.wait_ge(t_o.sem, t_o.at(c, t, 1))
                dve.wait_ge(v_u.sem, v_u.at(c, t, len(spans)))
                for b, r in spans:
                    for q in range(2):
                        state = Sd[:, b, q, :] if sample else S[:, q, :]
                        V.scalar_tensor_tensor(state, state, eg[:, q, r.stop - 1:r.stop], um[:, b, q, :],
                                               ALU.mult, ALU.add).then_inc(v_s.sem, 1)
                dve.wait_ge(t_sc.sem, t_sc.at(c, t, 1))
                if sample:
                    V.tensor_tensor(scf[:, 0:P + DT], ps[:, 4, 0:P + DT], bias_dec[:], ALU.add).then_inc(v_sc.sem, 1)
                    dve.wait_ge(v_sc.sem, v_sc.at(c, t, 1))
                    V.reduce_max(st_dec[:, 0:1], scf[:, 0:P + DT], AX.X).then_inc(v_max.sem, 1)
                    dve.wait_ge(v_max.sem, v_max.at(c, t, 1))
                    V.tensor_tensor(st_dec[:, 5:6], st_dec[:, 0:1], sink_dec[:], ALU.max).then_inc(v_max.sem, 1)
                    dve.wait_ge(v_max.sem, v_max.at(c, t, 2))
                    V.tensor_scalar(st_dec[:, 1:2], st_dec[:, 5:6], -1.0, None, ALU.mult).then_inc(v_max.sem, 1)
                    V.tensor_tensor(st_dec[:, 2:3], sink_dec[:], st_dec[:, 5:6], ALU.subtract).then_inc(v_max.sem, 1)
                else:
                    for m in range(4):
                        for g in range(2):
                            V.scalar_tensor_tensor(
                                sc[:, m, :, g, :], dist[:, :, :], -SLOPES[4 * g + m],
                                ps[:, 4 + m, :].rearrange("p (h g k) -> p h g k", h=2, g=2)[:, :, g, :],
                                ALU.mult, ALU.add).then_inc(v_sc.sem, 1)
                    dve.wait_ge(v_sc.sem, v_sc.at(c, t, 8))
                    V.tensor_copy(dist[:, 0, :], dist_prev[:]).then_inc(v_sc.sem, 1)
                    V.reduce_max(st[:, 0, :], scf.rearrange("p (a k) -> p a k", k=P), AX.X).then_inc(v_max.sem, 1)
                    dve.wait_ge(v_max.sem, v_max.at(c, t, 1))
                    mx = st[:, 0, :].rearrange("p (m h g) -> p m h g", h=2, g=2)
                    V.tensor_tensor(st[:, 1, 0:8].rearrange("p (m g) -> p m g", g=2), mx[:, :, 0, :], mx[:, :, 1, :],
                                    ALU.max).then_inc(v_max.sem, 1)
                    dve.wait_ge(v_max.sem, v_max.at(c, t, 2))
                    V.tensor_tensor(st[:, 2, 0:8], st[:, 1, 0:8], sinks[:], ALU.max).then_inc(v_max.sem, 1)
                    dve.wait_ge(v_max.sem, v_max.at(c, t, 3))
                    V.tensor_scalar(st[:, 3, 0:8], st[:, 2, 0:8], -1.0, None, ALU.mult).then_inc(v_max.sem, 1)
                    V.tensor_tensor(st[:, 4, 0:8], sinks[:], st[:, 2, 0:8], ALU.subtract).then_inc(v_max.sem, 1)
                mean, o = ps[:, 2, 0:4 * w], ps[:, 3, 0:4 * w]
                r_, h_ = nrm[0][:, 0:4 * w], nrm[1][:, 0:4 * w]
                steps = (
                    lambda: V.tensor_tensor(h_, r_, r_, ALU.mult),
                    lambda: V.scalar_tensor_tensor(h_, mean, cols[:, C_EPS:C_EPS + 1], h_, ALU.add, ALU.mult),
                    lambda: V.tensor_scalar(h_, h_, -0.5, 1.5, ALU.mult, ALU.add),
                    lambda: V.tensor_tensor(r_, r_, h_, ALU.mult),
                    lambda: V.scalar_tensor_tensor(h_, o, cols[:, C_HN:C_HN + 1], r_, ALU.mult, ALU.mult),
                    lambda: V.tensor_tensor(columns(mix, 0, 4, t, w), h_.rearrange("p (j i) -> p j i", j=4),
                                            columns(z, ZO, ZO + 4, t, w), ALU.mult))
                dve.wait_ge(a_rs.sem, a_rs.at(c, t, 2))
                for n, step in enumerate(steps):
                    step().then_inc(v_rs.sem, 1)
                    dve.wait_ge(v_rs.sem, v_rs.at(c, t, n + 1))
                if sample:
                    dve.wait_ge(a_exp.sem, a_exp.at(c, t, 2))
                    V.tensor_tensor(st_dec[:, 6:7], st_dec[:, 3:4], st_dec[:, 4:5], ALU.add).then_inc(v_den.sem, 1)
                    dve.wait_ge(v_den.sem, v_den.at(c, t, 1))
                    V.reciprocal(st_dec[:, 7:8], st_dec[:, 6:7]).then_inc(v_den.sem, 1)
                    dve.wait_ge(v_den.sem, v_den.at(c, t, 2))
                    V.tensor_scalar(scf[:, 0:P + DT], scf[:, 0:P + DT], st_dec[:, 7:8], None, ALU.mult
                                    ).then_inc(v_den.sem, 1)
                else:
                    dve.wait_ge(a_exp.sem, a_exp.at(c, t, HEADS + 1))
                    V.tensor_tensor(st[:, 7, 0:8], st[:, 5, 0:8], st[:, 6, 0:8], ALU.add).then_inc(v_den.sem, 1)
                    dve.wait_ge(v_den.sem, v_den.at(c, t, 1))
                    V.reciprocal(st[:, 8, 0:8], st[:, 7, 0:8]).then_inc(v_den.sem, 1)
                    dve.wait_ge(v_den.sem, v_den.at(c, t, 2))
                    for hf in range(2):
                        V.tensor_tensor(sc[:, :, hf, :, :], sc[:, :, hf, :, :],
                                        st[:, 8, 0:8].rearrange("p (m g a) -> p m g a", g=2, a=1)
                                        .broadcast_to([P, 4, 2, P]), ALU.mult).then_inc(v_den.sem, 1)
                dve.wait_ge(t_pv.sem, t_pv.at(c, t, 1))
                if sample:
                    for b, r in spans:
                        V.tensor_copy(mix[:, 4:8, PT + r.start:PT + r.stop],
                                      ps[:, 0, 32 * b:32 * b + 32].rearrange("p (m i) -> p m i", m=4)
                                      ).then_inc(v_pv.sem, 1)
                else:
                    V.tensor_copy(columns(mix, 4, 8, t, w), ps[:, 0, :].rearrange("p (m i) -> p m i", m=4)
                                  ).then_inc(v_pv.sem, 1)

            early = [w_lo.sem, w_lo.sem, w_used.sem, w_used.sem, drained[0].sem, drained[1].sem, gu_lo.sem]
            for s_ in early:
                V.memset(st[:, :, :], 0.0).then_inc(s_, 1)
                dve.drain()
            for b in zeroed:
                V.memset(b[:] if len(b.shape) == 2 else b[(slice(None),) * len(b.shape)], 0.0).then_inc(consts_set, 1)
            dve.wait_ge(consts_in, 16 * len(loads))
            dve.wait_ge(consts_set, N_SET - 3)
            V.tensor_tensor(lrl[:, :, :], lr_raw[:, :, :], lrh[:, :, :].bitcast(f32), ALU.subtract
                            ).then_inc(consts_set, 1)
            for wcol in (W_POST, W_PFFN):
                V.tensor_scalar(cols[:, wcol:wcol + KM], cols[:, wcol:wcol + KM], -0.5, None, ALU.mult
                                ).then_inc(consts_set, 1)
            dve.wait_ge(consts_set, N_SET)
            for s in range(2):
                dve.wait_ge(w_hi.sem, 1 + s)
                V.tensor_tensor(wl[s][:, 0:KM * P], w_raw[s][:, 0:KM * P], wh[s][:, 0:KM * P].bitcast(f32),
                                ALU.subtract).then_inc(w_lo.sem, 1)

            with dve.Fori(0, CHUNKS) as c:
                for k in range(KM):
                    lo_weighted(c, 0, k, W_PRE)
                newton(c, 0)
                dve.wait_ge(lr_sum.sem, lr_sum.at(c, 1))
                normed(half2(lr_t[:]), ps[0:LOW_RANK, 4:6, 0:H], slice(0, LOW_RANK)).then_inc(lr_got.sem, 1)

                def z_work(phase, z0):
                    def work(j, s, pair):
                        product_done(c, pair, s)
                        normed(half2(at(z, j * 2 + (z0 + s))), acc(s)).then_inc(drained[s].sem, 1)
                    units(c, phase, work)
                z_work(OG, ZO)
                dve.wait_ge(gate_sum.sem, gate_sum.at(c, 1))
                for q in range(2):
                    V.tensor_scalar(half2(G[:, q, :]), ps[:, 4 + 2 * q:6 + 2 * q, 0:H],
                                    cols[:, C_GB + q:C_GB + q + 1], None, ALU.add).then_inc(gate_vec.sem, 1)
                dve.wait_ge(gate_vec.sem, gate_vec.at(c, 2))
                V.scalar_tensor_tensor(tmp[:, :, :], G[:, :, :], -1.0, G[:, :, :], ALU.mult, ALU.min
                                       ).then_inc(gate_vec.sem, 1)
                dve.wait_ge(gate_act.sem, gate_act.at(c, 2))
                V.scalar_tensor_tensor(tmp[:, :, :], G[:, :, :], 0.0, tmp[:, :, :], ALU.min, ALU.subtract
                                       ).then_inc(gate_vec.sem, 1)
                dve.wait_ge(gate_vec.sem, gate_vec.at(c, 4))
                V.tensor_tensor_scan(G[:, :, :].rearrange("p q t -> p (q t)"), keep[:],
                                     tmp[:, :, :].rearrange("p q t -> p (q t)"), 0.0, ALU.mult, ALU.add
                                     ).then_inc(gate_vec.sem, 1)

                z_work(ZZ, 0)
                dve.wait_ge(og_silu.sem, og_silu.at(c, 1))
                dve.wait_ge(gate_vec.sem, gate_vec.at(c, 5))
                dve.wait_ge(drained[0].sem, drained[0].at(c, PAIR0[ZZ + 1]))
                dve.wait_ge(drained[1].sem, drained[1].at(c, PAIR0[ZZ + 1]))
                dve.sem_inc(passed["dve"])
                with dve.Fori(0, TILES) as t:
                    tile_work(c, t, P, LEVELS)
                dve.wait_ge(dec_in.sem, dec_in.at(c, 2 + DB + 4))
                tile_work(c, TILES, DT, DEC_LEVELS)
                dve.wait_ge(v_pv.sem, v_pv.chunk_end(c))
                for k in range(KM):
                    lo(c, KM, k, mix[:, k, :])

                def out_work(j, s, pair):
                    product_done(c, pair, s)
                    V.tensor_copy(half2(at(mix, j * 2 + s)), acc(s)).then_inc(drained[s].sem, 1)
                units(c, OUT, out_work)
                newton(c, 1)
                add_branch(c, 0, 0, W_POST, lambda k: lo_weighted(c, 2 * KM, k, W_FFN))
                newton(c, 2)
                dve.sem_inc(passed["dve"])
                for f in range(2):
                    def gu_work(j, s, pair):
                        product_done(c, pair, s)
                        if f == 0 and s == 0:
                            dve.wait_ge(kv_out.sem, kv_out.at(c, 1))
                        normed(half2(tmp[:, s, :]), acc(s)).then_inc(drained[s].sem, 1)
                        if s == 1:
                            dve.wait_ge(drained[1].sem, c * PAIRS + pair + 2)
                            dve.wait_ge(sig.sem, c * sig.chunk + j + (f * KF + 1))
                            V.tensor_tensor(tmp[:, 1, :], tmp[:, 0, :], tmp[:, 1, :], ALU.mult).then_inc(prod.sem, 1)
                            dve.wait_ge(gu_hi.sem, c * gu_hi.chunk + j + (f * KF + 1))
                            V.tensor_tensor(at(gl, j), tmp[:, 1, :], at(gh, j).bitcast(f32), ALU.subtract
                                            ).then_inc(gu_lo.sem, 1)
                    units(c, GU + 2 * f, gu_work)
                    if f == 0:
                        dve.wait_ge(p_hi.sem, p_hi.at(c, 1))
                        V.tensor_tensor(pl[:, :, :], p_raw[:, :, :], ph[:, :, :].bitcast(f32), ALU.subtract
                                        ).then_inc(p_lo.sem, 1)

                    def down_work(j, s, pair):
                        product_done(c, pair, s)
                        dst = half2(at(mix, j * 2 + s))
                        if f == 0:
                            V.tensor_copy(dst, acc(s)).then_inc(drained[s].sem, 1)
                        else:
                            V.tensor_tensor(dst, dst, acc(s), ALU.add).then_inc(drained[s].sem, 1)
                    units(c, GU + 1 + 2 * f, down_work)
                newton(c, 3)
                add_branch(c, KM, KM, W_PFFN, lambda k: lo(c, 3 * KM, k, x[:, k, :]))

                def ple_work(j, s, pair):
                    dve.wait_ge(sigm.sem, c * KM + j * 2 + (s + 1))
                    V.tensor_tensor(half2(tmp[:, s, :]), half2(tmp[:, s, :]), ps[:, 4 + 2 * s:6 + 2 * s, 0:H], ALU.mult
                                    ).then_inc(drained[s].sem, 1)
                    dve.wait_ge(drained[s].sem, c * PAIRS + pair + 2)
                    dst = at(x, j * 2 + s)
                    V.tensor_tensor(dst, dst, tmp[:, s, :], ALU.add).then_inc(res.sem, 1)
                units(c, PLE, ple_work)

        @block.tensor
        def _(pe):
            MM = nc.tensor.matmul

            def three_pass(out, k, K, whi, wlo, xhi, xlo, first):
                last = None
                for n_pass, (w_, x_) in enumerate(((whi, xhi), (whi, xlo), (wlo, xhi))):
                    for n in range(2):
                        last = MM(out[:, n, :], w_, x_[:, n * H:(n + 1) * H], start=(first and n_pass == 0),
                                  stop=(k == K - 1 and n_pass == 2))
                return last

            def unit(c, s, pair, K, hi, lo_, ready=None):
                pe.wait_ge(w_lo.sem, c * UNITS + pair * 2 + (s + 3))
                pe.wait_ge(drained[s].sem, c * PAIRS + pair + 1)
                for k in range(K):
                    if ready:
                        ready(k)
                    last = three_pass(acc(s), k, K, wh[s][:, k * P:(k + 1) * P], wl[s][:, k * P:(k + 1) * P],
                                      hi[:, k, :], lo_[:, k, :], k == 0)
                return last

            def units(c, i, hi, lo_, K, extra=None, ready=None, after_first=None):
                _, n, _ = PHASES[i]

                def pair(j, ready):
                    for s in range(2):
                        last = unit(c, s, j + PAIR0[i], K, hi, lo_, ready if s == 0 else None)
                        if extra:
                            last = extra(s)
                        last.then_inc(w_used.sem, 1)
                        if ready and s == 0 and after_first:
                            after_first()
                if ready:
                    pair(0, ready)
                with pe.Fori(1 if ready else 0, n // 2) as j:
                    pair(j, None)

            def split(c, i):
                def ready(k):
                    pe.wait_ge(a_lo.sem, a_lo.at(c, i * KM + k + 1))
                return ready

            def mean(c, i):
                for last_tile in (False, True):
                    if not last_tile:
                        pe.wait_ge(ss.sem, ss.at(c, (i + 1) * (KM - 2)))
                    elif i == 0:
                        pe.wait_ge(sq_x.sem, sq_x.at(c, KM))
                    else:
                        pe.wait_ge(sq.sem, sq.at(c, i * KM))
                    for n in range(2):
                        src = sqt[:, 1, n * H:(n + 1) * H] if last_tile else ssq[:, n * H:(n + 1) * H]
                        last = MM(ps[:, 6 + n, 0:H], mean_w[:], src, start=not last_tile, stop=last_tile)
                last.then_inc(ss_mean.sem, 1)

            def tile_work(c, t, w, levels):
                sample = isinstance(t, int)
                rt = w // 2
                spans = range(DB) if sample else range(1)
                pe.wait_ge(v_q.sem, v_q.at(c, t, 4))
                for q in range(2):
                    last = MM(ps[0:w, q, 0:4 * w].rearrange("p (h i) -> p h i", h=4), zt[:, ZK + q, 0:w],
                              qm[:, q, :, 0:w], start=True, stop=True)
                last.then_inc(t_diag.sem, 1)
                pe.wait_ge(a_stage.sem, a_stage.at(c, t, 5))
                for j in range(4):
                    nc.tensor.transpose(ps[0:w, 2, j * P:(j + 1) * P], zt[:, ZV + j, 0:w], ident[:])
                nc.tensor.transpose(ps[0:w, 3, 0:P], zt[:, ZSV, 0:w], ident[:]).then_inc(t_vt.sem, 1)
                if sample:
                    for b in range(DB):
                        for g in range(2):
                            i = 32 * (2 * b + g)
                            last = MM(ps[i:i + 32, 4, 0:P + DT],
                                      zt[:, ZSQ, 32 * b:32 * b + 32], kdec[:, b, g, :],
                                      start=True, stop=True)
                else:
                    for m in range(4):
                        last = MM(ps[:, 4 + m, :], zt[:, ZSQ + m, :], kwin[:, :, :, :].rearrange("p h g k -> p (h g k)"),
                                  start=True, stop=True)
                last.then_inc(t_sc.sem, 1)
                pe.wait_ge(v_qe.sem, v_qe.at(c, t, v_qe.dec if sample else 2))
                pe.wait_ge(a_vt.sem, a_vt.at(c, t, 2))
                for b in spans:
                    for q in range(2):
                        last = nc.tensor.transpose(ps[0:w, 3, (2 * b + q) * P:(2 * b + q + 1) * P],
                                                   ke2[:, b, q, :] if sample else ke[:, q, :], ident[:])
                last.then_inc(t_kt.sem, 1)
                pe.wait_ge(a_kt.sem, a_kt.at(c, t, 1))
                for b in spans:
                    for q in range(2):
                        last = MM(ps[:, 2 + b, q * 4 * DV:(q + 1) * 4 * DV], ktok[0:w, b, q * P:(q + 1) * P],
                                  padded(vpad[0:w, q * 4 * P:(q + 1) * 4 * P]), start=True, stop=True)
                    last.then_inc(t_u.sem, 1)
                for l in range(levels):
                    pe.wait_ge(v_lev.sem, v_lev.at(c, t, 3 * l + 3))
                    if l < 2:
                        pe.wait_ge(v_diag.sem, v_diag.at(c, t, 2))
                    else:
                        pe.wait_ge(v_put.sem, v_put.at(c, t, l - 1))
                    for q in range(2):
                        last = MM(ps[0:w, l % 2, q * 4 * rt:(q + 1) * 4 * rt].rearrange("p (h i) -> p h i", h=4),
                                  kd[l % 2][:, q, 0:w], qd[l % 2][:, q, :, 0:rt], start=True, stop=True)
                    last.then_inc(t_lev.sem, 1)
                pe.wait_ge(v_put.sem, v_put.at(c, t, levels))
                pe.wait_ge(v_u.sem, v_u.at(c, t, len(spans)))
                for j in range(4):
                    out = ps[:, 3, j * w:(j + 1) * w]
                    q = j // 2
                    for hh in range(2):
                        h = 2 * j + hh
                        MM(out, vpad[0:w, h * P:(h + 1) * P], A_t[0:w, h, 0:w], start=(hh == 0), stop=False)
                    r = slice((j % 2) * P, (j % 2) * P + P)
                    if sample:
                        for b in range(DB):
                            last = MM(out[:, DEC_SEQ * b:DEC_SEQ * b + DEC_SEQ], Sd[:, b, q, r],
                                      qe[:, q, DEC_SEQ * b:DEC_SEQ * b + DEC_SEQ], start=False, stop=(b == DB - 1))
                    else:
                        last = MM(out, S[:, q, r], qe[:, q, :], start=False, stop=True)
                last.then_inc(t_o.sem, 1)
                pe.wait_ge(a_sq.sem, a_sq.at(c, t, 1))
                MM(ps[:, 2, 0:4 * w], head_w[:], o_sq[:, 0:4 * w], start=True, stop=True).then_inc(t_hn.sem, 1)
                if sample:
                    pe.wait_ge(v_den.sem, v_den.at(c, t, 3))
                    nc.tensor.transpose(ps[:, 4, 0:P], scf[:, 0:P], ident[:])
                    nc.tensor.transpose(ps[0:DT, 4, P:2 * P], scf[:, P:P + DT], ident[:]).then_inc(t_pt.sem, 1)
                    pe.wait_ge(a_pt.sem, a_pt.at(c, t, 2))
                    for b in range(DB):
                        out = ps[:, 0, 32 * b:32 * b + 32]
                        for g in range(2):
                            i = 32 * (2 * b + g)
                            MM(out, vdec[:, b, g * P:(g + 1) * P], ptf[:, i:i + 32], start=(g == 0), stop=False)
                            last = MM(out, vsp[0:DT, 1, g * P:(g + 1) * P], ptf[0:DT, P + i:P + i + 32],
                                      start=False, stop=(g == 1))
                else:
                    pe.wait_ge(v_den.sem, v_den.at(c, t, 4))
                    for hf in range(2):
                        for g in range(2):
                            for m in range(4):
                                last = nc.tensor.transpose(ps[:, 4 + 2 * hf + g, m * P:(m + 1) * P],
                                                           sc[:, m, hf, g, :], ident[:])
                    last.then_inc(t_pt.sem, 1)
                    pe.wait_ge(a_pt.sem, a_pt.at(c, t, 4))
                    for i in range(4):
                        hf, g = divmod(i, 2)
                        last = MM(ps[:, 0, :], vsp[:, hf, g * P:(g + 1) * P], pt[:, hf, g, :],
                                  start=(i == 0), stop=(i == 3))
                last.then_inc(t_pv.sem, 1)

            pe.wait_ge(consts_set, N_SET)
            with pe.Fori(0, CHUNKS) as c:
                for k in range(KM):
                    split(c, 0)(k)
                    last = three_pass(ps[0:LOW_RANK, 4:6, 0:H], k, KM, lrh[:, k, :], lrl[:, k, :],
                                      ah[:, k, :], al[:, k, :], k == 0)
                last.then_inc(lr_sum.sem, 1)
                mean(c, 0)
                units(c, OG, ah, al, KM)
                pe.wait_ge(lr_got.sem, lr_got.at(c, 1))
                for q in range(2):
                    for n in range(2):
                        last = MM(ps[:, 4 + 2 * q + n, 0:H], gate_up[:, q * P:(q + 1) * P], lr_t[:, n * H:(n + 1) * H],
                                  start=True, stop=True)
                last.then_inc(gate_sum.sem, 1)
                units(c, ZZ, ah, al, KM)
                with pe.Fori(0, TILES) as t:
                    tile_work(c, t, P, LEVELS)
                tile_work(c, TILES, DT, DEC_LEVELS)
                units(c, OUT, ah, al, KM, ready=split(c, 1))
                mean(c, 1)
                for f in range(2):
                    if f == 0:
                        units(c, GU, ah, al, KM, ready=split(c, 2), after_first=lambda: mean(c, 2))
                    else:
                        units(c, GU + 2, ah, al, KM)

                    def ready(k):
                        pe.wait_ge(gu_lo.sem, gu_lo.at(c, f * KF + k + 1))
                    units(c, GU + 1 + 2 * f, gh, gl, KF, ready=ready)
                mean(c, 3)
                pe.wait_ge(p_lo.sem, p_lo.at(c, 1))
                pe.sem_inc(passed["pe"])

                def projection(s):
                    for k in range(KP):
                        col = slice((KM + k) * P, (KM + k + 1) * P)
                        last = three_pass(ps[:, 4 + 2 * s:6 + 2 * s, 0:H], k, KP, wh[s][:, col], wl[s][:, col],
                                          ph[:, k, :], pl[:, k, :], k == 0)
                    return last
                units(c, PLE, ah, al, KM, projection, ready=split(c, 3))


def constants():
    part = np.arange(P)
    head_mask = (part[:, None] // DK == np.arange(4)[None]).astype(np.float32)
    lev = np.zeros((P, LEVELS, P // 2), np.uint32)
    r = np.arange(P // 2)
    for l in range(LEVELS):
        s = 1 << l
        block = r // s
        lev[:, l, :] = (part[:, None] // (2 * s) == block[None]) & (part[:, None] % (2 * s) < s)
    keep = np.ones((2, T), np.float32)
    keep[:, 0:PT:P] = 0
    keep[:, PT::DEC_SEQ] = 0
    d = part[:, None, None] - (np.arange(P)[None, None] - P * (1 - np.arange(2))[None, :, None])
    dist = np.where((d >= 0) & (d < WINDOW), d, FAR).astype(np.float32)
    first = dist.copy()
    first[:, 0, :] = FAR
    bias_dec = np.full((DB, 2, 4, DEC_SEQ, P + DT), NEG, np.float32)
    for b in range(DB):
        for g in range(2):
            for m in range(4):
                for i in range(DEC_SEQ):
                    d = P + i - np.arange(P)
                    bias_dec[b, g, m, i, :P] = np.where(d < WINDOW, -SLOPES[4 * g + m] * d, NEG)
                    for j in range(i + 1):
                        bias_dec[b, g, m, i, P + DEC_SEQ * b + j] = -SLOPES[4 * g + m] * (i - j)
    return {
        "mean_w": np.full((P, P), 1 / D_MODEL, np.float32),
        "head_w": (part[:, None] // DV == part[None] // DV).astype(np.float32) / DV,
        "ident": np.eye(P, dtype=np.float32),
        "head_mask": head_mask,
        "block_mask": np.repeat(head_mask, DV, axis=1),
        "lev_mask": lev,
        "keep": np.broadcast_to(keep.reshape(1, -1), (P, 2 * T)).copy(),
        "dist": first,
        "dist_prev": dist[:, 0, :].copy(),
        "bias_dec": bias_dec.reshape(P, P + DT),
    }


def kernel(**inputs):
    import concourse.bacc as bacc
    from concourse.bass_utils import run_bass_kernel_spmd

    a = {k: np.asarray(v) for k, v in inputs.items()}

    def by_chunk(prompt, sample):
        F = prompt.shape[-1]
        both = np.concatenate([prompt.reshape(CHUNKS, PT, F), sample.reshape(CHUNKS, DT, F)], 1)
        return np.ascontiguousarray(both.reshape(CHUNKS, T, F // P, P).transpose(3, 0, 2, 1)).reshape(P, -1)

    def as_units(w):
        K, M = w.shape
        return np.ascontiguousarray(w.reshape(K // P, P, M // P, P).transpose(2, 1, 0, 3)).reshape(M // P, P, K)

    def per_tile(v):
        return v.reshape(-1, P).T

    w_in = a["w_in"][0]
    cut = np.cumsum([256, 256, 512, 512, LOW_RANK, 512, 128, 128])
    q_g, k_g, v_g, og, lr, q_s, k_s, v_s = np.split(w_in, cut[:-1], axis=1)
    q_s = q_s.reshape(D_MODEL, 2, 4, SWA_DIM).transpose(0, 2, 1, 3).reshape(D_MODEL, 512)
    w_out = a["w_out"][0]
    swa_rows = w_out[512:].reshape(2, 4, SWA_DIM, D_MODEL).transpose(1, 0, 2, 3).reshape(512, D_MODEL)
    gate, up = as_units(a["w_gate"][0]), as_units(a["w_up"][0])
    down = a["w_down"][0]
    state = a["state_gla"][0].reshape(CHUNKS, DB, 2, 4, DK, DV)
    sinks = a["swa_sinks"][0].reshape(2, 4)
    cache_k = a["cache_swa_k"][0].reshape(DEC_BATCH, P, P)
    cache_v = a["cache_swa_v"][0].reshape(DEC_BATCH, P, P)
    arrays = {
        "x": by_chunk(a["x_prompt"][0], a["x_sample"]),
        "p": by_chunk(a["p_prompt"][0, 0], a["p_sample"][0]),
        "w_z": as_units(np.concatenate([q_g, k_g, v_g, q_s, k_s, v_s, og], 1)),
        "w_lr": np.ascontiguousarray(lr.reshape(KM, P, LOW_RANK).transpose(1, 0, 2)),
        "w_out": as_units(np.concatenate([w_out[:512], swa_rows], 0)),
        "w_gu": np.stack([gate, up], 1).reshape(4 * KF, P, D_MODEL),
        "w_dn": np.concatenate([as_units(down[:KF * P]), as_units(down[KF * P:])], 0),
        "w_ple": np.concatenate([as_units(a["w_ple_gate"][0]), as_units(a["w_ple_proj"][0])], 2),
        "gate_up": a["gla_gate_up"][0],
        "cols": np.concatenate([per_tile(a["w_pre_mix"][0]), per_tile(a["w_post_mix"][0]), per_tile(a["w_pre_ffn"][0]),
                                per_tile(a["w_post_ffn"][0]), per_tile(a["gla_gate_b"][0]),
                                np.tile(a["gla_norm_w"][0], 2)[:, None], np.full((P, 1), EPS, np.float32)], 1),
        "sinks": np.broadcast_to(sinks.T.reshape(1, HEADS), (P, HEADS)),
        "sink_dec": np.broadcast_to(sinks.reshape(1, HEADS, 1), (DB, HEADS, DEC_SEQ)).reshape(P, 1),
        "state": state.transpose(3, 4, 0, 1, 2, 5).reshape(P, CHUNKS * DB * 2 * DV),
        "cache_k": cache_k,
        "cache_v": cache_v,
        "cache_kT": cache_k.transpose(2, 0, 1).reshape(P, DEC_BATCH * P),
        "cache_vr": cache_v.transpose(1, 0, 2).reshape(P, DEC_BATCH * P),
        **constants(),
    }
    outputs = {"y": (P, CHUNKS * KM * T), "kv": (P, CHUNKS * 2 * KVT), "state": (P, CHUNKS * DB * 2 * DV),
               "state_p": (P, 2, DV), "k_keep": (DEC_BATCH, P - DEC_SEQ, P), "v_keep": (DEC_BATCH, P - DEC_SEQ, P)}

    nc = bacc.Bacc("TRN2", target_bir_lowering=False, num_devices=1)
    arrays = {f"in_{k}": np.ascontiguousarray(v) for k, v in arrays.items()}
    ins = {k[3:]: nc.dram_tensor(k, v.shape, mybir.dt.from_np(v.dtype), kind="ExternalInput").ap()
           for k, v in arrays.items()}
    outs = {k: nc.dram_tensor(f"out_{k}", s, f32, kind="ExternalOutput").ap() for k, s in outputs.items()}
    build(nc, ins, outs)
    r = run_bass_kernel_spmd(nc, [arrays], core_ids=[0]).results[0]
    o = {k: r[f"out_{k}"] for k in outputs}

    y = o["y"].reshape(P, CHUNKS, KM, T).transpose(1, 3, 2, 0).reshape(CHUNKS, T, D_MODEL)
    kv = o["kv"].reshape(P, CHUNKS, 2, KVT).transpose(2, 1, 3, 0)
    prompt_kv = kv[:, CHUNKS - 1, :P].reshape(2, 1, 1, P, KV_HEADS, SWA_DIM)
    new = kv[:, :, P:].reshape(2, DEC_BATCH, DEC_SEQ, P)
    sample_kv = [np.concatenate([o[f"{n}_keep"], new[i]], 1).reshape(1, DEC_BATCH, P, KV_HEADS, SWA_DIM)
                 for i, n in enumerate("kv")]
    state_s = o["state"].reshape(4, DK, CHUNKS, DB, 2, DV).transpose(2, 3, 4, 0, 1, 5)
    state_p = o["state_p"].reshape(4, DK, 2, DV).transpose(2, 0, 1, 3)
    return (y[:, :PT].reshape(1, SEQ, D_MODEL), y[:, PT:].reshape(DEC_BATCH, DEC_SEQ, D_MODEL),
            state_p.reshape(1, 1, HEADS, DK, DV), prompt_kv[0], prompt_kv[1],
            state_s.reshape(1, DEC_BATCH, HEADS, DK, DV), sample_kv[0], sample_kv[1])
```

```python
from contextlib import ExitStack

import numpy as np
import concourse.bass as bass
from concourse import mybir

f32 = mybir.dt.float32
f32r = mybir.dt.float32r
u32 = mybir.dt.uint32
ACT = mybir.ActivationFunctionType
ALU = mybir.AluOpType
AX = mybir.AxisListType

P = 128
D_MODEL, SEQ, DEC_BATCH, DEC_SEQ, PLE_DIM, D_FF = 1024, 2048, 8, 8, 256, 2816
HEADS, DK, DV, LOW_RANK, KV_HEADS, SWA_DIM, WINDOW = 8, 32, 64, 16, 2, 64, 128
GATE_NORM, EPS = 16.0, 1e-6
CHUNKS = 4
PT = SEQ // CHUNKS
TILES = PT // P
DB = DEC_BATCH // CHUNKS
DT = DB * DEC_SEQ
T = PT + DT
H = T // 2
KM = D_MODEL // P
KF = D_FF // P // 2
KP = PLE_DIM // P
KVT = P + DT
SCALE_G = DK ** -0.5
SCALE_S = SWA_DIM ** -0.5
FAR = 1e32
NEG = -1e30

ZQ, ZK, ZV, ZSQ, ZSK, ZSV, ZO, ZN = 0, 2, 4, 8, 12, 13, 14, 18
LEVELS = 7
DEC_LEVELS = 3
SLOPES = [2.0 ** (-8.0 * (h + 1) / HEADS) for h in range(HEADS)]

PHASES = [("og", ZN - ZO, KM), ("z", ZO, KM), ("out", KM, KM), ("gu0", 2 * KF, KM), ("dn0", KM, KF),
          ("gu1", 2 * KF, KM), ("dn1", KM, KF),
          ("proj", 2, KM), ("ple", KM, KM)]
OG, ZZ, OUT, GU, PROJ, PLE = 0, 1, 2, 3, 7, 8
UNITS = sum(n for _, n, _ in PHASES)
PAIRS = UNITS // 2
PAIR0 = [sum(n for _, n, _ in PHASES[:i]) // 2 for i in range(len(PHASES) + 1)]
WCOLS = max(k for _, _, k in PHASES) * P

W_PRE, W_POST, W_FFN, W_PFFN, C_GB, C_HN, C_EPS, C_GN, N_COLS = \
    0, KM, 2 * KM, 3 * KM, 4 * KM, 4 * KM + 2, 4 * KM + 3, 4 * KM + 4, 4 * KM + 5


class Signal:

    def __init__(self, sem, chunk, first=0, unit=1):
        self.sem, self.chunk, self.first, self.unit = sem, chunk, first, unit

    def at(self, c, k):
        return c * (self.chunk * self.unit) + (k + self.first) * self.unit


class TileSignal:

    def __init__(self, sem, tile, dec, first=0):
        self.sem, self.tile, self.dec, self.first = sem, tile, dec, first

    def at(self, c, t, k):
        return c * (TILES * self.tile + self.dec) + t * self.tile + (k + self.first)

    def chunk_end(self, c):
        return self.at(c, TILES, self.dec)


def build(nc, A, O):
    ctx = ExitStack()
    with ctx:
        def sb(name, shape, dt=f32):
            return ctx.enter_context(nc.sbuf_tensor(name, shape, dt))

        def sem(name):
            return ctx.enter_context(nc.semaphore(name))

        x = sb("x", [P, KM, T])
        mix = sb("mix", [P, KM, T])
        w_raw = [sb(f"w_raw{s}", [P, WCOLS]) for s in range(2)]
        wh = [sb(f"wh{s}", [P, WCOLS], f32r) for s in range(2)]
        wl = [sb(f"wl{s}", [P, WCOLS], f32r) for s in range(2)]
        lr_raw = sb("lr_raw", [P, KM, LOW_RANK])
        lrh = sb("lrh", [P, KM, LOW_RANK], f32r)
        lrl = sb("lrl", [P, KM, LOW_RANK], f32r)
        gate_up = sb("gate_up", [LOW_RANK, 2 * P])
        cols = sb("cols", [P, N_COLS])
        mean_w = sb("mean_w", [P, P])
        head_w = sb("head_w", [P, P])
        ident = sb("ident", [P, P])
        head_mask = sb("head_mask", [P, 4])
        block_mask = sb("block_mask", [P, 4 * DV])
        lev_mask = sb("lev_mask", [P, LEVELS, P // 2], u32)
        keep = sb("keep", [P, 2 * T])
        dist = sb("dist", [P, 2, P])
        dist_prev = sb("dist_prev", [P, P])
        bias_dec = sb("bias_dec", [P, P + DT])
        sinks = sb("sinks", [P, HEADS])
        sink_dec = sb("sink_dec", [P, 1])
        rs = sb("rs", [P, T])
        tmp_a = sb("tmp_a", [P, T])
        tmp = sb("tmp", [P, 2, T])
        ssq = sb("ssq", [P, T])
        sqt = sb("sqt", [P, 2, T])
        S = sb("S", [P, 2, 4 * DV])
        Sd = sb("Sd", [P, DB, 2, 4 * DV])
        kwin = sb("kwin", [P, 2, 2, P])
        kdec = sb("kdec", [P, DB, 2, P + DT])
        vsp = sb("vsp", [P, 2, 4 * DV])
        vdec = sb("vdec", [P, DB, 4 * DV])
        vpad = sb("vpad", [P, HEADS * P])
        ke2 = sb("ke2", [P, DB, 2, DT])
        st = sb("st", [P, 9, 16])
        st_dec = sb("st_dec", [P, 8])

        class Region:
            def __init__(self, offset, size):
                self.offset, self.size, self.used = offset, size, 0

            def put(self, name, shape, dt=f32, at=None):
                n = int(np.prod(shape[1:])) * 4
                o = self.used if at is None else at
                assert o + n <= self.size, (name, o + n, self.size)
                self.used = max(self.used, o + n)
                return nc.alloc_sbuf_tensor_at(name, shape, dt, offset=self.offset + o)

        free = nc.sbuf_base
        sz_a, sz_p, sz_f = 2 * KM * T * 4, 3 * KP * T * 4, 2 * KF * T * 4
        arena = sb("arena", [P, (sz_a + sz_p + sz_f) // 4])
        ra = Region(free, sz_a)
        ah = ra.put("ah", [P, KM, T], f32r)
        al = ra.put("al", [P, KM, T], f32r)
        ra.used = 0
        qm = ra.put("qm", [P, 2, 4, P])
        e_lev = [ra.put(f"e_lev{i}", [P, 2, P]) for i in range(2)]
        kd = [ra.put(f"kd{i}", [P, 2, P]) for i in range(2)]
        qd = [ra.put(f"qd{i}", [P, 2, 4, P // 2]) for i in range(2)]
        A_t = ra.put("A_t", [P, HEADS, P])
        eg = ra.put("eg", [P, 2, P])
        ke = ra.put("ke", [P, 2, P])
        qe = ra.put("qe", [P, 2, P])
        gt = ra.put("gt", [P, 2, P])
        ktok = ra.put("ktok", [P, DB, 2 * P])
        sc = ra.put("sc", [P, 4, 2, 2, P])
        pt3 = ra.put("pt3", [P, 4 * P])
        gend = ra.put("gend", [P, 2, DB])
        pt = [ssq[:, 0:4 * P], sqt[:, 0, 0:4 * P], sqt[:, 1, 0:4 * P], pt3[:]]
        pt_dec = sqt[:, 0, 0:2 * P]
        o_sq = tmp_a
        od = rs[:, 0:4 * P]
        nrm = [tmp[:, i, :] for i in range(2)]
        scf = sc[:, :, :, :, :].rearrange("p m h g k -> p (m h g k)")
        rp = Region(free + sz_a, sz_p)
        p_raw = rp.put("p_raw", [P, KP, T])
        ph = rp.put("ph", [P, KP, T], f32r)
        pl = rp.put("pl", [P, KP, T], f32r)
        rp.used = 0
        zt = rp.put("zt", [P, ZO, P])
        qk = rp.put("qk", [P, 2, P])
        um = rp.put("um", [P, DB, 2, 4 * DV])
        rf = Region(free + sz_a + sz_p, sz_f)
        gh = rf.put("gh", [P, KF, T], f32r)
        gl = rf.put("gl", [P, KF, T], f32r)
        rf.used = 0
        z = rf.put("z", [P, ZN, T])
        G = rf.put("G", [P, 2, T])
        lr_t = rf.put("lr_t", [LOW_RANK, T])
        proj = rf.put("proj", [P, KM, T], at=0)

        ps = ctx.enter_context(nc.psum_tensor("ps", [P, 8, 512], f32))

        def acc(s):
            return ps[:, 2 * s:2 * s + 2, 0:H]

        PROJ_ACC = [4, 0, 2, 4, 0, 2, 4, 4]
        PROJ_PREV = {3: 0, 4: 1, 5: 2, 6: 3, 7: 6}

        def half2(ap):
            return ap.rearrange("p (a b) -> p a b", a=2)

        def at(tensor, i):
            return tensor[:, i, :] if isinstance(i, int) else \
                tensor[:, bass.ds(i, 1), :].rearrange("p u n -> p (u n)")

        first_in = sem("first_in")
        consts_in = sem("consts_in")
        consts_set = sem("consts_set")
        w_in = [sem(f"w_in{s}") for s in range(2)]
        w_hi = Signal(sem("w_hi"), UNITS)
        w_lo = Signal(sem("w_lo"), UNITS, 2)
        w_used = Signal(sem("w_used"), UNITS, 2)
        drained = [Signal(sem(f"drained{s}"), PAIRS, 1) for s in range(2)]
        x_in = [Signal(sem(f"x_in{s}"), KM // 2, unit=16) for s in range(2)]
        y_out = [Signal(sem(f"y_out{s}"), KM // 2, unit=16) for s in range(2)]
        p_in = Signal(sem("p_in"), 1, unit=16)
        p_hi = Signal(sem("p_hi"), 1)
        p_lo = Signal(sem("p_lo"), 1)
        sq_x = Signal(sem("sq_x"), KM)
        sq = Signal(sem("sq"), 3 * KM)
        ss = Signal(sem("ss"), 4 * (KM - 2))
        ss_mean = Signal(sem("ss_mean"), 4)
        rs_guess = Signal(sem("rs_guess"), 8)
        rs_newton = Signal(sem("rs_newton"), 12)
        a_hi = Signal(sem("a_hi"), 4 * KM)
        a_lo = Signal(sem("a_lo"), 4 * KM)
        branch = Signal(sem("branch"), 2 * KM)
        res = Signal(sem("res"), 3 * KM)
        gu_hi = Signal(sem("gu_hi"), 2 * KF)
        gu_lo = Signal(sem("gu_lo"), 2 * KF, 1)
        sig = Signal(sem("sig"), 2 * KF)
        prod = Signal(sem("prod"), 2 * KF)
        gated = Signal(sem("gated"), KM)
        t_proj = Signal(sem("t_proj"), KM - 2)
        proj_out = Signal(sem("proj_out"), KM)
        lr_sum = Signal(sem("lr_sum"), 1)
        lr_got = Signal(sem("lr_got"), 1)
        gate_sum = Signal(sem("gate_sum"), 1)
        gate_act = Signal(sem("gate_act"), 2)
        gate_vec = Signal(sem("gate_vec"), 5)
        og_silu = Signal(sem("og_silu"), 1)
        L, LD = LEVELS, DEC_LEVELS
        v_q = TileSignal(sem("v_q"), 4, 4)
        p_gt = TileSignal(sem("p_gt"), 1, 1)
        a_stage = TileSignal(sem("a_stage"), 5, 5)
        t_diag = TileSignal(sem("t_diag"), 1, 1)
        p_qk = TileSignal(sem("p_qk"), 1, 1)
        v_diag = TileSignal(sem("v_diag"), 1, 1)
        v_zero = Signal(sem("v_zero"), 2)
        v_o = TileSignal(sem("v_o"), 1, 1)
        p_gate = TileSignal(sem("p_gate"), 1, 1)
        t_vt = TileSignal(sem("t_vt"), 1, 1)
        a_vt = TileSignal(sem("a_vt"), 2, 2)
        t_sc = TileSignal(sem("t_sc"), 4, 1)
        v_sc = TileSignal(sem("v_sc"), 9, 1)
        p_diff = TileSignal(sem("p_diff"), 2 * L, 2 * LD)
        a_lev = TileSignal(sem("a_lev"), L, LD)
        v_lev = TileSignal(sem("v_lev"), 3 * L, 3 * LD)
        t_lev = TileSignal(sem("t_lev"), L, LD)
        v_put = TileSignal(sem("v_put"), L, LD)
        p_gend = TileSignal(sem("p_gend"), 1, DB)
        a_eg = TileSignal(sem("a_eg"), 3, 1 + 2 * DB)
        p_qe = TileSignal(sem("p_qe"), 2, 1 + DB)
        t_kt = TileSignal(sem("t_kt"), 1, 1)
        a_kt = TileSignal(sem("a_kt"), 1, 1)
        t_u = TileSignal(sem("t_u"), 1, DB)
        v_u = TileSignal(sem("v_u"), 1, DB)
        p_s = TileSignal(sem("p_s"), 2, 2 * DB, first=1)
        t_o = TileSignal(sem("t_o"), 1, 1)
        a_sq = TileSignal(sem("a_sq"), 1, 1)
        t_hn = TileSignal(sem("t_hn"), 1, 1)
        a_rs = TileSignal(sem("a_rs"), 2, 2)
        v_rs = TileSignal(sem("v_rs"), 4, 4, first=3)
        v_max = TileSignal(sem("v_max"), 5, 4)
        a_exp = TileSignal(sem("a_exp"), HEADS + 1, 2)
        v_den = TileSignal(sem("v_den"), 2, 2)
        a_norm = TileSignal(sem("a_norm"), HEADS, 1)
        t_pt = TileSignal(sem("t_pt"), 1, 1)
        a_pt = TileSignal(sem("a_pt"), 4, 2)
        t_pv = TileSignal(sem("t_pv"), 1, 1)
        a_pv = TileSignal(sem("a_pv"), 1, DB, first=1)
        p_kshift = TileSignal(sem("p_kshift"), 1, 0)
        p_vshift = TileSignal(sem("p_vshift"), 1, 0, first=1)
        dec_in = Signal(sem("dec_in"), 2 + DB + 4, unit=16)
        kv_out = Signal(sem("kv_out"), 1, unit=16)
        s_out = Signal(sem("s_out"), 4, unit=16)
        last_out = sem("last_out")
        passed = {e: sem(f"passed_{e}") for e in ("pool", "dve", "pe")}

        first_loads = [(lr_raw[:, :, :], A["w_lr"]), (cols[:], A["cols"]), (mean_w[:], A["mean_w"]),
                       (gate_up[:], A["gate_up"])]
        loads = [(head_w[:], A["head_w"]), (ident[:], A["ident"]),
                 (head_mask[:], A["head_mask"]), (block_mask[:], A["block_mask"]),
                 (lev_mask[:, :, :], A["lev_mask"]), (keep[:], A["keep"]), (dist[:, :, :], A["dist"]),
                 (dist_prev[:], A["dist_prev"]), (bias_dec[:], A["bias_dec"]), (sinks[:], A["sinks"]),
                 (sink_dec[:], A["sink_dec"])]
        zeroed = [S, Sd, kwin, kdec, vsp, vdec, vpad, ke2]
        N_SET = len(zeroed) + 5

        block = ctx.enter_context(nc.Block())

        W = {k: A[k].rearrange("u p n -> p u n") for k in ("w_z", "w_out", "w_gu", "w_dn", "w_proj", "w_ple")}
        SRC = {"og": ("w_z", ZO), "z": ("w_z", 0), "out": ("w_out", 0), "gu0": ("w_gu", 0), "gu1": ("w_gu", 2 * KF),
               "dn0": ("w_dn", 0), "dn1": ("w_dn", KM), "proj": ("w_proj", 0), "ple": ("w_ple", 0)}

        def following(i):
            return PHASES[(i + 1) % len(PHASES)]

        def columns(tensor, lo, hi, t, w):
            if isinstance(t, int):
                return tensor[:, lo:hi, t * P:t * P + w]
            return tensor[:, lo:hi, bass.ds(t * P, w)]

        def tokens(t):
            return slice(t * P, t * P + P) if isinstance(t, int) else bass.ds(t * P, P)

        def tile_loop(engine, edge, main):
            def w(t):
                return DT if isinstance(t, int) and t == TILES else P
            edge(0, P, None, None)
            with engine.Fori(0, TILES - 1) as t:
                main(t, P)
                edge(t + 1, P, t, P)
            for t in (TILES - 1, TILES):
                main(t, w(t))
                edge(*((t + 1, w(t + 1)) if t < TILES else (None, None)), t, w(t))

        def is_sample(t):
            return isinstance(t, int) and t == TILES

        def sample_spans(sample):
            return [(b, slice(DEC_SEQ * b, DEC_SEQ * b + DEC_SEQ)) for b in range(DB)] if sample else [(0, slice(0, P))]

        def split_blocks(ap, l):
            return ap.rearrange("p q (b two s) -> p q b two s", two=2, s=1 << l)

        def padded(ap):
            return ap.rearrange("p (j a d) -> p j a d", a=4, d=DV)[:, :, 0:4:3, :]

        @block.sync
        def _(sp):
            def load_unit(c, name, u, pair, s):
                key, off = SRC[name]
                n = A[key].shape[-1]
                sp.wait_ge(w_lo.sem, c * UNITS + pair * 2 + (s + 1))
                sp.dma_start(w_raw[s][:, 0:n], at(W[key], u + off)).then_inc(w_in[s], 16)

            for dst, src in first_loads:
                sp.dma_start(dst, src).then_inc(first_in, 16)
            for s in range(2):
                sp.dma_start(w_raw[s][:, 0:KM * P], W["w_z"][:, ZO + s, :]).then_inc(w_in[s], 16)
            sp.wait_ge(x_in[1].sem, 16 * (KM // 2))
            for dst, src in loads:
                sp.dma_start(dst, src).then_inc(consts_in, 16)
            with sp.Fori(0, CHUNKS) as c:
                for i, (name, n, _) in enumerate(PHASES):
                    if n > 2:
                        with sp.Fori(0, n // 2 - 1) as j:
                            for s in range(2):
                                load_unit(c, name, j * 2 + (2 + s), j + (PAIR0[i] + 1), s)
                    for s in range(2):
                        load_unit(c, following(i)[0], s, PAIR0[i + 1], s)

        @block.gpsimd
        def _(gp):
            for k in range(KM):
                if k >= 2:
                    gp.wait_ge(x_in[k % 2].sem, 16 * (k // 2))
                gp.dma_start(x[:, k, :], A["x"][:, k * T:(k + 1) * T]).then_inc(x_in[k % 2].sem, 16)
            gp.dma_start(O["k_keep"], A["cache_k"][:, DEC_SEQ:, :]).then_inc(last_out, 16)
            gp.dma_start(O["v_keep"], A["cache_v"][:, DEC_SEQ:, :]).then_inc(last_out, 16)
            gp.wait_ge(consts_set, N_SET)

            def x_square(c, k):
                gp.wait_ge(x_in[k % 2].sem, x_in[k % 2].at(c, k // 2 + 1))
                if k >= 3:
                    gp.wait_ge(ss.sem, ss.at(c, k - 2))
                nc.gpsimd.tensor_tensor(sqt[:, k % 2, :] if k else ssq[:], x[:, k, :], x[:, k, :], ALU.mult
                                        ).then_inc(sq_x.sem, 1)
                if 1 <= k < KM - 1:
                    gp.wait_ge(sq_x.sem, sq_x.at(c, k + 1))
                    if k >= 2:
                        gp.wait_ge(ss.sem, ss.at(c, k - 1))
                    nc.gpsimd.tensor_tensor(ssq[:], ssq[:], sqt[:, k % 2, :], ALU.add).then_inc(ss.sem, 1)

            def add_squares(c, i):
                for k in range(1, KM - 1):
                    gp.wait_ge(sq.sem, sq.at(c, (i - 1) * KM + k + 1))
                    if k >= 2:
                        gp.wait_ge(ss.sem, ss.at(c, i * (KM - 2) + k - 1))
                    nc.gpsimd.tensor_tensor(ssq[:], ssq[:], sqt[:, k % 2, :], ALU.add).then_inc(ss.sem, 1)

            GP = nc.gpsimd

            def diff(c, t, w, l):
                s, e = 1 << l, split_blocks(e_lev[l % 2][:, :, 0:w], l)
                g = split_blocks(gt[:, :, 0:w], l)
                n = w // (2 * s)
                if l >= 2:
                    gp.wait_ge(v_lev.sem, v_lev.at(c, t, 3 * (l - 1)))
                left = g[:, :, :, 0, :]
                mid = g[:, :, :, 0, s - 1:s].broadcast_to([P, 2, n, s])
                GP.tensor_tensor(e[:, :, :, 0, :], mid, left, ALU.subtract).then_inc(p_diff.sem, 1)
                GP.tensor_tensor(e[:, :, :, 1, :], g[:, :, :, 1, :], mid, ALU.subtract).then_inc(p_diff.sem, 1)

            def tile_edge(c, t, w, before, wb):
                if t is not None:
                    if before is not None:
                        gp.wait_ge(a_eg.sem, a_eg.at(c, before, 3))
                        gp.wait_ge(v_lev.sem, v_lev.at(c, before, v_lev.tile))
                        gp.sem_inc(passed["pool"])
                    GP.tensor_copy(gt[:, :, 0:w], columns(G, 0, 2, t, w)).then_inc(p_gt.sem, 1)
                    gp.wait_ge(p_gt.sem, p_gt.at(c, t, 1))
                    diff(c, t, w, 0)
                    diff(c, t, w, 1)
                    for b, r in sample_spans(is_sample(t)):
                        GP.tensor_tensor(gend[:, :, b:b + 1], gt[:, :, r.stop - 1:r.stop],
                                         cols[:, C_GN:C_GN + 1].rearrange("p (a b) -> p a b", a=1)
                                         .broadcast_to([P, 2, 1]), ALU.mult).then_inc(p_gend.sem, 1)
                    gp.wait_ge(v_q.sem, v_q.at(c, t, 2))
                    GP.tensor_tensor(qk[:, :, 0:w], zt[:, ZQ:ZQ + 2, 0:w], zt[:, ZK:ZK + 2, 0:w], ALU.mult
                                     ).then_inc(p_qk.sem, 1)
                if before is not None:
                    sample = is_sample(before)
                    if sample:
                        gp.wait_ge(dec_in.sem, dec_in.at(c, 2 + DB + 4))
                    gp.wait_ge(v_u.sem, v_u.at(c, before, v_u.dec if sample else 1))
                    gp.wait_ge(t_o.sem, t_o.at(c, before, 1))
                    gp.sem_inc(passed["pool"])
                    for n, (b, r) in enumerate(sample_spans(sample)):
                        state = Sd[:, b, :, :] if sample else S[:, :, :]
                        decay = eg[:, :, r.stop - 1:r.stop].broadcast_to([P, 2, 4 * DV])
                        GP.tensor_tensor(state, state, decay, ALU.mult).then_inc(p_s.sem, 1)
                        gp.wait_ge(p_s.sem, p_s.at(c, before, 2 * n + 1))
                        gp.sem_inc(passed["pool"])
                        GP.tensor_tensor(state, state, um[:, b, :, :], ALU.add).then_inc(p_s.sem, 1)
                if t is not None and not is_sample(t):
                    gp.wait_ge(t_sc.sem, t_sc.at(c, t, 4))
                    gp.sem_inc(passed["pool"])
                    GP.tensor_copy(kwin[:, 0, :, :], kwin[:, 1, :, :]).then_inc(p_kshift.sem, 1)
                if t is not None:
                    gp.wait_ge(a_eg.sem, a_eg.at(c, t, a_eg.dec if is_sample(t) else 3))
                    if is_sample(t):
                        for b, r in sample_spans(True):
                            GP.tensor_tensor(ke2[:, b, :, r], zt[:, ZK:ZK + 2, r], ke[:, :, r], ALU.mult
                                             ).then_inc(p_qe.sem, 1)
                    else:
                        GP.tensor_tensor(ke[:, :, :], zt[:, ZK:ZK + 2, :], ke[:, :, :], ALU.mult).then_inc(p_qe.sem, 1)
                    diff(c, t, w, 2)
                if before is not None:
                    if not is_sample(before):
                        gp.wait_ge(t_pv.sem, t_pv.at(c, before, 1))
                        gp.sem_inc(passed["pool"])
                        GP.tensor_copy(vsp[:, 0, :], vsp[:, 1, :]).then_inc(p_vshift.sem, 1)
                    gp.wait_ge(v_rs.sem, v_rs.at(c, before, 4))
                    GP.tensor_tensor(columns(mix, 0, 4, before, wb), nrm[1][:, 0:4 * wb]
                                     .rearrange("p (j i) -> p j i", j=4), columns(z, ZO, ZO + 4, before, wb),
                                     ALU.mult).then_inc(p_gate.sem, 1)

            def tile_main(c, t, w):
                sample = is_sample(t)
                GP.tensor_tensor(qe[:, :, 0:w], zt[:, ZQ:ZQ + 2, 0:w], eg[:, :, 0:w], ALU.mult).then_inc(p_qe.sem, 1)
                for l in range(3, DEC_LEVELS if sample else LEVELS):
                    diff(c, t, w, l)

            def chunk(c, last):
                gp.wait_ge(a_lo.sem, a_lo.at(c, KM))
                for g in range(2):
                    r = slice(DV * g, DV * g + DV)
                    gp.dma_start(kdec[r, :, g, 0:P],
                                 A["cache_kT"][r, bass.ds(c * (DB * P), DB * P)].rearrange("p (b n) -> p b n", b=DB)
                                 ).then_inc(dec_in.sem, 16)
                for b in range(DB):
                    gp.dma_start(padded(vdec[:, b, :]).rearrange("p j a d -> p (j a) d"),
                                 A["cache_vr"][:, bass.ds(c * (DB * P) + b * P, P)].rearrange("p (g d) -> p g d", g=2)
                                 ).then_inc(dec_in.sem, 16)
                for h in range(4):
                    r = slice(DK * h, DK * h + DK)
                    gp.dma_start(Sd[r, :, :, DV * h:DV * h + DV].rearrange("p b q v -> p (b q) v"),
                                 A["state"][r, bass.ds(c * (DB * 2 * DV), DB * 2 * DV)]
                                 .rearrange("p (b v) -> p b v", v=DV)).then_inc(dec_in.sem, 16)
                gp.wait_ge(v_zero.sem, v_zero.at(c, 1))
                gp.sem_inc(passed["pool"])
                tile_loop(gp, lambda *a: tile_edge(c, *a), lambda *a: tile_main(c, *a))
                gp.wait_ge(a_pv.sem, a_pv.chunk_end(c))
                gp.wait_ge(p_gate.sem, p_gate.chunk_end(c))
                gp.wait_ge(p_s.sem, p_s.chunk_end(c))
                gp.dma_start(p_raw[:, :, :], A["p"][:, bass.ds(c * (KP * T), KP * T)]
                             .rearrange("p (k t) -> p k t", k=KP)).then_inc(p_in.sem, 16)
                gp.dma_start(O["kv"][:, bass.ds(c * (2 * KVT), 2 * KVT)].rearrange("p (a t) -> p a t", a=2),
                             z[:, ZSK:ZSK + 2, T - KVT:T]).then_inc(kv_out.sem, 16)
                for h in range(4):
                    r = slice(DK * h, DK * h + DK)
                    gp.dma_start(O["state"][r, bass.ds(c * (DB * 2 * DV), DB * 2 * DV)]
                                 .rearrange("p (b v) -> p b v", v=DV),
                                 Sd[r, :, :, DV * h:DV * h + DV].rearrange("p b q v -> p (b q) v")
                                 ).then_inc(s_out.sem, 16)
                gp.wait_ge(kv_out.sem, kv_out.at(c, 1))
                gp.wait_ge(s_out.sem, s_out.at(c, 4))
                for i in range(1, 4):
                    add_squares(c, i)
                gp.wait_ge(w_lo.sem, w_lo.at(c, PAIR0[PLE] * 2))
                for s in range(2):
                    u = c * UNITS + PAIR0[PLE] * 2 + s
                    gp.wait_ge(w_hi.sem, u + 1)
                    GP.tensor_tensor(wl[s][:, 0:KM * P], w_raw[s][:, 0:KM * P], wh[s][:, 0:KM * P].bitcast(f32),
                                     ALU.subtract).then_inc(w_lo.sem, 1)
                for k in range(KM + 2):
                    if k < KM:
                        gp.wait_ge(res.sem, res.at(c, 2 * KM + k + 1))
                        gp.dma_start(O["y"][:, bass.ds(c * (KM * T) + k * T, T)], x[:, k, :]
                                     ).then_inc(y_out[k % 2].sem, 16)
                    if 1 <= k <= KM:
                        s = (k - 1) % 2
                        gp.wait_ge(y_out[s].sem, y_out[s].at(c, (k - 1) // 2 + 1))
                        if not last:
                            gp.dma_start(x[:, k - 1, :], A["x"][:, bass.ds(c * (KM * T) + (KM + k - 1) * T, T)]
                                         ).then_inc(x_in[s].sem, 16)
                    if k >= 2 and not last:
                        x_square(c + 1, k - 2)

            with gp.Fori(0, CHUNKS - 1) as c:
                chunk(c, False)
            chunk(CHUNKS - 1, True)
            for h in range(4):
                r = slice(DK * h, DK * h + DK)
                gp.dma_start(O["state_p"][r, :, :], S[r, :, DV * h:DV * h + DV]).then_inc(last_out, 16)
            gp.wait_ge(last_out, 16 * 6)

        @block.scalar
        def _(act):
            A_ = nc.scalar.activation

            def split_hi(c, K, pair, s):
                act.wait_ge(w_in[s], c * (16 * PAIRS) + pair * 16 + 16)
                act.wait_ge(w_used.sem, c * UNITS + pair * 2 + (s + 1))
                A_(wh[s][:, 0:K * P], w_raw[s][:, 0:K * P], ACT.Copy).then_inc(w_hi.sem, 1)

            def units(c, i, work):
                _, n, K = PHASES[i]
                with act.Fori(0, n // 2 - 1) as j:
                    for s in range(2):
                        split_hi(c, K, j + (PAIR0[i] + 1), s)
                        work(j, s, j + PAIR0[i])
                split_hi(c, following(i)[2], PAIR0[i + 1], 0)
                for s in range(2):
                    work(n // 2 - 1, s, PAIR0[i + 1] - 1)
                split_hi(c, following(i)[2], PAIR0[i + 1], 1)

            def product_done(c, pair, s):
                act.wait_ge(w_used.sem, c * UNITS + pair * 2 + (s + 3))

            def both_drained(c, i):
                for s in range(2):
                    act.wait_ge(drained[s].sem, drained[s].at(c, PAIR0[i + 1]))

            def logs_and_exps():
                nc.scalar.preload_act_table_set("natural_log_exp_and_others")

            def first_guess(c, i):
                act.wait_ge(ss_mean.sem, ss_mean.at(c, i + 1))
                A_(half2(tmp_a[:]), ps[:, 6:8, 0:H], ACT.Ln, bias=cols[:, C_EPS:C_EPS + 1]).then_inc(rs_guess.sem, 1)
                act.wait_ge(rs_guess.sem, rs_guess.at(c, 2 * i + 1))
                A_(rs[:], tmp_a[:], ACT.Exp, scale=-0.5).then_inc(rs_guess.sem, 1)

            def square(c, i, k, src):
                if k >= 3:
                    act.wait_ge(ss.sem, ss.at(c, i * (KM - 2) + k - 2))
                A_(sqt[:, k % 2, :] if k else ssq[:], src, ACT.Square).then_inc(sq.sem, 1)

            def squares(c, i, phase):
                _, n, K = PHASES[phase]
                for j in range(n // 2):
                    last = j == n // 2 - 1

                    def split(s):
                        split_hi(c, following(phase)[2] if last else K, PAIR0[phase] + j + 1, s)

                    def tile(s):
                        act.wait_ge(drained[s].sem, drained[s].at(c, PAIR0[phase] + j + 1))
                        square(c, i, 2 * j + s, mix[:, 2 * j + s, :])
                    for step, s in ((split, 0), (tile, 0), (tile, 1), (split, 1)) if last \
                            else ((split, 0), (tile, 0), (split, 1), (tile, 1)):
                        step(s)

            def lev(c, t, w, l):
                act.wait_ge(p_diff.sem, p_diff.at(c, t, 2 * l + 2))
                A_(e_lev[l % 2][:, :, 0:w], e_lev[l % 2][:, :, 0:w], ACT.Exp, scale=1 / GATE_NORM
                   ).then_inc(a_lev.sem, 1)

            def tile_edge(c, t, w, before, wb):
                if t is not None:
                    sample = is_sample(t)
                    zq_, q_in = zt[:, ZSQ:ZSQ + 4, 0:w], columns(z, ZSQ, ZSQ + 4, t, w)
                    if sample:
                        zq_ = zt[:, ZSQ, 0:4 * DT].rearrange("p (b m i) -> p m b i", b=DB, m=4)
                        q_in = q_in.rearrange("p m (b i) -> p m b i", b=DB)
                    A_(zq_, q_in, ACT.Copy, scale=SCALE_S).then_inc(a_stage.sem, 1)
                    if sample:
                        act.wait_ge(dec_in.sem, dec_in.at(c, 2 + DB + 4))
                    elif before is not None:
                        act.wait_ge(p_kshift.sem, p_kshift.at(c, before, 1))
                    for g in range(2):
                        r = slice(DV * g, DV * g + DV)
                        if sample:
                            A_(kdec[r, :, g, P:P + DT], z[r, ZSK:ZSK + 1, PT:PT + DT].broadcast_to([DV, DB, DT]),
                               ACT.Copy).then_inc(a_stage.sem, 1)
                        else:
                            A_(kwin[r, 1, g, :], z[r, ZSK, tokens(t)], ACT.Copy).then_inc(a_stage.sem, 1)
                    lev(c, t, w, 0)
                    lev(c, t, w, 1)
                if before is not None:
                    act.wait_ge(v_o.sem, v_o.at(c, before, 1))
                    A_(o_sq[:, 0:4 * wb], od[:, 0:4 * wb], ACT.Square).then_inc(a_sq.sem, 1)
                if t is not None:
                    A_(zt[:, ZV:ZV + 4, 0:w], columns(z, ZV, ZV + 4, t, w), ACT.Copy).then_inc(a_stage.sem, 1)
                    A_(zt[:, ZSV:ZSV + 1, 0:w], columns(z, ZSV, ZSV + 1, t, w), ACT.Copy).then_inc(a_stage.sem, 1)
                    act.wait_ge(p_gend.sem, p_gend.at(c, t, p_gend.dec if sample else 1))
                    act.wait_ge(p_s.sem, p_s.at(c, t, 0))
                    A_(eg[:, :, 0:w], gt[:, :, 0:w], ACT.Exp, scale=1 / GATE_NORM).then_inc(a_eg.sem, 1)
                    for q in range(2):
                        for b, r in sample_spans(sample):
                            A_(ke[:, q, r], gt[:, q, r], ACT.Exp, bias=gend[:, q, b:b + 1], scale=-1 / GATE_NORM
                               ).then_inc(a_eg.sem, 1)
                if before is not None:
                    act.wait_ge(t_hn.sem, t_hn.at(c, before, 1))
                    A_(nrm[0][:, 0:4 * wb], ps[:, 0, 0:4 * wb], ACT.Ln, bias=cols[:, C_EPS:C_EPS + 1]
                       ).then_inc(a_rs.sem, 1)
                    act.wait_ge(a_rs.sem, a_rs.at(c, before, 1))
                    A_(nrm[0][:, 0:4 * wb], nrm[0][:, 0:4 * wb], ACT.Exp, scale=-0.5).then_inc(a_rs.sem, 1)
                if t is not None:
                    lev(c, t, w, 2)
                    act.wait_ge(v_max.sem, v_max.at(c, t, 4 if sample else 5))
                    if sample:
                        A_(scf[:, 0:P + DT], scf[:, 0:P + DT], ACT.Exp, bias=st_dec[:, 1:2], accum_out=st_dec[:, 3:4]
                           ).then_inc(a_exp.sem, 1)
                        A_(st_dec[:, 4:5], st_dec[:, 2:3], ACT.Exp).then_inc(a_exp.sem, 1)
                    else:
                        for m in range(4):
                            for g in range(2):
                                i = 2 * m + g
                                A_(sc[:, m, :, g, :], sc[:, m, :, g, :], ACT.Exp, bias=st[:, 3, i:i + 1],
                                   accum_out=st[:, 5, i:i + 1]).then_inc(a_exp.sem, 1)
                        A_(st[:, 6, 0:HEADS], st[:, 4, 0:HEADS], ACT.Exp).then_inc(a_exp.sem, 1)
                if before is not None:
                    act.wait_ge(t_pv.sem, t_pv.at(c, before, 1))
                    for b, r in sample_spans(is_sample(before)):
                        out = mix[:, 4:8, PT + r.start:PT + r.stop] if is_sample(before) \
                            else columns(mix, 4, 8, before, wb)
                        n = 4 * (r.stop - r.start)
                        A_(out, ps[:, 2, n * b:n * b + n].rearrange("p (m i) -> p m i", m=4), ACT.Copy
                           ).then_inc(a_pv.sem, 1)

            def tile_main(c, t, w):
                sample = is_sample(t)
                levels = DEC_LEVELS if sample else LEVELS
                act.wait_ge(t_vt.sem, t_vt.at(c, t, 1))
                act.wait_ge(p_vshift.sem, p_vshift.at(c, t, 0))
                A_(padded(vpad[0:w, :]), ps[0:w, 2, :].rearrange("p (j a d) -> p j a d", a=2, d=DV), ACT.Copy
                   ).then_inc(a_vt.sem, 1)
                A_(padded(vsp[0:w, 1, :]), ps[0:w, 3, 0:P].rearrange("p (j a d) -> p j a d", a=2, d=DV), ACT.Copy
                   ).then_inc(a_vt.sem, 1)
                act.wait_ge(t_kt.sem, t_kt.at(c, t, 1))
                n = 2 * P * (DB if sample else 1)
                A_(ktok[0:w, :, :].rearrange("p b n -> p (b n)")[:, 0:n], ps[0:w, 3, 0:n], ACT.Copy
                   ).then_inc(a_kt.sem, 1)
                if not sample:
                    lev(c, t, w, 3)
                act.wait_ge(v_den.sem, v_den.at(c, t, 2))
                if sample:
                    A_(scf[:, 0:P + DT], scf[:, 0:P + DT], ACT.Copy, scale=st_dec[:, 7:8]).then_inc(a_norm.sem, 1)
                    act.wait_ge(t_pt.sem, t_pt.at(c, t, 1))
                    A_(pt_dec[:, 0:P], ps[:, 4, 0:P], ACT.Copy).then_inc(a_pt.sem, 1)
                    A_(pt_dec[0:DT, P:2 * P], ps[0:DT, 4, P:2 * P], ACT.Copy).then_inc(a_pt.sem, 1)
                    return

                def normalise(m):
                    for g in range(2):
                        A_(sc[:, m, :, g, :], sc[:, m, :, g, :], ACT.Copy, scale=st[:, 8, 2 * m + g:2 * m + g + 1]
                           ).then_inc(a_norm.sem, 1)

                def by_key(hf):
                    if hf == 0:
                        act.wait_ge(t_pt.sem, t_pt.at(c, t, 1))
                    for i in (2 * hf, 2 * hf + 1):
                        A_(pt[i], ps[:, 4 + i, :], ACT.Copy).then_inc(a_pt.sem, 1)
                normalise(0)
                lev(c, t, w, 4)
                normalise(1)
                normalise(2)
                lev(c, t, w, 5)
                normalise(3)
                lev(c, t, w, 6)
                by_key(0)
                by_key(1)
            act.wait_ge(first_in, 16 * len(first_loads))
            A_(lrh[:, :, :], lr_raw[:, :, :], ACT.Copy).then_inc(consts_set, 1)
            act.wait_ge(consts_set, N_SET)
            for s in range(2):
                act.wait_ge(w_in[s], 16)
                A_(wh[s][:, 0:KM * P], w_raw[s][:, 0:KM * P], ACT.Copy).then_inc(w_hi.sem, 1)

            for k in range(KM):
                act.wait_ge(x_in[k % 2].sem, 16 * (k // 2 + 1))
                if k >= 3:
                    act.wait_ge(ss.sem, k - 2)
                A_(sqt[:, k % 2, :] if k else ssq[:], x[:, k, :], ACT.Square).then_inc(sq_x.sem, 1)

            with act.Fori(0, CHUNKS) as c:
                for k in range(KM):
                    act.wait_ge(x_in[k % 2].sem, x_in[k % 2].at(c, k // 2 + 1))
                    A_(ah[:, k, :], x[:, k, :], ACT.Copy, scale=cols[:, W_PRE + k:W_PRE + k + 1]).then_inc(a_hi.sem, 1)
                logs_and_exps()
                first_guess(c, 0)
                units(c, OG, lambda j, s, pair: None)
                both_drained(c, OG)
                A_(z[:, ZO:ZO + 4, :], z[:, ZO:ZO + 4, :], ACT.Silu).then_inc(og_silu.sem, 1)
                logs_and_exps()
                act.wait_ge(gate_vec.sem, gate_vec.at(c, 3))
                A_(tmp[:, :, :], tmp[:, :, :], ACT.Exp).then_inc(gate_act.sem, 1)
                act.wait_ge(gate_act.sem, gate_act.at(c, 1))
                A_(tmp[:, :, :], tmp[:, :, :], ACT.Ln, bias=1.0).then_inc(gate_act.sem, 1)
                units(c, ZZ, lambda j, s, pair: None)
                both_drained(c, ZZ)

                tile_loop(act, lambda *a: tile_edge(c, *a), lambda *a: tile_main(c, *a))
                act.wait_ge(a_pv.sem, a_pv.chunk_end(c))
                act.wait_ge(p_gate.sem, p_gate.chunk_end(c))
                act.wait_ge(p_s.sem, p_s.chunk_end(c))
                for k in range(KM):
                    A_(ah[:, k, :], mix[:, k, :], ACT.Copy).then_inc(a_hi.sem, 1)

                squares(c, 1, OUT)
                first_guess(c, 1)
                for k in range(KM):
                    act.wait_ge(res.sem, res.at(c, k + 1))
                    A_(ah[:, k, :], x[:, k, :], ACT.Copy, scale=cols[:, W_FFN + k:W_FFN + k + 1]).then_inc(a_hi.sem, 1)
                    square(c, 2, k, x[:, k, :])
                first_guess(c, 2)

                for f in range(2):
                    def gu_work(j, s, pair):
                        if s == 0:
                            act.wait_ge(drained[0].sem, c * PAIRS + pair + 2)
                            A_(tmp[:, 0, :], tmp[:, 0, :], ACT.Silu).then_inc(sig.sem, 1)
                        else:
                            act.wait_ge(prod.sem, c * prod.chunk + j + (KF * f + 1))
                            A_(at(gh, j), tmp[:, 1, :], ACT.Copy).then_inc(gu_hi.sem, 1)
                    units(c, GU + 2 * f, gu_work)
                    if f == 0:
                        act.wait_ge(p_in.sem, p_in.at(c, 1))
                        A_(ph[:, :, :], p_raw[:, :, :], ACT.Copy).then_inc(p_hi.sem, 1)
                        units(c, GU + 1, lambda j, s, pair: None)
                logs_and_exps()
                squares(c, 3, GU + 3)
                first_guess(c, 3)

                def proj_move(m):
                    if m % 4 == 3:
                        act.wait_ge(w_used.sem, c * UNITS + PAIR0[PROJ] * 2 + (m // 4 + 3))
                    else:
                        act.wait_ge(t_proj.sem, t_proj.at(c, m - m // 4 + 1))
                    b = PROJ_ACC[m]
                    A_(half2(proj[:, m, :]), ps[:, b:b + 2, 0:H], ACT.Copy).then_inc(proj_out.sem, 1)
                for m in range(4):
                    proj_move(m)
                split_hi(c, KM, PAIR0[PLE], 0)
                for m in (4, 5):
                    proj_move(m)
                act.wait_ge(proj_out.sem, proj_out.at(c, 6))
                for s in range(2):
                    act.sem_inc(drained[s].sem)
                for k in range(KM):
                    act.wait_ge(res.sem, res.at(c, KM + k + 1))
                    A_(ah[:, k, :], x[:, k, :], ACT.Copy).then_inc(a_hi.sem, 1)
                    if k in (1, 2):
                        proj_move(k + 5)
                    if k == 4:
                        split_hi(c, KM, PAIR0[PLE], 1)

                def ple_work(j, s, pair):
                    product_done(c, pair, s)
                    act.wait_ge(res.sem, c * res.chunk + j * 2 + (2 * KM + s - 1))
                    A_(half2(tmp[:, s, :]), acc(s), ACT.Sigmoid).then_inc(drained[s].sem, 1)
                units(c, PLE, ple_work)

        @block.vector
        def _(dve):
            V = nc.vector

            def split_lo(c, K, pair, s):
                dve.wait_ge(w_hi.sem, c * UNITS + pair * 2 + (s + 1))
                V.tensor_tensor(wl[s][:, 0:K * P], w_raw[s][:, 0:K * P], wh[s][:, 0:K * P].bitcast(f32),
                                ALU.subtract).then_inc(w_lo.sem, 1)

            def units(c, i, work):
                _, n, K = PHASES[i]
                with dve.Fori(0, n // 2 - 1) as j:
                    for s in range(2):
                        split_lo(c, K, j + (PAIR0[i] + 1), s)
                        work(j, s, j + PAIR0[i])
                split_lo(c, following(i)[2], PAIR0[i + 1], 0)
                for s in range(2):
                    work(n // 2 - 1, s, PAIR0[i + 1] - 1)
                split_lo(c, following(i)[2], PAIR0[i + 1], 1)

            def product_done(c, pair, s):
                dve.wait_ge(w_used.sem, c * UNITS + pair * 2 + (s + 3))

            def newton(c, i):
                steps = (
                    lambda: V.tensor_tensor(tmp_a[:], rs[:], rs[:], ALU.mult),
                    lambda: V.scalar_tensor_tensor(half2(tmp_a[:]), ps[:, 6:8, 0:H], cols[:, C_EPS:C_EPS + 1],
                                                   half2(tmp_a[:]), ALU.add, ALU.mult),
                    lambda: V.scalar_tensor_tensor(rs[:], tmp_a[:], -3.0, rs[:], ALU.add, ALU.mult))
                dve.wait_ge(rs_guess.sem, rs_guess.at(c, 2 * i + 2))
                for n, step in enumerate(steps):
                    step().then_inc(rs_newton.sem, 1)
                    dve.wait_ge(rs_newton.sem, rs_newton.at(c, 3 * i + n + 1))

            def normed(dst, src, part=slice(0, P)):
                return V.scalar_tensor_tensor(dst, src, -0.5, half2(rs[part, :]), ALU.mult, ALU.mult)

            def lo(c, a0, k, src):
                dve.wait_ge(a_hi.sem, a_hi.at(c, a0 + k + 1))
                V.tensor_tensor(al[:, k, :], src, ah[:, k, :].bitcast(f32), ALU.subtract).then_inc(a_lo.sem, 1)

            def lo_weighted(c, a0, k, wcol):
                dve.wait_ge(a_hi.sem, a_hi.at(c, a0 + k + 1))
                V.scalar_tensor_tensor(al[:, k, :], x[:, k, :], cols[:, wcol + k:wcol + k + 1],
                                       ah[:, k, :].bitcast(f32), ALU.mult, ALU.subtract).then_inc(a_lo.sem, 1)

            def add_branch(c, n0, r0, wcol, then):
                for k in range(KM):
                    if k >= 2:
                        dve.wait_ge(res.sem, res.at(c, r0 + k - 1))
                    V.scalar_tensor_tensor(tmp[:, k % 2, :], mix[:, k, :], cols[:, wcol + k:wcol + k + 1], rs[:],
                                           ALU.mult, ALU.mult).then_inc(branch.sem, 1)
                    dve.wait_ge(branch.sem, branch.at(c, n0 + k + 1))
                    V.tensor_tensor(x[:, k, :], x[:, k, :], tmp[:, k % 2, :], ALU.add).then_inc(res.sem, 1)
                    if k:
                        then(k - 1)
                then(KM - 1)

            def decay(c, t, w, l):
                s, n = 1 << l, w >> (l + 1)
                e = split_blocks(e_lev[l % 2][:, :, 0:w], l)
                dve.wait_ge(a_lev.sem, a_lev.at(c, t, l + 1))
                if l >= 2:
                    dve.wait_ge(t_lev.sem, t_lev.at(c, t, l - 1))
                if l == 0:
                    dve.wait_ge(v_q.sem, v_q.at(c, t, 2))
                V.tensor_tensor(kd[l % 2][:, :, 0:w], zt[:, ZK:ZK + 2, 0:w], e_lev[l % 2][:, :, 0:w], ALU.mult
                                ).then_inc(v_lev.sem, 1)
                if l == 0:
                    dve.wait_ge(v_q.sem, v_q.at(c, t, 4))
                for q in range(2):
                    V.tensor_tensor(
                        qd[l % 2][:, q, :, 0:w // 2].rearrange("p h (b s) -> p h b s", s=s),
                        split_blocks(qm[:, q, :, 0:w], l)[:, :, :, 1, :],
                        e[:, q:q + 1, :, 1, :].broadcast_to([P, 4, n, s]), ALU.mult).then_inc(v_lev.sem, 1)

            def tile_edge(c, t, w, before, wb):
                if t is not None:
                    V.tensor_scalar(zt[:, ZQ:ZQ + 2, 0:w], columns(z, ZQ, ZQ + 2, t, w), SCALE_G, None, ALU.mult
                                    ).then_inc(v_q.sem, 1)
                    V.tensor_copy(zt[:, ZK:ZK + 2, 0:w], columns(z, ZK, ZK + 2, t, w)).then_inc(v_q.sem, 1)
                    dve.wait_ge(v_q.sem, v_q.at(c, t, 1))
                    for q in range(2):
                        V.tensor_tensor(
                            qm[:, q, :, 0:w], zt[:, ZQ + q:ZQ + q + 1, 0:w].broadcast_to([P, 4, w]),
                            head_mask[:, :].rearrange("p (h a) -> p h a", a=1).broadcast_to([P, 4, w]),
                            ALU.mult).then_inc(v_q.sem, 1)
                    decay(c, t, w, 0)
                if before is not None:
                    dve.wait_ge(t_o.sem, t_o.at(c, before, 1))
                    V.tensor_tensor(od[:, 0:4 * wb], od[:, 0:4 * wb], ps[:, 0, 0:4 * wb], ALU.add).then_inc(v_o.sem, 1)
                if t is not None:
                    scores(c, t, w)
                if before is not None:
                    mean, o = ps[:, 0, 0:4 * wb], od[:, 0:4 * wb]
                    r_, h_ = nrm[0][:, 0:4 * wb], nrm[1][:, 0:4 * wb]
                    steps = (
                        lambda: V.tensor_tensor(h_, r_, r_, ALU.mult),
                        lambda: V.scalar_tensor_tensor(h_, mean, cols[:, C_EPS:C_EPS + 1], h_, ALU.add, ALU.mult),
                        lambda: V.scalar_tensor_tensor(r_, h_, -3.0, r_, ALU.add, ALU.mult),
                        lambda: V.scalar_tensor_tensor(h_, o, cols[:, C_HN:C_HN + 1], r_, ALU.mult, ALU.mult))
                    dve.wait_ge(a_rs.sem, a_rs.at(c, before, 2))
                    for n, step in enumerate(steps):
                        step().then_inc(v_rs.sem, 1)
                        dve.wait_ge(v_rs.sem, v_rs.at(c, before, n + 1))
                    dve.sem_inc(passed["dve"])

            def scores(c, t, w):
                if is_sample(t):
                    dve.wait_ge(t_sc.sem, t_sc.at(c, t, 1))
                    V.tensor_tensor(scf[:, 0:P + DT], ps[:, 4, 0:P + DT], bias_dec[:], ALU.add).then_inc(v_sc.sem, 1)
                    dve.wait_ge(v_sc.sem, v_sc.at(c, t, 1))
                    V.reduce_max(st_dec[:, 0:1], scf[:, 0:P + DT], AX.X).then_inc(v_max.sem, 1)
                    dve.wait_ge(v_max.sem, v_max.at(c, t, 1))
                    V.tensor_tensor(st_dec[:, 5:6], st_dec[:, 0:1], sink_dec[:], ALU.max).then_inc(v_max.sem, 1)
                    dve.wait_ge(v_max.sem, v_max.at(c, t, 2))
                    V.tensor_scalar(st_dec[:, 1:2], st_dec[:, 5:6], -1.0, None, ALU.mult).then_inc(v_max.sem, 1)
                    V.tensor_tensor(st_dec[:, 2:3], sink_dec[:], st_dec[:, 5:6], ALU.subtract).then_inc(v_max.sem, 1)
                    return
                for m in range(4):
                    dve.wait_ge(t_sc.sem, t_sc.at(c, t, m + 1))
                    for g in range(2):
                        V.scalar_tensor_tensor(
                            sc[:, m, :, g, :], dist[:, :, :], -SLOPES[4 * g + m],
                            ps[:, 4 + m, :].rearrange("p (h g k) -> p h g k", h=2, g=2)[:, :, g, :],
                            ALU.mult, ALU.add).then_inc(v_sc.sem, 1)
                dve.wait_ge(v_sc.sem, v_sc.at(c, t, 8))
                V.tensor_copy(dist[:, 0, :], dist_prev[:]).then_inc(v_sc.sem, 1)
                V.reduce_max(st[:, 0, :], scf.rearrange("p (a k) -> p a k", k=P), AX.X).then_inc(v_max.sem, 1)
                dve.wait_ge(v_max.sem, v_max.at(c, t, 1))
                mx = st[:, 0, :].rearrange("p (m h g) -> p m h g", h=2, g=2)
                V.tensor_tensor(st[:, 1, 0:8].rearrange("p (m g) -> p m g", g=2), mx[:, :, 0, :], mx[:, :, 1, :],
                                ALU.max).then_inc(v_max.sem, 1)
                dve.wait_ge(v_max.sem, v_max.at(c, t, 2))
                V.tensor_tensor(st[:, 2, 0:8], st[:, 1, 0:8], sinks[:], ALU.max).then_inc(v_max.sem, 1)
                dve.wait_ge(v_max.sem, v_max.at(c, t, 3))
                V.tensor_scalar(st[:, 3, 0:8], st[:, 2, 0:8], -1.0, None, ALU.mult).then_inc(v_max.sem, 1)
                V.tensor_tensor(st[:, 4, 0:8], sinks[:], st[:, 2, 0:8], ALU.subtract).then_inc(v_max.sem, 1)

            def tile_main(c, t, w):
                sample = is_sample(t)
                levels = DEC_LEVELS if sample else LEVELS
                def put(l):
                    s, n = 1 << l, w >> (l + 1)
                    dve.wait_ge(t_lev.sem, t_lev.at(c, t, l + 1))
                    if l:
                        dve.wait_ge(v_put.sem, v_put.at(c, t, l))
                    dve.sem_inc(passed["dve"])
                    V.copy_predicated(
                        split_blocks(A_t[0:w, :, 0:w], l)[:, :, :, 1, :],
                        lev_mask[0:w, l:l + 1, 0:w // 2].rearrange("p h (b s) -> p h b s", s=s)
                        .broadcast_to([w, 8, n, s]),
                        ps[0:w, (l + 1) % 2, 0:4 * w].rearrange("p (h b s) -> p h b s", h=8, s=s)
                    ).then_inc(v_put.sem, 1)

                dve.wait_ge(t_diag.sem, t_diag.at(c, t, 1))
                dve.wait_ge(a_stage.sem, a_stage.at(c, t, 4))
                V.tensor_tensor(od[:, 0:4 * w].rearrange("p (j i) -> p j i", j=4),
                                ps[:, 0, 0:4 * w].rearrange("p (j i) -> p j i", j=4),
                                zt[:, ZV:ZV + 4, 0:w], ALU.mult).then_inc(v_diag.sem, 1)
                if sample:
                    V.memset(A_t[0:w, :, 0:w], 0.0).then_inc(v_zero.sem, 1)
                    dve.wait_ge(v_zero.sem, v_zero.at(c, 2))
                for l in range(1, levels):
                    decay(c, t, w, l)
                    if l == 2:
                        s_ = [st_dec[:, i:i + 1] for i in (3, 4, 6, 7)] if sample \
                            else [st[:, i, 0:HEADS] for i in (5, 6, 7, 8)]
                        dve.wait_ge(a_exp.sem, a_exp.at(c, t, 2 if sample else HEADS + 1))
                        V.tensor_tensor(s_[2], s_[0], s_[1], ALU.add).then_inc(v_den.sem, 1)
                        dve.wait_ge(v_den.sem, v_den.at(c, t, 1))
                        V.reciprocal(s_[3], s_[2]).then_inc(v_den.sem, 1)
                    put(l - 1)
                    if l == (2 if sample else 3):
                        for b, _ in sample_spans(sample):
                            dve.wait_ge(t_u.sem, t_u.at(c, t, b + 1))
                            V.tensor_tensor(um[:, b, :, :], ps[:, 2 + b, :].rearrange("p (q n) -> p q n", q=2),
                                            block_mask[:, :].rearrange("p (a n) -> p a n", a=1)
                                            .broadcast_to([P, 2, 4 * DV]), ALU.mult).then_inc(v_u.sem, 1)
                put(levels - 1)
                dve.wait_ge(v_diag.sem, v_diag.at(c, t, 1))
                dve.sem_inc(passed["dve"])

            early = [g.sem for g in (w_lo, w_used, *drained, gu_lo, v_rs, a_pv, p_s, p_vshift) for _ in range(g.first)]
            for s_ in early:
                V.memset(st[:, :, :], 0.0).then_inc(s_, 1)
                dve.drain()
            for b in zeroed:
                V.memset(b[:] if len(b.shape) == 2 else b[(slice(None),) * len(b.shape)], 0.0).then_inc(consts_set, 1)
            dve.wait_ge(first_in, 16 * len(first_loads))
            dve.wait_ge(consts_set, N_SET - 4)
            V.tensor_tensor(lrl[:, :, :], lr_raw[:, :, :], lrh[:, :, :].bitcast(f32), ALU.subtract
                            ).then_inc(consts_set, 1)
            for wcol, n in ((W_POST, KM), (W_PFFN, KM), (C_HN, 1)):
                V.tensor_scalar(cols[:, wcol:wcol + n], cols[:, wcol:wcol + n], -0.5, None, ALU.mult
                                ).then_inc(consts_set, 1)
            dve.wait_ge(consts_set, N_SET)
            for s in range(2):
                dve.wait_ge(w_hi.sem, 1 + s)
                V.tensor_tensor(wl[s][:, 0:KM * P], w_raw[s][:, 0:KM * P], wh[s][:, 0:KM * P].bitcast(f32),
                                ALU.subtract).then_inc(w_lo.sem, 1)

            for k in range(1, KM - 1):
                dve.wait_ge(sq_x.sem, k + 1)
                if k >= 2:
                    dve.wait_ge(ss.sem, k - 1)
                V.tensor_tensor(ssq[:], ssq[:], sqt[:, k % 2, :], ALU.add).then_inc(ss.sem, 1)

            with dve.Fori(0, CHUNKS) as c:
                for k in range(KM):
                    lo_weighted(c, 0, k, W_PRE)
                newton(c, 0)
                dve.wait_ge(lr_sum.sem, lr_sum.at(c, 1))
                normed(half2(lr_t[:]), ps[0:LOW_RANK, 4:6, 0:H], slice(0, LOW_RANK)).then_inc(lr_got.sem, 1)

                def z_work(phase, z0):
                    def work(j, s, pair):
                        product_done(c, pair, s)
                        normed(half2(at(z, j * 2 + (z0 + s))), acc(s)).then_inc(drained[s].sem, 1)
                    units(c, phase, work)
                z_work(OG, ZO)
                dve.wait_ge(consts_in, 16 * len(loads))
                dve.wait_ge(gate_sum.sem, gate_sum.at(c, 1))
                for q in range(2):
                    V.tensor_scalar(half2(G[:, q, :]), ps[:, 4 + 2 * q:6 + 2 * q, 0:H],
                                    cols[:, C_GB + q:C_GB + q + 1], None, ALU.add).then_inc(gate_vec.sem, 1)
                dve.wait_ge(gate_vec.sem, gate_vec.at(c, 2))
                V.scalar_tensor_tensor(tmp[:, :, :], G[:, :, :], -1.0, G[:, :, :], ALU.mult, ALU.min
                                       ).then_inc(gate_vec.sem, 1)
                dve.wait_ge(gate_act.sem, gate_act.at(c, 2))
                V.scalar_tensor_tensor(tmp[:, :, :], G[:, :, :], 0.0, tmp[:, :, :], ALU.min, ALU.subtract
                                       ).then_inc(gate_vec.sem, 1)
                dve.wait_ge(gate_vec.sem, gate_vec.at(c, 4))
                V.tensor_tensor_scan(G[:, :, :].rearrange("p q t -> p (q t)"), keep[:],
                                     tmp[:, :, :].rearrange("p q t -> p (q t)"), 0.0, ALU.mult, ALU.add
                                     ).then_inc(gate_vec.sem, 1)

                z_work(ZZ, 0)
                dve.wait_ge(og_silu.sem, og_silu.at(c, 1))
                dve.wait_ge(gate_vec.sem, gate_vec.at(c, 5))
                dve.wait_ge(drained[0].sem, drained[0].at(c, PAIR0[ZZ + 1]))
                dve.wait_ge(drained[1].sem, drained[1].at(c, PAIR0[ZZ + 1]))
                dve.sem_inc(passed["dve"])
                V.memset(A_t[:, :, :], 0.0).then_inc(v_zero.sem, 1)
                dve.wait_ge(v_zero.sem, v_zero.at(c, 1))
                dve.sem_inc(passed["dve"])
                tile_loop(dve, lambda *a: tile_edge(c, *a), lambda *a: tile_main(c, *a))
                for k in range(KM):
                    lo(c, KM, k, mix[:, k, :])

                def out_work(j, s, pair):
                    product_done(c, pair, s)
                    V.tensor_copy(half2(at(mix, j * 2 + s)), acc(s)).then_inc(drained[s].sem, 1)
                units(c, OUT, out_work)
                newton(c, 1)
                add_branch(c, 0, 0, W_POST, lambda k: lo_weighted(c, 2 * KM, k, W_FFN))
                newton(c, 2)
                dve.sem_inc(passed["dve"])
                for f in range(2):
                    def gu_work(j, s, pair):
                        product_done(c, pair, s)
                        if f == 0 and s == 0:
                            dve.wait_ge(kv_out.sem, kv_out.at(c, 1))
                        if s == 1:
                            dve.wait_ge(gu_lo.sem, c * gu_lo.chunk + j + (f * KF + 1))
                        normed(half2(tmp[:, s, :]), acc(s)).then_inc(drained[s].sem, 1)
                        if s == 1:
                            dve.wait_ge(drained[1].sem, c * PAIRS + pair + 2)
                            dve.wait_ge(sig.sem, c * sig.chunk + j + (f * KF + 1))
                            V.tensor_tensor(tmp[:, 1, :], tmp[:, 0, :], tmp[:, 1, :], ALU.mult).then_inc(prod.sem, 1)
                            dve.wait_ge(gu_hi.sem, c * gu_hi.chunk + j + (f * KF + 1))
                            V.tensor_tensor(at(gl, j), tmp[:, 1, :], at(gh, j).bitcast(f32), ALU.subtract
                                            ).then_inc(gu_lo.sem, 1)
                    units(c, GU + 2 * f, gu_work)
                    if f == 0:
                        dve.wait_ge(p_hi.sem, p_hi.at(c, 1))
                        V.tensor_tensor(pl[:, :, :], p_raw[:, :, :], ph[:, :, :].bitcast(f32), ALU.subtract
                                        ).then_inc(p_lo.sem, 1)

                    def down_work(j, s, pair):
                        product_done(c, pair, s)
                        dst = half2(at(mix, j * 2 + s))
                        if f == 0:
                            V.tensor_copy(dst, acc(s)).then_inc(drained[s].sem, 1)
                        else:
                            V.tensor_tensor(dst, dst, acc(s), ALU.add).then_inc(drained[s].sem, 1)
                    units(c, GU + 1 + 2 * f, down_work)
                newton(c, 3)
                add_branch(c, KM, KM, W_PFFN, lambda k: lo(c, 3 * KM, k, x[:, k, :]))

                dve.wait_ge(proj_out.sem, proj_out.at(c, KM))
                dve.wait_ge(w_lo.sem, w_lo.at(c, PAIR0[PLE] * 2 + 2))
                dve.sem_inc(passed["dve"])

                def ple_work(j, s, pair):
                    dve.wait_ge(drained[s].sem, c * PAIRS + pair + 2)
                    V.tensor_tensor(tmp[:, s, :], tmp[:, s, :], at(proj, j * 2 + s), ALU.mult).then_inc(gated.sem, 1)
                    dve.wait_ge(gated.sem, c * KM + j * 2 + (s + 1))
                    dst = at(x, j * 2 + s)
                    V.tensor_tensor(dst, dst, tmp[:, s, :], ALU.add).then_inc(res.sem, 1)
                units(c, PLE, ple_work)

        @block.tensor
        def _(pe):
            MM = nc.tensor.matmul

            def three_pass(out, k, K, whi, wlo, xhi, xlo, first):
                last = None
                for n_pass, (w_, x_) in enumerate(((whi, xhi), (whi, xlo), (wlo, xhi))):
                    for n in range(2):
                        last = MM(out[:, n, :], w_, x_[:, n * H:(n + 1) * H], start=(first and n_pass == 0),
                                  stop=(k == K - 1 and n_pass == 2))
                return last

            def unit(c, s, pair, K, hi, lo_, ready=None):
                pe.wait_ge(w_lo.sem, c * UNITS + pair * 2 + (s + 3))
                pe.wait_ge(drained[s].sem, c * PAIRS + pair + 1)
                for k in range(K):
                    if ready:
                        ready(k)
                    last = three_pass(acc(s), k, K, wh[s][:, k * P:(k + 1) * P], wl[s][:, k * P:(k + 1) * P],
                                      hi[:, k, :], lo_[:, k, :], k == 0)
                return last

            def units(c, i, hi, lo_, K, ready=None, after_first=None):
                _, n, _ = PHASES[i]

                def pair(j, ready):
                    for s in range(2):
                        last = unit(c, s, j + PAIR0[i], K, hi, lo_, ready if s == 0 else None)
                        last.then_inc(w_used.sem, 1)
                        if ready and s == 0 and after_first:
                            after_first()
                if ready:
                    pair(0, ready)
                with pe.Fori(1 if ready else 0, n // 2) as j:
                    pair(j, None)

            def split(c, i):
                def ready(k):
                    pe.wait_ge(a_lo.sem, a_lo.at(c, i * KM + k + 1))
                return ready

            def mean(c, i, parts=(False, True)):
                for last_tile in parts:
                    if not last_tile:
                        pe.wait_ge(ss.sem, ss.at(c, (i + 1) * (KM - 2)))
                    elif i == 0:
                        pe.wait_ge(sq_x.sem, sq_x.at(c, KM))
                    else:
                        pe.wait_ge(sq.sem, sq.at(c, i * KM))
                    for n in range(2):
                        src = sqt[:, 1, n * H:(n + 1) * H] if last_tile else ssq[:, n * H:(n + 1) * H]
                        last = MM(ps[:, 6 + n, 0:H], mean_w[:], src, start=not last_tile, stop=last_tile)
                if parts[-1]:
                    last.then_inc(ss_mean.sem, 1)

            def level(c, t, w, l):
                rt = w // 2
                pe.wait_ge(v_lev.sem, v_lev.at(c, t, 3 * l + 3))
                if l == 1:
                    pe.wait_ge(v_diag.sem, v_diag.at(c, t, 1))
                elif l:
                    pe.wait_ge(v_put.sem, v_put.at(c, t, l - 1))
                for q in range(2):
                    last = MM(ps[0:w, (l + 1) % 2, q * 4 * rt:(q + 1) * 4 * rt].rearrange("p (h i) -> p h i", h=4),
                              kd[l % 2][:, q, 0:w], qd[l % 2][:, q, :, 0:rt], start=True, stop=True)
                last.then_inc(t_lev.sem, 1)

            def window_out(c, t, hf):
                if hf == 0:
                    pe.wait_ge(v_u.sem, v_u.at(c, t, 1))
                pe.wait_ge(a_pt.sem, a_pt.at(c, t, 2 * hf + 2))
                for g in range(2):
                    i = 2 * hf + g
                    last = MM(ps[:, 2, :], vsp[:, hf, g * P:(g + 1) * P], pt[i], start=(i == 0), stop=(i == 3))
                if hf:
                    last.then_inc(t_pv.sem, 1)

            def tile_edge(c, t, w, before, wb):
                if t is not None:
                    pe.wait_ge(a_stage.sem, a_stage.at(c, t, 3))
                    if is_sample(t):
                        for b in range(DB):
                            for g in range(2):
                                i = 32 * (2 * b + g)
                                last = MM(ps[i:i + 32, 4, 0:P + DT], zt[:, ZSQ, 32 * b:32 * b + 32], kdec[:, b, g, :],
                                          start=True, stop=True)
                    else:
                        for m in range(4):
                            last = MM(ps[:, 4 + m, :], zt[:, ZSQ + m, :],
                                      kwin[:, :, :, :].rearrange("p h g k -> p (h g k)"), start=True, stop=True)
                            if m < 3:
                                last.then_inc(t_sc.sem, 1)
                    last.then_inc(t_sc.sem, 1)
                    level(c, t, w, 0)
                if before is not None:
                    pe.wait_ge(a_sq.sem, a_sq.at(c, before, 1))
                    MM(ps[:, 0, 0:4 * wb], head_w[:], o_sq[:, 0:4 * wb], start=True, stop=True).then_inc(t_hn.sem, 1)
                    if not is_sample(before):
                        window_out(c, before, 0)
                        window_out(c, before, 1)
            def tile_main(c, t, w):
                sample = is_sample(t)
                spans = range(DB) if sample else range(1)

                def by_key(m0):
                    pe.wait_ge(a_norm.sem, a_norm.at(c, t, 2 * m0 + 4))
                    for i in range(4):
                        hf, g = divmod(i, 2)
                        for m in (m0, m0 + 1):
                            last = nc.tensor.transpose(ps[:, 4 + i, m * P:(m + 1) * P], sc[:, m, hf, g, :], ident[:])
                    if m0:
                        last.then_inc(t_pt.sem, 1)

                pe.wait_ge(p_qk.sem, p_qk.at(c, t, 1))
                pe.wait_ge(v_rs.sem, v_rs.at(c, t, -2))
                for jj in range(2):
                    last = MM(ps[:, 0, 0:4 * w].rearrange("p (q j i) -> p q j i", q=2, j=2)[:, :, jj, :],
                              block_mask[:, jj * P:(jj + 1) * P], qk[:, :, 0:w], start=True, stop=True)
                last.then_inc(t_diag.sem, 1)
                level(c, t, w, 1)
                pe.wait_ge(a_stage.sem, a_stage.at(c, t, 5))
                pe.wait_ge(a_pv.sem, a_pv.at(c, t, 0))
                for j in range(4):
                    nc.tensor.transpose(ps[0:w, 2, j * P:(j + 1) * P], zt[:, ZV + j, 0:w], ident[:])
                nc.tensor.transpose(ps[0:w, 3, 0:P], zt[:, ZSV, 0:w], ident[:]).then_inc(t_vt.sem, 1)
                pe.wait_ge(p_qe.sem, p_qe.at(c, t, DB if sample else 1))
                pe.wait_ge(a_vt.sem, a_vt.at(c, t, 2))
                for b in spans:
                    for q in range(2):
                        last = nc.tensor.transpose(ps[0:w, 3, (2 * b + q) * P:(2 * b + q + 1) * P],
                                                   ke2[:, b, q, :] if sample else ke[:, q, :], ident[:])
                last.then_inc(t_kt.sem, 1)
                level(c, t, w, 2)
                pe.wait_ge(a_kt.sem, a_kt.at(c, t, 1))
                for b in spans:
                    for q in range(2):
                        last = MM(ps[:, 2 + b, q * 4 * DV:(q + 1) * 4 * DV], ktok[0:w, b, q * P:(q + 1) * P],
                                  padded(vpad[0:w, q * 4 * P:(q + 1) * 4 * P]), start=True, stop=True)
                    last.then_inc(t_u.sem, 1)
                if sample:
                    pe.wait_ge(a_norm.sem, a_norm.at(c, t, 1))
                    nc.tensor.transpose(ps[:, 4, 0:P], scf[:, 0:P], ident[:])
                    nc.tensor.transpose(ps[0:DT, 4, P:2 * P], scf[:, P:P + DT], ident[:]).then_inc(t_pt.sem, 1)
                    pe.wait_ge(v_u.sem, v_u.at(c, t, DB))
                    pe.wait_ge(a_pt.sem, a_pt.at(c, t, 2))
                    for b in range(DB):
                        out = ps[:, 2, 32 * b:32 * b + 32]
                        for g in range(2):
                            i = 32 * (2 * b + g)
                            MM(out, vdec[:, b, g * P:(g + 1) * P], pt_dec[:, i:i + 32], start=(g == 0), stop=False)
                            last = MM(out, vsp[0:DT, 1, g * P:(g + 1) * P], pt_dec[0:DT, P + i:P + i + 32],
                                      start=False, stop=(g == 1))
                    last.then_inc(t_pv.sem, 1)
                else:
                    level(c, t, w, 3)
                    by_key(0)
                    level(c, t, w, 4)
                    by_key(2)
                    level(c, t, w, 5)
                    level(c, t, w, 6)
                pe.wait_ge(v_put.sem, v_put.at(c, t, DEC_LEVELS if sample else LEVELS))
                pe.wait_ge(p_qe.sem, p_qe.at(c, t, p_qe.dec if sample else 2))
                pe.wait_ge(p_s.sem, p_s.at(c, t, 0))
                for j in range(4):
                    out = ps[:, 0, j * w:(j + 1) * w]
                    q = j // 2
                    for hh in range(2):
                        h = 2 * j + hh
                        MM(out, vpad[0:w, h * P:(h + 1) * P], A_t[0:w, h, 0:w], start=(hh == 0), stop=False)
                    r = slice((j % 2) * P, (j % 2) * P + P)
                    if sample:
                        for b in range(DB):
                            last = MM(out[:, DEC_SEQ * b:DEC_SEQ * b + DEC_SEQ], Sd[:, b, q, r],
                                      qe[:, q, DEC_SEQ * b:DEC_SEQ * b + DEC_SEQ], start=False, stop=(b == DB - 1))
                    else:
                        last = MM(out, S[:, q, r], qe[:, q, :], start=False, stop=True)
                last.then_inc(t_o.sem, 1)

            pe.wait_ge(consts_set, N_SET)
            with pe.Fori(0, CHUNKS) as c:
                for k in range(KM):
                    split(c, 0)(k)
                    last = three_pass(ps[0:LOW_RANK, 4:6, 0:H], k, KM, lrh[:, k, :], lrl[:, k, :],
                                      ah[:, k, :], al[:, k, :], k == 0)
                last.then_inc(lr_sum.sem, 1)
                mean(c, 0)
                units(c, OG, ah, al, KM)
                pe.wait_ge(lr_got.sem, lr_got.at(c, 1))
                for q in range(2):
                    for n in range(2):
                        last = MM(ps[:, 4 + 2 * q + n, 0:H], gate_up[:, q * P:(q + 1) * P], lr_t[:, n * H:(n + 1) * H],
                                  start=True, stop=True)
                last.then_inc(gate_sum.sem, 1)
                units(c, ZZ, ah, al, KM)
                tile_loop(pe, lambda *a: tile_edge(c, *a), lambda *a: tile_main(c, *a))
                units(c, OUT, ah, al, KM, ready=split(c, 1))
                mean(c, 1)
                for f in range(2):
                    if f == 0:
                        units(c, GU, ah, al, KM, ready=split(c, 2), after_first=lambda: mean(c, 2))
                    else:
                        units(c, GU + 2, ah, al, KM)

                    def ready(k):
                        pe.wait_ge(gu_lo.sem, gu_lo.at(c, f * KF + k + 1))
                    units(c, GU + 1 + 2 * f, gh, gl, KF, ready=ready)
                pe.wait_ge(p_lo.sem, p_lo.at(c, 1))
                mean(c, 3, (False,))
                for m in range(KM):
                    s = m // 4
                    if m % 4 == 0:
                        pe.wait_ge(w_lo.sem, c * UNITS + PAIR0[PROJ] * 2 + (s + 3))
                    if m in (1, 2):
                        pe.wait_ge(drained[m - 1].sem, drained[m - 1].at(c, PAIR0[PROJ]))
                    if m in PROJ_PREV:
                        pe.wait_ge(proj_out.sem, proj_out.at(c, PROJ_PREV[m] + 1))
                    b = PROJ_ACC[m]
                    for k in range(KP):
                        col = slice((m % 4 * KP + k) * P, (m % 4 * KP + k + 1) * P)
                        last = three_pass(ps[:, b:b + 2, 0:H], k, KP, wh[s][:, col], wl[s][:, col],
                                          ph[:, k, :], pl[:, k, :], k == 0)
                    last.then_inc((w_used if m % 4 == 3 else t_proj).sem, 1)
                    if m == 1:
                        mean(c, 3, (True,))
                units(c, PLE, ah, al, KM, ready=split(c, 3))


def constants():
    part = np.arange(P)
    head_mask = (part[:, None] // DK == np.arange(4)[None]).astype(np.float32)
    lev = np.zeros((P, LEVELS, P // 2), np.uint32)
    r = np.arange(P // 2)
    for l in range(LEVELS):
        s = 1 << l
        block = r // s
        lev[:, l, :] = (part[:, None] // (2 * s) == block[None]) & (part[:, None] % (2 * s) < s)
    keep = np.ones((2, T), np.float32)
    keep[:, 0:PT:P] = 0
    keep[:, PT::DEC_SEQ] = 0
    d = part[:, None, None] - (np.arange(P)[None, None] - P * (1 - np.arange(2))[None, :, None])
    dist = np.where((d >= 0) & (d < WINDOW), d, FAR).astype(np.float32)
    first = dist.copy()
    first[:, 0, :] = FAR
    bias_dec = np.full((DB, 2, 4, DEC_SEQ, P + DT), NEG, np.float32)
    for b in range(DB):
        for g in range(2):
            for m in range(4):
                for i in range(DEC_SEQ):
                    d = P + i - np.arange(P)
                    bias_dec[b, g, m, i, :P] = np.where(d < WINDOW, -SLOPES[4 * g + m] * d, NEG)
                    for j in range(i + 1):
                        bias_dec[b, g, m, i, P + DEC_SEQ * b + j] = -SLOPES[4 * g + m] * (i - j)
    return {
        "mean_w": np.full((P, P), 1 / D_MODEL, np.float32),
        "head_w": (part[:, None] // DV == part[None] // DV).astype(np.float32) / DV,
        "ident": np.eye(P, dtype=np.float32),
        "head_mask": head_mask,
        "block_mask": np.repeat(head_mask, DV, axis=1),
        "lev_mask": lev,
        "keep": np.broadcast_to(keep.reshape(1, -1), (P, 2 * T)).copy(),
        "dist": first,
        "dist_prev": dist[:, 0, :].copy(),
        "bias_dec": bias_dec.reshape(P, P + DT),
    }


def kernel(**inputs):
    import concourse.bacc as bacc
    from concourse.bass_utils import run_bass_kernel_spmd

    a = {k: np.asarray(v) for k, v in inputs.items()}

    def by_chunk(prompt, sample):
        F = prompt.shape[-1]
        both = np.concatenate([prompt.reshape(CHUNKS, PT, F), sample.reshape(CHUNKS, DT, F)], 1)
        return np.ascontiguousarray(both.reshape(CHUNKS, T, F // P, P).transpose(3, 0, 2, 1)).reshape(P, -1)

    def as_units(w):
        K, M = w.shape
        return np.ascontiguousarray(w.reshape(K // P, P, M // P, P).transpose(2, 1, 0, 3)).reshape(M // P, P, K)

    def per_tile(v):
        return v.reshape(-1, P).T

    w_in = a["w_in"][0]
    cut = np.cumsum([256, 256, 512, 512, LOW_RANK, 512, 128, 128])
    q_g, k_g, v_g, og, lr, q_s, k_s, p_s = np.split(w_in, cut[:-1], axis=1)
    q_s = q_s.reshape(D_MODEL, 2, 4, SWA_DIM).transpose(0, 2, 1, 3).reshape(D_MODEL, 512)
    w_out = a["w_out"][0]
    swa_rows = w_out[512:].reshape(2, 4, SWA_DIM, D_MODEL).transpose(1, 0, 2, 3).reshape(512, D_MODEL)
    gate, up = as_units(a["w_gate"][0]), as_units(a["w_up"][0])
    down = a["w_down"][0]
    state = a["state_gla"][0].reshape(CHUNKS, DB, 2, 4, DK, DV)
    sinks = a["swa_sinks"][0].reshape(2, 4)
    cache_k = a["cache_swa_k"][0].reshape(DEC_BATCH, P, P)
    cache_v = a["cache_swa_v"][0].reshape(DEC_BATCH, P, P)
    arrays = {
        "x": by_chunk(a["x_prompt"][0], a["x_sample"]),
        "p": by_chunk(a["p_prompt"][0, 0], a["p_sample"][0]),
        "w_z": as_units(np.concatenate([q_g, k_g, v_g, q_s, k_s, p_s, og], 1)),
        "w_lr": np.ascontiguousarray(lr.reshape(KM, P, LOW_RANK).transpose(1, 0, 2)),
        "w_out": as_units(np.concatenate([w_out[:512], swa_rows], 0)),
        "w_gu": np.stack([gate, up], 1).reshape(4 * KF, P, D_MODEL),
        "w_dn": np.concatenate([as_units(down[:KF * P]), as_units(down[KF * P:])], 0),
        "w_proj": as_units(a["w_ple_proj"][0]).reshape(2, 4, P, PLE_DIM).transpose(0, 2, 1, 3).reshape(2, P, D_MODEL),
        "w_ple": as_units(a["w_ple_gate"][0]),
        "gate_up": a["gla_gate_up"][0],
        "cols": np.concatenate([per_tile(a["w_pre_mix"][0]), per_tile(a["w_post_mix"][0]), per_tile(a["w_pre_ffn"][0]),
                                per_tile(a["w_post_ffn"][0]), per_tile(a["gla_gate_b"][0]),
                                np.tile(a["gla_norm_w"][0], 2)[:, None], np.full((P, 1), EPS, np.float32),
                                np.full((P, 1), 1 / GATE_NORM, np.float32)], 1),
        "sinks": np.broadcast_to(sinks.T.reshape(1, HEADS), (P, HEADS)),
        "sink_dec": np.broadcast_to(sinks.reshape(1, HEADS, 1), (DB, HEADS, DEC_SEQ)).reshape(P, 1),
        "state": state.transpose(3, 4, 0, 1, 2, 5).reshape(P, CHUNKS * DB * 2 * DV),
        "cache_k": cache_k,
        "cache_v": cache_v,
        "cache_kT": cache_k.transpose(2, 0, 1).reshape(P, DEC_BATCH * P),
        "cache_vr": cache_v.transpose(1, 0, 2).reshape(P, DEC_BATCH * P),
        **constants(),
    }
    outputs = {"y": (P, CHUNKS * KM * T), "kv": (P, CHUNKS * 2 * KVT), "state": (P, CHUNKS * DB * 2 * DV),
               "state_p": (P, 2, DV), "k_keep": (DEC_BATCH, P - DEC_SEQ, P), "v_keep": (DEC_BATCH, P - DEC_SEQ, P)}

    nc = bacc.Bacc("TRN2", target_bir_lowering=False, num_devices=1)
    arrays = {f"in_{k}": np.ascontiguousarray(v) for k, v in arrays.items()}
    ins = {k[3:]: nc.dram_tensor(k, v.shape, mybir.dt.from_np(v.dtype), kind="ExternalInput").ap()
           for k, v in arrays.items()}
    outs = {k: nc.dram_tensor(f"out_{k}", s, f32, kind="ExternalOutput").ap() for k, s in outputs.items()}
    build(nc, ins, outs)
    r = run_bass_kernel_spmd(nc, [arrays], core_ids=[0]).results[0]
    o = {k: r[f"out_{k}"] for k in outputs}

    y = o["y"].reshape(P, CHUNKS, KM, T).transpose(1, 3, 2, 0).reshape(CHUNKS, T, D_MODEL)
    kv = o["kv"].reshape(P, CHUNKS, 2, KVT).transpose(2, 1, 3, 0)
    prompt_kv = kv[:, CHUNKS - 1, :P].reshape(2, 1, 1, P, KV_HEADS, SWA_DIM)
    new = kv[:, :, P:].reshape(2, DEC_BATCH, DEC_SEQ, P)
    sample_kv = [np.concatenate([o[f"{n}_keep"], new[i]], 1).reshape(1, DEC_BATCH, P, KV_HEADS, SWA_DIM)
                 for i, n in enumerate("kv")]
    state_s = o["state"].reshape(4, DK, CHUNKS, DB, 2, DV).transpose(2, 3, 4, 0, 1, 5)
    state_p = o["state_p"].reshape(4, DK, 2, DV).transpose(2, 0, 1, 3)
    return (y[:, :PT].reshape(1, SEQ, D_MODEL), y[:, PT:].reshape(DEC_BATCH, DEC_SEQ, D_MODEL),
            state_p.reshape(1, 1, HEADS, DK, DV), prompt_kv[0], prompt_kv[1],
            state_s.reshape(1, DEC_BATCH, HEADS, DK, DV), sample_kv[0], sample_kv[1])
```
